# Optimizing a Trainium2 kernel written in Bass

```python
import math
import jax, jax.numpy as jnp
from jax import lax
import numpy as np

D_MODEL = 1024
BATCH = 1
SEQ = 256
DEPTH = 2

N_MIXERS = 2
CONV_WIDTH = 31
SSM_GROUP = 16
SSM_GROUPS = D_MODEL // SSM_GROUP
SSM_STATE = 64
DT_MIN = 1e-3
DT_MAX = 1e-1
D_FF_DENSE = 2816
N_EXPERTS = 8
TOP_K = 2
D_FF_EXPERT = 3584
NORM_EPS = 1e-6
N_CONV_LAYERS = (DEPTH + 1) // 2
N_SSM_LAYERS = DEPTH // 2

kernel_name = "hybrid_conformer_s5_moe_adaln"

F32 = jnp.float32

def rms_norm(x, g):
    x32 = x.astype(F32)
    y = x32 * lax.rsqrt(jnp.mean(x32 * x32, axis=-1, keepdims=True) + NORM_EPS)
    return (y * g.astype(F32)).astype(x.dtype)

def layer_norm(x, g, b):
    x32 = x.astype(F32)
    mu = jnp.mean(x32, axis=-1, keepdims=True)
    xc = x32 - mu
    var = jnp.mean(xc * xc, axis=-1, keepdims=True)
    return (xc * lax.rsqrt(var + NORM_EPS) * g.astype(F32) + b.astype(F32)).astype(x.dtype)

def conformer_conv(h, w_pw1, b_pw1, w_dw, b_dw, ln_g, ln_b, w_pw2, b_pw2):
    u = h @ w_pw1 + b_pw1
    a, g = jnp.split(u, 2, axis=-1)
    u = a * jax.nn.sigmoid(g)
    u = lax.conv_general_dilated(
        u, w_dw[:, None, :].astype(u.dtype),
        window_strides=(1,), padding=[(CONV_WIDTH - 1, 0)],
        dimension_numbers=("NWC", "WIO", "NWC"),
        feature_group_count=D_MODEL) + b_dw
    u = jax.nn.silu(layer_norm(u, ln_g, ln_b))
    return u @ w_pw2 + b_pw2

def _ssm_combine(left, right):
    ar_i, ai_i, br_i, bi_i = left
    ar_j, ai_j, br_j, bi_j = right
    ar = ar_j * ar_i - ai_j * ai_i
    ai = ar_j * ai_i + ai_j * ar_i
    br = ar_j * br_i - ai_j * bi_i + br_j
    bi = ar_j * bi_i + ai_j * br_i + bi_j
    return (ar, ai, br, bi)

def s5_layer(h, a_re, a_im, log_dt, b_re, b_im, c_re, c_im, d_skip, w_glu, b_glu):
    nb, ns, _ = h.shape
    h32 = h.astype(F32)
    u = h32.reshape(nb, ns, SSM_GROUPS, SSM_GROUP)
    dt = jnp.exp(log_dt.astype(F32))[:, None]
    lam_re = a_re.astype(F32)
    lam_im = a_im.astype(F32)
    mag = jnp.exp(dt * lam_re)
    ab_re = mag * jnp.cos(dt * lam_im)
    ab_im = mag * jnp.sin(dt * lam_im)
    den = lam_re * lam_re + lam_im * lam_im
    f_re = ((ab_re - 1.0) * lam_re + ab_im * lam_im) / den
    f_im = (ab_im * lam_re - (ab_re - 1.0) * lam_im) / den
    br = b_re.astype(F32)
    bim = b_im.astype(F32)
    bb_re = f_re[..., None] * br - f_im[..., None] * bim
    bb_im = f_re[..., None] * bim + f_im[..., None] * br
    bu_re = jnp.einsum("bsgc,gpc->bsgp", u, bb_re)
    bu_im = jnp.einsum("bsgc,gpc->bsgp", u, bb_im)
    a_seq_re = jnp.broadcast_to(ab_re[None, None], (1, ns, SSM_GROUPS, SSM_STATE))
    a_seq_im = jnp.broadcast_to(ab_im[None, None], (1, ns, SSM_GROUPS, SSM_STATE))
    _, _, st_re, st_im = lax.associative_scan(
        _ssm_combine, (a_seq_re, a_seq_im, bu_re, bu_im), axis=1)
    y = (jnp.einsum("bsgp,gcp->bsgc", st_re, c_re.astype(F32))
         - jnp.einsum("bsgp,gcp->bsgc", st_im, c_im.astype(F32)))
    y = y.reshape(nb, ns, D_MODEL) + d_skip.astype(F32) * h32
    y = jax.nn.gelu(y)
    z = y @ w_glu.astype(F32) + b_glu.astype(F32)
    za, zg = jnp.split(z, 2, axis=-1)
    return (za * jax.nn.sigmoid(zg)).astype(h.dtype)

def swiglu(t, w_gate, w_up, w_down):
    return (jax.nn.silu(t @ w_gate) * (t @ w_up)) @ w_down

def moe_swiglu(h, w_router, b_router, w_gate, w_up, w_down):
    nb, ns, d = h.shape
    t = h.reshape(nb * ns, d)
    logits = (t @ w_router + b_router).astype(F32)
    top_vals, top_idx = lax.top_k(logits, TOP_K)
    top_w = jax.nn.softmax(top_vals, axis=-1)
    gates = jnp.sum(jax.nn.one_hot(top_idx, N_EXPERTS, dtype=F32) * top_w[..., None], axis=1)
    out = jnp.zeros((nb * ns, d), F32)
    for e in range(N_EXPERTS):
        out = out + gates[:, e:e + 1] * swiglu(t, w_gate[e], w_up[e], w_down[e]).astype(F32)
    return out.reshape(nb, ns, d).astype(h.dtype)

def setup_inputs(seed: int = 0) -> dict:
    key = jax.random.key(seed)
    ks = iter(jax.random.split(key, 40))
    D, G, P = D_MODEL, SSM_GROUPS, SSM_STATE

    def nrm(shape, scale):
        return jax.random.normal(next(ks), shape, F32) * scale

    def gain(shape):
        return 1.0 + nrm(shape, 0.01)

    nA, nB = N_CONV_LAYERS, N_SSM_LAYERS
    inp = {}
    inp["x"] = nrm((BATCH, SEQ, D), 1.0)
    inp["c"] = nrm((BATCH, D), 1.0)
    inp["mod_w"] = nrm((DEPTH, D, 6 * D), D ** -0.5)
    inp["mod_b"] = nrm((DEPTH, 6 * D), 0.01)
    inp["norm1_g"] = gain((DEPTH, D))
    inp["norm2_g"] = gain((DEPTH, D))
    inp["conv_w_pw1"] = nrm((nA, D, 2 * D), D ** -0.5)
    inp["conv_b_pw1"] = nrm((nA, 2 * D), 0.01)
    inp["conv_w_dw"] = nrm((nA, CONV_WIDTH, D), CONV_WIDTH ** -0.5)
    inp["conv_b_dw"] = nrm((nA, D), 0.01)
    inp["conv_ln_g"] = gain((nA, D))
    inp["conv_ln_b"] = nrm((nA, D), 0.01)
    inp["conv_w_pw2"] = nrm((nA, D, D), D ** -0.5)
    inp["conv_b_pw2"] = nrm((nA, D), 0.01)
    inp["ssm_a_re"] = -0.5 * jnp.exp(nrm((nB, G, P), 0.01))
    inp["ssm_a_im"] = math.pi * jnp.arange(P, dtype=F32)[None, None, :] + nrm((nB, G, P), 0.01)
    inp["ssm_log_dt"] = jax.random.uniform(next(ks), (nB, G), F32,
                                           math.log(DT_MIN), math.log(DT_MAX))
    inp["ssm_b_re"] = nrm((nB, G, P, SSM_GROUP), (2 * SSM_GROUP) ** -0.5)
    inp["ssm_b_im"] = nrm((nB, G, P, SSM_GROUP), (2 * SSM_GROUP) ** -0.5)
    inp["ssm_c_re"] = nrm((nB, G, SSM_GROUP, P), (2 * P) ** -0.5)
    inp["ssm_c_im"] = nrm((nB, G, SSM_GROUP, P), (2 * P) ** -0.5)
    inp["ssm_d"] = nrm((nB, D), 1.0)
    inp["ssm_w_glu"] = nrm((nB, D, 2 * D), D ** -0.5)
    inp["ssm_b_glu"] = nrm((nB, 2 * D), 0.01)
    inp["ffn_w_gate"] = nrm((nA, D, D_FF_DENSE), D ** -0.5)
    inp["ffn_w_up"] = nrm((nA, D, D_FF_DENSE), D ** -0.5)
    inp["ffn_w_down"] = nrm((nA, D_FF_DENSE, D), D_FF_DENSE ** -0.5)
    inp["moe_w_router"] = nrm((nB, D, N_EXPERTS), D ** -0.5)
    inp["moe_b_router"] = nrm((nB, N_EXPERTS), 0.01)
    inp["moe_w_gate"] = nrm((nB, N_EXPERTS, D, D_FF_EXPERT), D ** -0.5)
    inp["moe_w_up"] = nrm((nB, N_EXPERTS, D, D_FF_EXPERT), D ** -0.5)
    inp["moe_w_down"] = nrm((nB, N_EXPERTS, D_FF_EXPERT, D), D_FF_EXPERT ** -0.5)
    inp["final_norm_g"] = gain((D,))
    return inp

def reference(x, c, mod_w, mod_b, norm1_g, norm2_g,
              conv_w_pw1, conv_b_pw1, conv_w_dw, conv_b_dw, conv_ln_g, conv_ln_b,
              conv_w_pw2, conv_b_pw2,
              ssm_a_re, ssm_a_im, ssm_log_dt, ssm_b_re, ssm_b_im, ssm_c_re, ssm_c_im,
              ssm_d, ssm_w_glu, ssm_b_glu,
              ffn_w_gate, ffn_w_up, ffn_w_down,
              moe_w_router, moe_b_router, moe_w_gate, moe_w_up, moe_w_down,
              final_norm_g):
    cond = jax.nn.silu(c.astype(F32))
    h = x
    for i in range(DEPTH):
        j = i // N_MIXERS
        mod = cond @ mod_w[i].astype(F32) + mod_b[i].astype(F32)
        sh1, sc1, g1, sh2, sc2, g2 = jnp.split(mod[:, None, :], 6, axis=-1)

        y = (rms_norm(h, norm1_g[i]).astype(F32) * (1.0 + sc1) + sh1).astype(h.dtype)
        if i % N_MIXERS == 0:
            y = conformer_conv(y, conv_w_pw1[j], conv_b_pw1[j], conv_w_dw[j], conv_b_dw[j],
                               conv_ln_g[j], conv_ln_b[j], conv_w_pw2[j], conv_b_pw2[j])
        else:
            y = s5_layer(y, ssm_a_re[j], ssm_a_im[j], ssm_log_dt[j], ssm_b_re[j], ssm_b_im[j],
                         ssm_c_re[j], ssm_c_im[j], ssm_d[j], ssm_w_glu[j], ssm_b_glu[j])
        h = (h.astype(F32) + g1 * y.astype(F32)).astype(x.dtype)

        y = (rms_norm(h, norm2_g[i]).astype(F32) * (1.0 + sc2) + sh2).astype(h.dtype)
        if i % 2 == 0:
            y = swiglu(y, ffn_w_gate[j], ffn_w_up[j], ffn_w_down[j])
        else:
            y = moe_swiglu(y, moe_w_router[j], moe_b_router[j],
                           moe_w_gate[j], moe_w_up[j], moe_w_down[j])
        h = (h.astype(F32) + g2 * y.astype(F32)).astype(x.dtype)
    return rms_norm(h, final_norm_g)


_drawn_inputs = setup_inputs


def setup_inputs(seed=0):
    import zlib

    import numpy as np

    out = dict(_drawn_inputs(seed))
    spreads = {}
    factors = {'norm1_g': 10.049,
     'conv_b_pw1': 8.0,
     'conv_b_dw': 3.472,
     'conv_ln_g': 36.034,
     'conv_ln_b': 36.252,
     'conv_b_pw2': 26.352,
     'ssm_a_re': 64.0,
     'ssm_log_dt': 26.312,
     'ssm_b_im': 25.16,
     'ssm_c_re': 27.16,
     'ssm_b_glu': 29.186,
     'moe_b_router': 25.198,
     'final_norm_g': 30.593,
     'norm2_g': 7.226,
     'ssm_a_im': 8.0,
     'ssm_b_re': 8.0,
     'ssm_c_im': 8.0}
    for name, (base, spread) in spreads.items():
        noise = np.random.default_rng([zlib.crc32(name.encode()), seed]).standard_normal(out[name].shape)
        drawn = base * np.exp(spread * noise) if base else spread * noise
        out[name] = __import__('jax').numpy.asarray(drawn.astype(out[name].dtype))
    for name, factor in factors.items():
        out[name] = (out[name] * factor).astype(out[name].dtype)
    return out
```

```python
from contextlib import ExitStack

import numpy as np
import concourse.bass as bass
from concourse import mybir

F32 = mybir.dt.float32
F32R = mybir.dt.float32r
I32 = mybir.dt.int32
ACT = mybir.ActivationFunctionType
ALU = mybir.AluOpType
AX = mybir.AxisListType

P = 128
D, T, DEPTH = 1024, 256, 2
KC = D // P
TB = T // P
TAPS = 31
GROUPS, GC, NS = 64, 16, 64
TILES = GROUPS * NS // P
FD, FE, NE = 2816, 3584, 8
FBLOCKS = FD // 256
EPS = 1e-6

EARLY_SLOTS = 5
MODS_AT = [0, 2, 1, 2, 1, 2, 1, 2, 1, 1, 1]
SH1, SC1, G1, SH2, SC2, G2 = range(6)


def early_stream():
    tiles = [("mod", (0, v, h), "pe") for v in (SC1, SH1) for h in range(2)]
    tiles += [("pw1", q, "pe") for q in range(4)]
    tiles += [("mod", (0, v, h), "pe") for v in (G1, SC2, SH2) for h in range(2)]
    tiles += [("pw2", q, "pe") for q in range(2)]
    late = [("mod", (l, v, h), "dve") for l, v in
            ((0, G2), (1, SC1), (1, SH1), (1, G1), (1, SC2), (1, SH2), (1, G2)) for h in range(2)]
    for b in range(FBLOCKS):
        tiles.append(("gu", b, "pe"))
        if b:
            tiles.append(("down", b - 1, "pe"))
        tiles += [late.pop(0) for _ in range(MODS_AT[b])]
    tiles.append(("down", FBLOCKS - 1, "pe"))
    tiles += [("glu", q, "pe") for q in range(4)]
    assert not late
    return tiles


STREAM = early_stream()
SHIFT = -len(STREAM) % EARLY_SLOTS
WHERE = {(k, i): n for n, (k, i, _) in enumerate(STREAM)}
DMAS_OF = {"mod": 1, "pw1": 2, "pw2": 1, "gu": 2, "down": 1, "glu": 2}


def slot_of(n):
    return (n + SHIFT) % EARLY_SLOTS


def arrived_count(n):
    return 16 * sum(DMAS_OF[STREAM[m][0]] for m in range(n + 1) if slot_of(m) == slot_of(n))


LATE_MODS = [i for k, i, who in STREAM if who == "dve"]
EARLY_MODS = [i for k, i, who in STREAM if k == "mod" and who == "pe"]


def consumed(n):
    kind, i, who = STREAM[n]
    if kind == "mod":
        return ("modacc_ready", LATE_MODS.index(i) + 1) if who == "dve" else ("modp", EARLY_MODS.index(i) + 1)
    return {"pw1": ("pair_done", 2 * i + 2), "glu": ("pair_done", KC + 2 * i + 2),
            "pw2": ("pw2_done", 4 * i + 4), "gu": ("gu_done", 2 * i + 2),
            "down": ("down_used", 2 * i + 2)}[kind]


FT = FE // 512


def expert_halves():
    out = []
    for j in range(FT):
        out += [("G", j, h) for h in range(2)] + [("U", j, h) for h in range(2)]
        if j >= 2:
            out += [("D", j - 2, h) for h in range(2)]
    return out + [("D", j, h) for j in (FT - 2, FT - 1) for h in range(2)]


HALVES = expert_halves()
NH = len(HALVES)
AT = {x: n for n, x in enumerate(HALVES)}
RAW_SLOTS = 14
HI_SLOTS, LO_SLOTS = 3, 2
assert NH % RAW_SLOTS == 0 and NH % HI_SLOTS == 0 and NH % LO_SLOTS == 0
HW = 2048
T_AFTER = {AT[("U", j + 1, 1)]: j for j in range(FT - 1)}
T_AFTER[AT[("D", FT - 3, 1)]] = FT - 1
NCOMB = 2 * TB
COMB_AFTER = {AT[("U", m, 1)]: m for m in range(NCOMB)}
SGT_AFTER = AT[("U", 4, 1)]
GATHER_AFTER = {AT[("D", FT - 3, 1)]: 0, AT[("D", FT - 2, 1)]: 1}
MAX_ITEMS = NE + 3

MAGIC = 1.5 * 2.0 ** 23
LOG2E = 1.4426950408889634
LN2_HI, LN2_LO = 0.693359375, -2.12194440e-4
TWO_PI = [6.28125, 0.0019350051879882812, 3.0199159819567e-7]
EXP_COEF = [1.0 / 5040, 1.0 / 720, 1.0 / 120, 1.0 / 24, 1.0 / 6, 0.5, 1.0]

ROWS = {}
for _tile, _names in enumerate([
        [("mod_b", 96)],
        [("dw_lo", 128)],
        [("dw_hi", TAPS * KC - 128)],
        [("c", 8), ("norm1_g", 16), ("norm2_g", 16), ("b_pw1", 16), ("b_dw", 8), ("ln_g", 8),
         ("ln_b", 8), ("b_pw2", 8), ("ssm_d", 8), ("b_glu", 16)],
        [("a_re", 32), ("a_im", 32), ("log_dt", 32)]]):
    _r = 0
    for _n, _k in _names:
        ROWS[_n] = (_tile, _r, _k)
        _r += _k
ROW_TILES = [96, 128, TAPS * KC - 128, 112, 96]


def trunk(nc, x, c, mod_w, mod_b, norm1_g, norm2_g, w_pw1, b_pw1, w_dw, b_dw, ln_g, ln_b, w_pw2,
          b_pw2, a_re, a_im, log_dt, b_re, b_im, c_re, c_im, ssm_d, w_glu, b_glu, w_gate, w_up,
          w_down, w_router, b_router, e_gate, e_up, e_down, final_g, out):
    ctx = ExitStack()
    with ctx:
        BASE = 16512

        def at(name, shape, offset, dtype=F32):
            return nc.alloc_sbuf_tensor_at(name, shape, dtype, offset=BASE + offset)

        def sem(name):
            return ctx.enter_context(nc.semaphore(name))

        KB = 1024
        ring = at("ring", [P, RAW_SLOTS * HW], 0)
        LOW = 80 * KB
        bbT = [at(f"bbT_{n}", [P, KC, P], LOW + 4 * KB * n) for n, _ in enumerate("ri")]
        cT = [at(f"cT_{n}", [P, KC, P], LOW + 8 * KB + 4 * KB * n) for n, _ in enumerate("ri")]
        modacc = at("modacc", [P, 2, 512], LOW + 16 * KB)
        hid = at("hid", [P, 4, T], LOW + 20 * KB)
        xrot = at("xrot", [P, 2, 2, 2, T], LOW + 16 * KB)
        sq = at("sq", [P, KC, T], LOW + 24 * KB)
        prod = at("prod", [P, 4, 2, T], LOW + 24 * KB)
        B = 112 * KB
        x_tok = at("x_tok", [P, TB, D], B)
        PAD = T + TAPS - 1
        upad = at("upad", [P, KC, PAD], B + 8 * KB)
        conv = at("conv", [P, KC, T], B + 17 * KB + 512)
        rows = at("rows", [P, len(ROW_TILES), P], B + 26 * KB)
        braw = [at(f"braw_{n}", [P, TILES, GC], B + 29 * KB + 2 * KB * n) for n in range(2)]
        bblk = [at(f"bblk_{n}", [P, TILES, 2 * GC], B + 33 * KB + 4 * KB * n) for n in range(2)]
        craw = [at(f"craw_{n}", [P, KC, NS], B + 41 * KB + 2 * KB * n) for n in range(2)]
        cblk = [at(f"cblk_{n}", [P, KC, P], B + 45 * KB + 4 * KB * n) for n in range(2)]
        btmp = [at(f"btmp_{n}", [P, TILES, GC], B + 53 * KB + 2 * KB * n) for n in range(4)]
        tabc = at("tabc", [P, TILES, T], B)
        tabs = at("tabs", [P, TILES, T], B + 32 * KB)
        whi = at("whi", [P, HI_SLOTS, HW], B, F32R)
        wlo = at("wlo", [P, LO_SLOTS, HW], B + 24 * KB, F32R)
        acc = at("acc", [P, TB, D], B + 40 * KB)
        sq_late = at("sq_late", [P, KC, T], B + 40 * KB)
        y_tok = at("y_tok", [P, TB, D], B + 48 * KB)
        g2_row = at("g2_row", [P, D], B + 56 * KB)
        y_exp = at("y_exp", [P, D], B + 60 * KB)
        fin_g = at("fin_g", [P, D], 0)
        fin_sq = at("fin_sq", [P, D], 4 * KB)
        hT = at("hT", [P, KC, T], 176 * KB)
        yT = at("yT", [P, KC, T], 184 * KB)
        xe_hi = at("xe_hi", [P, KC, P], 176 * KB, F32R)
        xe_lo = at("xe_lo", [P, KC, P], 180 * KB, F32R)
        hh = at("hh", [P, 2, 4, P], 184 * KB, F32R)
        hl = at("hl", [P, 2, 4, P], 188 * KB, F32R)
        M = 192 * KB
        ident = at("ident", [P, P], M)
        ones = at("ones", [P, P], M + 512)
        cols = at("cols", [P, len(ROW_TILES), P], M + 1024)
        modc = at("modc", [P, DEPTH * 6, KC], M + 3584)
        ab = at("ab", [P, 8, KC], M + 3968)
        cond = at("cond", [P, KC], M + 4224)
        sp5 = at("sp5", [P, 20, TILES], M + 4256)
        sp5i = at("sp5i", [P, TILES], M + 6816, I32)
        masks = at("masks", [P, 4], M + 6944)
        iota_t = at("iota_t", [P, T], M + 6976)
        nrm = at("nrm", [P, 3, T], M + 8000)
        sel = at("sel", [P, TB, P], M + 8000)
        selg = at("selg", [P, TB, P], M + 9024)
        selgT = at("selgT", [P, T], M + 10048)
        tmp = at("tmp", [P, 2, 512], M + 11072)
        silu_g = at("silu_g", [P, 512], M + 11072)
        hid_e = at("hid_e", [P, 512], M + 13120)
        rt = at("rt", [P, 12, TB, NE], M + 4256)
        tri = at("tri", [P, P], M + 6976)
        iota_s = at("iota_s", [P, P], M + 6976 + 512)
        wr = at("wr", [P, KC, NE], B)
        R = M + 15168
        logit = at("logit", [P, TB, NE], R)
        items = at("items", [P, MAX_ITEMS + 1, 4], R + 64)
        now = at("now", [P, 8], R + 256)
        count_i = at("count_i", [P, 1], R + 288, I32)
        iota_e = at("iota_e", [P, NE], R + 320)
        brow = at("brow", [1, NE], R + 352)
        over_i = at("over_i", [P, 4], R + 384, I32)
        ldt_rows = at("ldt_rows", [P, 4], R + 416)

        psum = [ctx.enter_context(nc.psum_tensor(f"bank{n}", [P, 512], F32)) for n in range(8)]

        def col(name, i=0):
            tile, r, _ = ROWS[name]
            return cols[:, tile, r + i:r + i + 1]

        def colv(name, i, n):
            tile, r, _ = ROWS[name]
            return cols[:, tile, r + i:r + i + n]

        def dw(tap, kc):
            r = tap * KC + kc
            return cols[:, 1 + r // P, r % P:r % P + 1]

        def early(n, parts):
            s = slot_of(n)
            return ring[:, s * 4096:(s + 1) * 4096].rearrange("p (k n) -> p k n", k=parts)

        x_in, rows_in, s5_in, wr_in, fg_in, out_done = (
            sem(n) for n in ("x_in", "rows_in", "s5_in", "wr_in", "fg_in", "out_done"))
        arr = [sem(f"arr{n}") for n in range(EARLY_SLOTS)]
        consts = sem("consts")
        rows_ready = sem("rows_ready")
        rows_t, cols_ready = sem("rows_t"), sem("cols_ready")
        cond_ready = sem("cond_ready")
        x_t, h_ready = sem("x_t"), sem("h_ready")
        modp, modc_ready = sem("modp"), sem("modc_ready")
        modacc_ready = sem("modacc_ready")
        ab_ready = sem("ab_ready")
        sq_ready, sum_ready, var_ready, std_ready = (sem(n) for n in ("sq_ready", "sum_ready", "var_ready", "std_ready"))
        raw_ready, y_ready = sem("raw_ready"), sem("y_ready")
        pair_done, sig_ready, pair_used = sem("pair_done"), sem("sig_ready"), sem("pair_used")
        conv_ready, mean_sum, cent_ready = sem("conv_ready"), sem("mean_sum"), sem("cent_ready")
        pw2_done, pw2_tmp, h2_ready = sem("pw2_done"), sem("pw2_tmp"), sem("h2_ready")
        gu_done, gsil, hid_ready, down_used = (sem(n) for n in ("gu_done", "gsil", "hid_ready", "down_used"))
        h3_ready, h4_ready = sem("h3_ready"), sem("h4_ready")
        chain = sem("chain")
        blk_ready, blk_t, blk_c = sem("blk_ready"), sem("blk_t"), sem("blk_c")
        trig_in, trig, trig_out = sem("trig_in"), sem("trig"), sem("trig_out")
        rnd_ready, frac_ready, sin_ready, tab_ready = (sem(n) for n in ("rnd_ready", "frac_ready", "sin_ready", "tab_ready"))
        act_own, pool_own = sem("act_own"), sem("pool_own")
        ones_pad = sem("ones_pad")
        bu_done, bu_used, scan_ready, prod_d, prod_p, prod_used, ys_pre, z_ready = (
            sem(n) for n in ("bu_done", "bu_used", "scan_ready", "prod_d", "prod_p", "prod_used",
                             "ys_pre", "z_ready"))
        log_done, rank_done, mask_ready, diag_ready, g2_done = (
            sem(n) for n in ("log_done", "rank_done", "mask_ready", "diag_ready", "g2_done"))
        tok_t, tok_c, exp2_in, exp2 = sem("tok_t"), sem("tok_c"), sem("exp2_in"), sem("exp2")
        items_ready, g2row_ready = sem("items_ready"), sem("g2row_ready")
        raw_in = [sem(f"raw_in{n}") for n in range(RAW_SLOTS)]
        hi_ready, lo_ready, hi_used, lo_used = (sem(n) for n in ("hi_ready", "lo_ready", "hi_used", "lo_used"))
        s_ready, he_ready, t_done, hh_ready, hl_ready = (
            sem(n) for n in ("s_ready", "he_ready", "t_done", "hh_ready", "hl_ready"))
        yx_ready, comb_done, comb_used = (sem(n) for n in ("yx_ready", "comb_done", "comb_used"))
        sel_ready, selg_ready, selg_t, selgT_ready = (sem(n) for n in ("sel_ready", "selg_ready", "selg_t", "selgT_ready"))
        gath_done, xh_ready, xl_ready = sem("gath_done"), sem("xh_ready"), sem("xl_ready")
        fin_var, fin_std, fin_ready = (sem(n) for n in ("fin_var", "fin_std", "fin_ready"))
        selgT_zero, now_ready, acc_half = sem("selgT_zero"), sem("now_ready"), sem("acc_half")

        block = ctx.enter_context(nc.Block())
        S5_TABLE_ORDER = [(2 * m + k) * 4 + q for m in range(4) for q in range(4) for k in range(2)]
        TABLES_AT = [0, 4, 4] + [3] * 8
        NB = 16

        MOD_ORDER = [(0, SC1), (0, SH1), (0, G1), (0, SC2), (0, SH2),
                     (0, G2), (1, SC1), (1, SH1), (1, G1), (1, SC2), (1, SH2), (1, G2)]
        PE_MODS = 5
        MOD_BANK = [6, 3, 6, 2, 3, 7, 6, 7, 6, 7, 6, 7]

        def mc(l, v, kc=None):
            a = modc[:, l * 6 + v, :]
            return a if kc is None else a[:, kc:kc + 1]

        CONSUMED = {"modacc_ready": modacc_ready, "modp": modp, "pair_done": pair_done,
                    "pw2_done": pw2_done, "gu_done": gu_done, "down_used": down_used}

        @block.sync
        def _(sp):
            for n, (kind, i, who) in enumerate(STREAM):
                prev = n - EARLY_SLOTS
                if prev >= 0:
                    name, count = consumed(prev)
                    sp.wait_ge(CONSUMED[name], count)
                a = arr[slot_of(n)]
                if kind == "mod":
                    l, v, h = i
                    src = mod_w[l, :, v * D + h * 512:v * D + (h + 1) * 512]
                    sp.dma_start(early(n, KC), src.rearrange("(k p) n -> p k n", p=P)).then_inc(a, 16)
                elif kind in ("pw1", "glu"):
                    w = w_pw1 if kind == "pw1" else w_glu
                    for g in range(2):
                        src = w[0, :, g * D + i * 256:g * D + (i + 1) * 256]
                        sp.dma_start(early(n, KC)[:, :, g * 256:(g + 1) * 256],
                                     src.rearrange("(k p) n -> p k n", p=P)).then_inc(a, 16)
                elif kind == "gu":
                    for g, w in enumerate((w_gate, w_up)):
                        src = w[0, :, i * 256:(i + 1) * 256]
                        sp.dma_start(early(n, KC)[:, :, g * 256:(g + 1) * 256],
                                     src.rearrange("(k p) n -> p k n", p=P)).then_inc(a, 16)
                elif kind == "pw2":
                    src = w_pw2[0, :, i * 512:(i + 1) * 512]
                    sp.dma_start(early(n, KC), src.rearrange("(k p) n -> p k n", p=P)).then_inc(a, 16)
                else:
                    src = w_down[0, i * 256:(i + 1) * 256, :]
                    sp.dma_start(early(n, 4)[:, 0:2, :], src.rearrange("(k p) n -> p k n", p=P)).then_inc(a, 16)

            def half(e, n):
                kind, j, h = HALVES[n]
                s = n % RAW_SLOTS
                e1 = bass.ds(e, 1)
                if kind == "D":
                    src = e_down[0, e1, j * 512 + h * 256:j * 512 + (h + 1) * 256, :]
                    src = src.rearrange("e (k p) n -> p (e k) n", p=P)
                    dst = ring[:, s * HW:(s + 1) * HW].rearrange("p (k n) -> p k n", k=2)
                else:
                    w = e_gate if kind == "G" else e_up
                    src = w[0, e1, h * 512:(h + 1) * 512, j * 512:(j + 1) * 512]
                    src = src.rearrange("e (k p) n -> p (e k) n", p=P)
                    dst = ring[:, s * HW:(s + 1) * HW].rearrange("p (k n) -> p k n", k=4)
                sp.dma_start(dst, src).then_inc(raw_in[s], 16)

            for n in range(NH):
                if n < 2 * EARLY_SLOTS:
                    if n % 2 == 0:
                        m = len(STREAM) - EARLY_SLOTS + n // 2
                        name, count = consumed(m)
                        sp.wait_ge(CONSUMED[name], count)
                elif n < RAW_SLOTS:
                    if n == 2 * EARLY_SLOTS:
                        sp.wait_ge(z_ready, KC)
                else:
                    sp.wait_ge(lo_ready, n - RAW_SLOTS + 1)
                half(0, n)
            with sp.Fori(1, NE) as e:
                for n in range(NH):
                    sp.wait_ge(lo_ready, e * NH + (n - RAW_SLOTS + 1))
                    half(e, n)
            sp.wait_ge(items_ready, 1)
            total = sp.value_load(count_i[0:1, 0:1], min_val=NE, max_val=MAX_ITEMS)
            with sp.If(total > NE):
                with sp.Fori(NE, total) as i:
                    e = sp.value_load(over_i[0:1, bass.ds(i - NE, 1)], min_val=0, max_val=NE - 1)
                    for n in range(NH):
                        sp.wait_ge(lo_ready, i * NH + (n - RAW_SLOTS + 1))
                        half(e, n)
            sp.wait_ge(lo_ready, total * NH)
            sp.dma_start(fin_g[:, :], final_g.rearrange("(a n) -> a n", a=1).broadcast_to([P, D])).then_inc(fg_in, 16)
            for tb in range(TB):
                sp.wait_ge(fin_ready, tb + 1)
                sp.dma_start(out[0, tb * P:(tb + 1) * P, :], acc[:, tb, :]).then_inc(out_done, 16)
            sp.wait_ge(out_done, 16 * TB)

        @block.gpsimd
        def _(pool):
            pool.memset(ident[:, :], 0.0).then_inc(pool_own, 1)
            pool.memset(ones[:, :], 1.0).then_inc(consts, 1)
            pool.wait_ge(pool_own, 1)
            pool.affine_select(out=ident[:, :], in_=ident[:, :], compare_op=ALU.not_equal, fill=1.0,
                               base=0, pattern=[[-1, P]], channel_multiplier=1).then_inc(consts, 1)
            pool.iota(iota_t[:, :], pattern=[[1, T]], base=0, channel_multiplier=0,
                      allow_small_or_imprecise_dtypes=True).then_inc(consts, 1)
            pool.memset(upad[:, :, 0:TAPS - 1], 0.0).then_inc(ones_pad, 1)
            for n in range(2):
                pool.memset(bblk[n][:, :, :], 0.0).then_inc(ones_pad, 1)
            pool.iota(iota_e[:, :], pattern=[[1, NE]], base=0, channel_multiplier=0,
                      allow_small_or_imprecise_dtypes=True).then_inc(consts, 1)

            pool.wait_ge(trig_out, 1)
            pool.wait_ge(y_ready, 2 * KC)
            pool.wait_ge(blk_c, 8)
            own = 1
            for n, i in enumerate(S5_TABLE_ORDER):
                pool.tensor_scalar(tabs[:, n, :], iota_t[:, :], sp5[:, 10, i:i + 1], MAGIC,
                                   ALU.mult, ALU.add).then_inc(pool_own, 1)
                own += 1
                pool.wait_ge(pool_own, own)
                pool.tensor_scalar(tabs[:, n, :], tabs[:, n, :], MAGIC, None, ALU.subtract).then_inc(rnd_ready, 1)
                if n >= 2:
                    pool.wait_ge(sin_ready, n - 1)
                    pool.tensor_scalar(tabc[:, n - 2, :], tabc[:, n - 2, :], -2.0, 1.0,
                                       ALU.mult, ALU.add).then_inc(tab_ready, 1)
            for n in (TILES - 2, TILES - 1):
                pool.wait_ge(sin_ready, n + 1)
                pool.tensor_scalar(tabc[:, n, :], tabc[:, n, :], -2.0, 1.0,
                                   ALU.mult, ALU.add).then_inc(tab_ready, 1)
            pool.wait_ge(tab_ready, TILES)
            for b in range(NB):
                pool.wait_ge(scan_ready, b + 1)
                if b:
                    pool.wait_ge(prod_used, b)
                tc, ts = tabc[:, 2 * b:2 * b + 2, :], tabs[:, 2 * b:2 * b + 2, :]
                pool.tensor_tensor(prod[:, 2, :, :], ts, xrot[:, b % 2, 0, :, :], ALU.mult).then_inc(prod_p, 1)
                pool.tensor_tensor(prod[:, 3, :, :], tc, xrot[:, b % 2, 1, :, :], ALU.mult).then_inc(prod_p, 1)
            pool.iota(iota_s[:, :], pattern=[[1, P]], base=0, channel_multiplier=0,
                      allow_small_or_imprecise_dtypes=True).then_inc(consts, 1)
            pool.memset(tri[:, :], 1.0).then_inc(pool_own, 1)
            pool.wait_ge(pool_own, own + 1)
            pool.affine_select(out=tri[:, :], in_=tri[:, :], compare_op=ALU.is_ge, fill=0.0,
                               base=0, pattern=[[1, P]], channel_multiplier=-1).then_inc(consts, 1)

        @block.scalar
        def _(act):
            for tb in range(TB):
                act.dma_start(x_tok[:, tb, :], x[0, tb * P:(tb + 1) * P, :]).then_inc(x_in, 16)
            dwr = w_dw[0].rearrange("t (k p) -> (t k) p", p=P)
            srcs = {
                "mod_b": mod_b.rearrange("l (k p) -> (l k) p", p=P),
                "dw_lo": dwr[0:P, :], "dw_hi": dwr[P:TAPS * KC, :],
                "c": c.rearrange("a (k p) -> (a k) p", p=P),
                "norm1_g": norm1_g.rearrange("l (k p) -> (l k) p", p=P),
                "norm2_g": norm2_g.rearrange("l (k p) -> (l k) p", p=P),
                "b_pw1": b_pw1.rearrange("a (k p) -> (a k) p", p=P),
                "b_dw": b_dw.rearrange("a (k p) -> (a k) p", p=P),
                "ln_g": ln_g.rearrange("a (k p) -> (a k) p", p=P),
                "ln_b": ln_b.rearrange("a (k p) -> (a k) p", p=P),
                "b_pw2": b_pw2.rearrange("a (k p) -> (a k) p", p=P),
                "ssm_d": ssm_d.rearrange("a (k p) -> (a k) p", p=P),
                "b_glu": b_glu.rearrange("a (k p) -> (a k) p", p=P),
                "a_re": a_re[0].rearrange("(i g) s -> i (g s)", g=2),
                "a_im": a_im[0].rearrange("(i g) s -> i (g s)", g=2),
                "log_dt": log_dt[0].rearrange("(i g) -> i g", g=2),
            }
            for name, (tile, r, k) in ROWS.items():
                w = 2 if name == "log_dt" else P
                act.dma_start(rows[r:r + k, tile, 0:w] if name != "log_dt" else ldt_rows[64:96, 0:2],
                              srcs[name]).then_inc(rows_in, 16)
            for n, w in enumerate((b_re, b_im)):
                act.dma_start(braw[n][:, :, :], w[0].rearrange("g s c -> (g s) c").rearrange("(i p) c -> p i c", p=P)).then_inc(s5_in, 16)
            for n, w in enumerate((c_re, c_im)):
                act.dma_start(craw[n][:, :, :], w[0].rearrange("g c s -> (g c) s").rearrange("(k p) s -> p k s", p=P)).then_inc(s5_in, 16)

            for n, k in enumerate(ROW_TILES):
                act.wait_ge(rows_t, 4 if n < 4 else 5)
                act.activation(cols[:, n, 0:k], psum[0 if n < 4 else 1][:, (n % 4) * P:(n % 4) * P + k],
                               ACT.Copy).then_inc(cols_ready, 1)
            act.wait_ge(cols_ready, 4)
            act.activation(cond[:, :], colv("c", 0, KC), ACT.Silu).then_inc(cond_ready, 1)
            for n in range(4):
                act.wait_ge(x_t, n + 1)
                act.activation(hT[:, 2 * n:2 * n + 2, :], psum[2 + n % 2][:, :].rearrange("p (k t) -> p k t", k=2),
                               ACT.Copy).then_inc(h_ready, 1)

            def squares(src, dst, ready, first):
                for kc in range(KC):
                    act.wait_ge(ready, first(kc))
                    act.activation(dst[:, kc, :], src[:, kc, :], ACT.Square).then_inc(sq_ready, 1)

            def root(k):
                act.wait_ge(var_ready, k + 1)
                act.activation(nrm[:, 1, :], nrm[:, 0, :], ACT.Sqrt).then_inc(std_ready, 1)

            def shifted(k, func, shift, src):
                for kc in range(KC):
                    act.wait_ge(raw_ready, k * KC + kc + 1)
                    act.activation(yT[:, kc, :], src[:, kc, :], func, bias=shift(kc)).then_inc(y_ready, 1)

            squares(hT, sq, h_ready, lambda kc: kc // 2 + 1)
            root(0)
            act.wait_ge(trig_in, 1)
            act.activation(sp5[:, 11, :], sp5[:, 8, :], ACT.Sin).then_inc(trig, 1)
            act.activation(sp5[:, 12, :], sp5[:, 8, :], ACT.Sin, scale=0.5).then_inc(trig, 1)
            act.wait_ge(modc_ready, 2)
            shifted(0, ACT.Identity, lambda kc: mc(0, SH1, kc), yT)

            def sigmoids(k0, bias):
                for n in range(KC):
                    act.wait_ge(pair_done, k0 + n + 1)
                    if k0 + n >= 2:
                        act.wait_ge(pair_used, k0 + n - 1)
                    act.activation(tmp[:, n % 2, 0:T], psum[4 + n % 2][:, T:2 * T], ACT.Sigmoid,
                                   bias=bias(n)).then_inc(sig_ready, 1)

            def s5_copies(ns):
                for n in ns:
                    act.wait_ge(blk_t, n + 1)
                    src = psum[n % 2][:, :].rearrange("p (k s) -> p k s", k=4)
                    dst = (bbT[n // 2] if n < 4 else cT[n // 2 - 2])[:, (n % 2) * 4:(n % 2) * 4 + 4, :]
                    act.activation(dst, src, ACT.Copy).then_inc(blk_c, 1)

            sigmoids(0, lambda n: col("b_pw1", KC + n))
            s5_copies(range(8))
            squares(conv, sq, cent_ready, lambda kc: kc + 1)
            root(1)
            shifted(1, ACT.Silu, lambda kc: col("ln_b", kc), conv)
            act.wait_ge(ab_ready, 3)
            for n in range(KC):
                act.wait_ge(pw2_done, n + 1)
                if n >= 2:
                    act.wait_ge(h2_ready, n - 1)
                act.activation(tmp[:, n % 2, 0:T], psum[4 + n % 2][:, 0:T], ACT.Identity,
                               scale=mc(0, G1, n), bias=ab[:, 2, n:n + 1]).then_inc(pw2_tmp, 1)
            squares(hT, sq, h2_ready, lambda kc: kc + 1)
            root(2)
            shifted(2, ACT.Identity, lambda kc: mc(0, SH2, kc), yT)

            def sin_tables(n):
                act.wait_ge(frac_ready, n + 1)
                act.activation(tabs[:, n, :], tabc[:, n, :], ACT.Sin, scale=6.2831840).then_inc(act_own, 1)
                if n >= 2:
                    act.wait_ge(sin_ready, n - 1)
                act.activation(nrm[:, n % 2, :], tabc[:, n, :], ACT.Sin, scale=3.14159265).then_inc(act_own, 1)
                act.wait_ge(act_own, 2 * n + 2)
                act.activation(tabc[:, n, :], nrm[:, n % 2, :], ACT.Square).then_inc(sin_ready, 1)

            made = 0
            for b in range(FBLOCKS):
                for f in (2 * b, 2 * b + 1):
                    act.wait_ge(gu_done, f + 1)
                    if f >= 2:
                        act.wait_ge(hid_ready, f - 1)
                    act.activation(tmp[:, f % 2, 0:T], psum[4 + f % 2][:, 0:T], ACT.Silu).then_inc(gsil, 1)
                for _ in range(TABLES_AT[b]):
                    sin_tables(made)
                    made += 1
            squares(hT, sq, h3_ready, lambda kc: kc + 1)
            root(3)
            shifted(3, ACT.Identity, lambda kc: mc(1, SH1, kc), yT)
            for kc in range(KC):
                act.wait_ge(ys_pre, kc + 1)
                act.activation(yT[:, kc, :], yT[:, kc, :], ACT.Gelu_apprx_tanh).then_inc(z_ready, 1)
            sigmoids(KC, lambda n: col("b_glu", KC + n))
            act.dma_start(wr[:, :, :], w_router[0].rearrange("(k p) e -> p k e", p=P)).then_inc(wr_in, 16)
            act.dma_start(brow[:, :], b_router).then_inc(wr_in, 16)
            squares(hT, sq_late, h4_ready, lambda kc: kc + 1)
            root(4)
            shifted(4, ACT.Identity, lambda kc: mc(1, SH2, kc), yT)
            act.wait_ge(exp2_in, 1)
            act.activation(rt[:, 4, :, 1], rt[:, 4, :, 0], ACT.Exp).then_inc(exp2, 1)
            for n in range(8):
                act.wait_ge(tok_t, n + 1)
                src = psum[n % 4][:, :]
                dst = (acc if n < 4 else y_tok)[:, (n // 2) % 2, (n % 2) * 512:(n % 2) * 512 + 512]
                act.activation(dst, src, ACT.Copy).then_inc(tok_c, 1)
            for n in range(2):
                act.wait_ge(g2_done, n + 1)
                act.activation(g2_row[:, n * 512:(n + 1) * 512], psum[4 + n][:, :], ACT.Copy).then_inc(g2row_ready, 1)

            for g in range(2):
                act.wait_ge(gath_done, g + 1)
                act.activation(xe_hi[:, 4 * g:4 * g + 4, :], psum[7][:, :].rearrange("p (k s) -> p k s", k=4),
                               ACT.Copy).then_inc(xh_ready, 1)

            act.wait_ge(items_ready, 1)
            total = act.value_load(count_i[0:1, 0:1], min_val=NE, max_val=MAX_ITEMS)
            with act.Fori(0, total) as i:
                for n in range(NH):
                    s = n % RAW_SLOTS
                    act.wait_ge(raw_in[s], (i * (NH // RAW_SLOTS) + (n // RAW_SLOTS + 1)) * 16)
                    act.wait_ge(hi_used, i * NH + n + 1)
                    act.activation(whi[:, n % HI_SLOTS, :], ring[:, s * HW:(s + 1) * HW],
                                   ACT.Copy).then_inc(hi_ready, 1)
                    if n >= 3 and HALVES[n - 3][0] == "U" and HALVES[n - 3][2] == 1:
                        j = HALVES[n - 3][1]
                        act.wait_ge(lo_used, i * NH + (AT[("U", j, 1)] + 1 + LO_SLOTS))
                        act.activation(silu_g[:, :], psum[j % 2][:, :], ACT.Silu).then_inc(s_ready, 1)
                    if n - 3 in T_AFTER:
                        j = T_AFTER[n - 3]
                        act.wait_ge(t_done, i * FT + j + 1)
                        act.activation(hh[:, j % 2, :, :], psum[6][:, :].rearrange("p (k s) -> p k s", k=4),
                                       ACT.Copy).then_inc(hh_ready, 1)
                    if n - 3 == SGT_AFTER:
                        act.wait_ge(selg_t, i + 1)
                        act.activation(selgT[:, :], psum[7][:, 0:T], ACT.Copy).then_inc(selgT_ready, 1)
                    g = GATHER_AFTER.get(n - 2)
                    if g is not None:
                        act.wait_ge(gath_done, i * 2 + g + 3)
                        act.activation(xe_hi[:, 4 * g:4 * g + 4, :],
                                       psum[7][:, :].rearrange("p (k s) -> p k s", k=4),
                                       ACT.Copy).then_inc(xh_ready, 1)
            act.wait_ge(fg_in, 16)
            for tb in range(TB):
                act.wait_ge(acc_half, 2 * tb + 2)
                if tb:
                    act.wait_ge(act_own, 2 * TILES + tb)
                act.activation(fin_sq[:, :], acc[:, tb, :], ACT.Square,
                               accum_out=now[:, 4 + tb:5 + tb]).then_inc(act_own, 1)
                act.wait_ge(act_own, 2 * TILES + tb + 1)
            act.wait_ge(fin_var, 1)
            act.activation(now[:, 2:4], now[:, 6:8], ACT.Sqrt).then_inc(fin_std, 1)

        @block.vector
        def _(v):
            links = [0]

            def link(ins):
                links[0] += 1
                ins.then_inc(chain, 1)
                v.wait_ge(chain, links[0])

            v.wait_ge(rows_in, 16 * len(ROWS))
            for g in range(2):
                ins = v.tensor_copy(rows[64:96, 4, g * NS:(g + 1) * NS],
                                    ldt_rows[64:96, g:g + 1].broadcast_to([32, NS]))
            ins.then_inc(rows_ready, 1)
            v.wait_ge(consts, 2)
            idv = ident[:, :].rearrange("p (a g c) -> p g a c", g=2, c=GC)
            for g in range(2):
                link(v.tensor_reduce(masks[:, g:g + 1], idv[:, g], axis=AX.XY, op=ALU.add))
            for g in range(2):
                link(v.tensor_scalar(masks[:, 2 + g:3 + g], masks[:, g:g + 1], -1.0, None, ALU.mult))

            def q(n):
                return sp5[:, n, :]

            def exponential(o, src, t):
                xx, k, r = t
                link(v.tensor_scalar(q(xx), src, -87.0, 88.7, ALU.max, ALU.min))
                link(v.tensor_scalar(q(k), q(xx), LOG2E, MAGIC, ALU.mult, ALU.add))
                link(v.tensor_scalar(q(k), q(k), MAGIC, None, ALU.subtract))
                link(v.scalar_tensor_tensor(q(r), q(k), -LN2_HI, q(xx), ALU.mult, ALU.add))
                link(v.scalar_tensor_tensor(q(r), q(k), -LN2_LO, q(r), ALU.mult, ALU.add))
                link(v.tensor_scalar(q(xx), q(r), EXP_COEF[0], None, ALU.mult))
                for cf in EXP_COEF[1:]:
                    link(v.scalar_tensor_tensor(q(xx), q(xx), cf, q(r), ALU.add, ALU.mult))
                link(v.tensor_scalar(sp5i[:, :], q(k), 127.0, 2.0 ** 23, ALU.add, ALU.mult))
                link(v.scalar_tensor_tensor(q(o), q(xx), 1.0, sp5i[:, :].bitcast(F32), ALU.add, ALU.mult))

            v.wait_ge(cols_ready, 5)
            are, aim, ldt = (cols[:, 4, 32 * n:32 * n + 32] for n in range(3))
            exponential(3, ldt, (0, 1, 2))
            link(v.tensor_tensor(q(4), q(3), are, ALU.mult))
            exponential(5, q(4), (0, 1, 2))
            link(v.tensor_tensor(q(6), q(3), aim, ALU.mult))
            link(v.tensor_scalar(q(7), q(6), 1.0 / (2 * np.pi), MAGIC, ALU.mult, ALU.add))
            link(v.tensor_scalar(q(7), q(7), MAGIC, None, ALU.subtract))
            link(v.scalar_tensor_tensor(q(8), q(7), -TWO_PI[0], q(6), ALU.mult, ALU.add))
            link(v.scalar_tensor_tensor(q(8), q(7), -TWO_PI[1], q(8), ALU.mult, ALU.add))
            link(v.scalar_tensor_tensor(q(8), q(7), -TWO_PI[2], q(8), ALU.mult, ALU.add))
            link(v.tensor_scalar(q(8), q(8), -3.1415925, 3.1415925, ALU.max, ALU.min))
            v.tensor_scalar(q(10), q(8), 1.0 / (2 * np.pi), None, ALU.mult).then_inc(trig_in, 1)
            v.wait_ge(trig_in, 1)
            link(v.tensor_scalar(q(13), q(10), 384.0, None, ALU.add))
            link(v.tensor_scalar(q(13), q(13), 384.0, None, ALU.subtract))
            v.tensor_tensor(q(14), q(10), q(13), ALU.subtract).then_inc(trig_out, 1)

            def variance(k, waited, sums):
                v.wait_ge(sum_ready, k + 1)
                v.tensor_scalar(nrm[:, 0, :], psum[7][:, 0:T], 1.0 / D, EPS, ALU.mult, ALU.add).then_inc(var_ready, 1)

            def rsqrt(k):
                v.wait_ge(std_ready, k + 1)
                link(v.reciprocal(nrm[:, 2, :], nrm[:, 1, :]))
                link(v.tensor_tensor(nrm[:, 1, :], nrm[:, 0, :], nrm[:, 2, :], ALU.mult))
                link(v.scalar_tensor_tensor(nrm[:, 1, :], nrm[:, 1, :], -0.5, nrm[:, 2, :], ALU.mult, ALU.mult))
                link(v.scalar_tensor_tensor(nrm[:, 1, :], nrm[:, 1, :], 1.5, nrm[:, 2, :], ALU.add, ALU.mult))

            def scaled(dst, src, gain):
                for kc in range(KC):
                    v.scalar_tensor_tensor(dst[:, kc, :], src[:, kc, :], gain(kc), nrm[:, 1, :],
                                           ALU.mult, ALU.mult).then_inc(raw_ready, 1)

            def mod_evac(k):
                l, m = MOD_ORDER[k]
                v.wait_ge(modp, 2 * k + 2)
                v.tensor_tensor(mc(l, m), psum[MOD_BANK[k]][:, 0:KC], colv("mod_b", (l * 6 + m) * KC, KC),
                                ALU.add).then_inc(modc_ready, 1)
                v.wait_ge(modc_ready, k + 1)

            def gain_cols(o, l, m, name):
                v.scalar_tensor_tensor(ab[:, o, :], mc(l, m), 1.0, colv(name, l * KC, KC),
                                       ALU.add, ALU.mult).then_inc(ab_ready, 1)

            variance(0, None, None)
            rsqrt(0)
            v.wait_ge(trig, 2)
            link(v.tensor_tensor(q(15), q(12), q(12), ALU.mult))
            link(v.tensor_scalar(q(15), q(15), -2.0, 1.0, ALU.mult, ALU.add))
            link(v.tensor_tensor(q(15), q(15), q(5), ALU.mult))
            link(v.tensor_scalar(q(15), q(15), -1.0, None, ALU.add))
            link(v.tensor_tensor(q(16), q(11), q(5), ALU.mult))
            link(v.tensor_tensor(q(0), are, are, ALU.mult))
            link(v.tensor_tensor(q(1), aim, aim, ALU.mult))
            link(v.tensor_tensor(q(0), q(0), q(1), ALU.add))
            link(v.reciprocal(q(0), q(0)))
            link(v.tensor_tensor(q(1), q(15), are, ALU.mult))
            link(v.tensor_tensor(q(2), q(16), aim, ALU.mult))
            link(v.tensor_tensor(q(1), q(1), q(2), ALU.add))
            link(v.tensor_tensor(q(17), q(1), q(0), ALU.mult))
            link(v.tensor_tensor(q(1), q(16), are, ALU.mult))
            link(v.tensor_tensor(q(2), q(15), aim, ALU.mult))
            link(v.tensor_tensor(q(1), q(1), q(2), ALU.subtract))
            link(v.tensor_tensor(q(18), q(1), q(0), ALU.mult))
            v.wait_ge(s5_in, 64)
            fr, fi = (q(n).unsqueeze(2).broadcast_to([P, TILES, GC]) for n in (17, 18))
            for t, (f, w) in enumerate(((fr, 0), (fi, 1), (fr, 1), (fi, 0))):
                link(v.tensor_tensor(btmp[t][:, :, :], f, braw[w][:, :, :], ALU.mult))
            v.wait_ge(ones_pad, 3)
            for g in range(2):
                pr, cr = slice(64 * g, 64 * g + 64), slice(GC * g, GC * g + GC)
                v.tensor_tensor(bblk[0][pr, :, cr], btmp[0][pr, :, :], btmp[1][pr, :, :], ALU.subtract).then_inc(blk_ready, 1)
                v.tensor_tensor(bblk[1][pr, :, cr], btmp[2][pr, :, :], btmp[3][pr, :, :], ALU.add).then_inc(blk_ready, 1)
            for n in range(2):
                for g in range(2):
                    v.tensor_scalar(cblk[n][:, :, g * NS:(g + 1) * NS], craw[n][:, :, :],
                                    masks[:, 2 * n + g:2 * n + g + 1], None, ALU.mult).then_inc(blk_ready, 1)

            mod_evac(0)
            gain_cols(0, 0, SC1, "norm1_g")
            v.wait_ge(ab_ready, 1)
            scaled(yT, hT, lambda kc: ab[:, 0, kc:kc + 1])
            mod_evac(1)
            v.wait_ge(ones_pad, 1)
            v.wait_ge(x_t, 4)
            for n in range(KC):
                v.wait_ge(sig_ready, n + 1)
                v.scalar_tensor_tensor(upad[:, n, TAPS - 1:PAD], psum[4 + n % 2][:, 0:T], col("b_pw1", n),
                                       tmp[:, n % 2, 0:T], ALU.add, ALU.mult).then_inc(pair_used, 1)
                v.wait_ge(pair_used, n + 1)
                link(v.tensor_scalar(conv[:, n, :], upad[:, n, 0:T], dw(0, n), col("b_dw", n), ALU.mult, ALU.add))
                for k in range(1, TAPS):
                    ins = v.scalar_tensor_tensor(conv[:, n, :], upad[:, n, k:k + T], dw(k, n),
                                                 conv[:, n, :], ALU.mult, ALU.add)
                    if k < TAPS - 1:
                        link(ins)
                ins.then_inc(conv_ready, 1)
            for k in (2, 3, 4):
                mod_evac(k)
            v.tensor_tensor(ab[:, 2, :], mc(0, G1), colv("b_pw2", 0, KC), ALU.mult).then_inc(ab_ready, 1)
            gain_cols(1, 0, SC2, "norm2_g")
            v.wait_ge(mean_sum, 1)
            link(v.tensor_scalar(nrm[:, 2, :], psum[7][:, 0:T], 1.0 / D, None, ALU.mult))
            for kc in range(KC):
                v.tensor_tensor(conv[:, kc, :], conv[:, kc, :], nrm[:, 2, :], ALU.subtract).then_inc(cent_ready, 1)
            variance(1, None, None)
            rsqrt(1)
            scaled(conv, conv, lambda kc: col("ln_g", kc))
            for n in range(KC):
                v.wait_ge(pw2_tmp, n + 1)
                v.tensor_tensor(hT[:, n, :], hT[:, n, :], tmp[:, n % 2, 0:T], ALU.add).then_inc(h2_ready, 1)
            v.wait_ge(ab_ready, 3)
            variance(2, None, None)
            rsqrt(2)
            scaled(yT, hT, lambda kc: ab[:, 1, kc:kc + 1])

            mods = [i for k, i, w in STREAM if w == "dve"]
            done_mods = [0]

            def mod_tile():
                m = done_mods[0]
                done_mods[0] += 1
                n = WHERE[("mod", mods[m])]
                w = early(n, KC)
                v.wait_ge(arr[slot_of(n)], arrived_count(n))
                if m >= 2:
                    v.wait_ge(modp, 2 * PE_MODS + m - 1)
                dst = modacc[:, m % 2, :]
                link(v.tensor_scalar(dst, w[:, 0, :], cond[:, 0:1], None, ALU.mult))
                for kc in range(1, KC):
                    ins = v.scalar_tensor_tensor(dst, w[:, kc, :], cond[:, kc:kc + 1], dst, ALU.mult, ALU.add)
                    if kc < KC - 1:
                        link(ins)
                    else:
                        ins.then_inc(modacc_ready, 1)

            made = 0
            v.wait_ge(cond_ready, 1)
            evacs = 0
            for b in range(FBLOCKS):
                for f in (2 * b, 2 * b + 1):
                    v.wait_ge(gsil, f + 1)
                    if f >= 4:
                        v.wait_ge(down_used, f - 3)
                    v.tensor_tensor(hid[:, f % 4, :], psum[4 + f % 2][:, T:2 * T], tmp[:, f % 2, 0:T],
                                    ALU.mult).then_inc(hid_ready, 1)
                while evacs < done_mods[0] // 2:
                    mod_evac(PE_MODS + evacs)
                    evacs += 1
                for _ in range(MODS_AT[b]):
                    mod_tile()
                for _ in range(TABLES_AT[b]):
                    i = S5_TABLE_ORDER[made]
                    v.wait_ge(rnd_ready, made + 1)
                    link(v.scalar_tensor_tensor(tabc[:, made, :], iota_t[:, :], sp5[:, 13, i:i + 1],
                                                tabs[:, made, :], ALU.mult, ALU.subtract))
                    link(v.scalar_tensor_tensor(tabc[:, made, :], iota_t[:, :], sp5[:, 14, i:i + 1],
                                                tabc[:, made, :], ALU.mult, ALU.add))
                    v.tensor_scalar(tabc[:, made, :], tabc[:, made, :], -0.5, 0.5, ALU.max, ALU.min).then_inc(frac_ready, 1)
                    made += 1
            while evacs < 7:
                mod_evac(PE_MODS + evacs)
                evacs += 1
            gain_cols(3, 1, SC1, "norm1_g")
            gain_cols(4, 1, SC2, "norm2_g")
            v.wait_ge(down_used, 2 * FBLOCKS)
            for n in range(KC):
                v.scalar_tensor_tensor(hT[:, n, :], psum[n // 2][:, (n % 2) * T:(n % 2) * T + T], mc(0, G2, n),
                                       hT[:, n, :], ALU.mult, ALU.add).then_inc(h3_ready, 1)
            v.wait_ge(ab_ready, 5)
            variance(3, None, None)
            rsqrt(3)
            scaled(yT, hT, lambda kc: ab[:, 3, kc:kc + 1])

            v.wait_ge(tab_ready, TILES)
            ta, tb_ = tmp[:, 0, :], tmp[:, 1, :]
            for b in range(NB):
                m, qq = b // 4, b % 4
                ur, ui = psum[(b % 2) * 2][:, :], psum[(b % 2) * 2 + 1][:, :]
                tc = tabc[:, 2 * b:2 * b + 2, :].rearrange("p a t -> p (a t)")
                ts = tabs[:, 2 * b:2 * b + 2, :].rearrange("p a t -> p (a t)")
                xr = xrot[:, b % 2, 0, :, :].rearrange("p a t -> p (a t)")
                xi = xrot[:, b % 2, 1, :, :].rearrange("p a t -> p (a t)")
                v.wait_ge(bu_done, b + 1)
                if b >= 2:
                    v.wait_ge(prod_p, 2 * (b - 1))
                link(v.tensor_tensor(ta, ur, tc, ALU.mult))
                link(v.tensor_tensor(tb_, ui, ts, ALU.mult))
                link(v.tensor_tensor(xr, ta, tb_, ALU.add))
                link(v.tensor_tensor(ta, ui, tc, ALU.mult))
                v.tensor_tensor(tb_, ur, ts, ALU.mult).then_inc(bu_used, 1)
                v.wait_ge(bu_used, b + 1)
                link(v.tensor_tensor(xi, ta, tb_, ALU.subtract))
                for k in range(2):
                    i = (2 * m + k) * 4 + qq
                    mag = sp5[:, 5, i:i + 1].broadcast_to([P, T])
                    for c2 in range(2):
                        s = xrot[:, b % 2, c2, k, :]
                        ins = v.tensor_tensor_scan(s, mag, s, 0.0, ALU.mult, ALU.add)
                        if k == 0 or c2 == 0:
                            link(ins)
                ins.then_inc(scan_ready, 1)
                v.wait_ge(scan_ready, b + 1)
                if b:
                    v.wait_ge(prod_used, b)
                v.tensor_tensor(prod[:, 0, :, :].rearrange("p a t -> p (a t)"), tc, xr, ALU.mult).then_inc(prod_d, 1)
                v.scalar_tensor_tensor(prod[:, 1, :, :].rearrange("p a t -> p (a t)"), ts, -1.0, xi,
                                       ALU.mult, ALU.mult).then_inc(prod_d, 1)
                if b % 4 == 1 and b > 1:
                    mm = b // 4 - 1
                    v.wait_ge(prod_used, 4 * mm + 4)
                    for k in range(2):
                        kc = 2 * mm + k
                        v.scalar_tensor_tensor(yT[:, kc, :], yT[:, kc, :], col("ssm_d", kc),
                                               psum[4 + mm % 2][:, k * T:(k + 1) * T], ALU.mult, ALU.add).then_inc(ys_pre, 1)
            v.wait_ge(prod_used, NB)
            for k in range(2):
                kc = 6 + k
                v.scalar_tensor_tensor(yT[:, kc, :], yT[:, kc, :], col("ssm_d", kc),
                                       psum[5][:, k * T:(k + 1) * T], ALU.mult, ALU.add).then_inc(ys_pre, 1)
            for n in range(KC):
                v.wait_ge(sig_ready, KC + n + 1)
                v.scalar_tensor_tensor(tmp[:, n % 2, T:2 * T], psum[4 + n % 2][:, 0:T], col("b_glu", n),
                                       tmp[:, n % 2, 0:T], ALU.add, ALU.mult).then_inc(pair_used, 1)
                v.wait_ge(pair_used, KC + n + 1)
                v.scalar_tensor_tensor(hT[:, n, :], tmp[:, n % 2, T:2 * T], mc(1, G1, n), hT[:, n, :],
                                       ALU.mult, ALU.add).then_inc(h4_ready, 1)
            variance(4, None, None)
            rsqrt(4)
            scaled(yT, hT, lambda kc: ab[:, 4, kc:kc + 1])

            def r(n):
                return rt[:, n, :, :]

            def rb(n, c0):
                return rt[:, n, :, c0:c0 + 1].broadcast_to([P, TB, NE])

            v.wait_ge(log_done, TB)
            for tb in range(TB):
                link(v.tensor_copy(logit[:, tb, :], psum[6][:, 64 * tb:64 * tb + NE]))
            ie = iota_e[:, :].unsqueeze(1).broadcast_to([P, TB, NE])
            for k in range(2):
                src = logit[:, :, :] if k == 0 else r(3)
                link(v.tensor_reduce(rt[:, 5 + k, :, 0:1], src, axis=AX.X, op=ALU.max))
                link(v.tensor_tensor(r(7), src, rb(5 + k, 0), ALU.is_equal))
                link(v.tensor_scalar(r(8), ie, -1.0, float(NE), ALU.mult, ALU.add))
                link(v.tensor_tensor(r(7), r(7), r(8), ALU.mult))
                link(v.tensor_reduce(rt[:, 9, :, 0:1], r(7), axis=AX.X, op=ALU.max))
                link(v.tensor_tensor(r(k), r(8), rb(9, 0), ALU.is_equal))
                if k == 0:
                    link(v.tensor_scalar(r(3), r(0), -3.0e38, None, ALU.mult))
                    link(v.tensor_tensor(r(3), r(3), logit[:, :, :], ALU.add))
            v.tensor_tensor(r(2), r(0), r(1), ALU.add).then_inc(mask_ready, 1)
            v.tensor_tensor(rt[:, 4, :, 0], rt[:, 6, :, 0], rt[:, 5, :, 0], ALU.subtract).then_inc(exp2_in, 1)
            v.wait_ge(exp2, 1)
            link(v.tensor_scalar(rt[:, 4, :, 2], rt[:, 4, :, 1], 1.0, None, ALU.add))
            link(v.reciprocal(rt[:, 4, :, 3], rt[:, 4, :, 2]))
            link(v.tensor_tensor(rt[:, 4, :, 4], rt[:, 4, :, 3], rt[:, 4, :, 1], ALU.mult))
            link(v.tensor_tensor(r(0), r(0), rb(4, 3), ALU.mult))
            link(v.tensor_tensor(r(1), r(1), rb(4, 4), ALU.mult))
            link(v.tensor_tensor(r(10), r(0), r(1), ALU.add))
            v.wait_ge(rank_done, 1)
            for tb in range(TB):
                link(v.tensor_scalar(rt[:, 11, tb, :], psum[6][:, 128 + 64 * tb:128 + 64 * tb + NE], 999.0, None, ALU.add))
            link(v.tensor_tensor(r(11), r(11), r(2), ALU.mult))
            link(v.tensor_scalar(r(11), r(11), -1000.0, None, ALU.add))
            link(v.tensor_scalar(rt[:, 0, 0, :], psum[6][:, 256:256 + NE], float(P), None, ALU.is_gt))
            link(v.memset(rt[:, 0, 1, :], 1.0))
            link(v.tensor_tensor_scan(rt[:, 1, 0, :], rt[:, 0, 1, :], rt[:, 0, 0, :], 0.0, ALU.mult, ALU.add))
            link(v.memset(items[:, :, :], -1000.0))
            iv = items[:, 0:NE, :].rearrange("p e k -> p k e")
            link(v.tensor_copy(iv[:, 0:2, :], r(11)))
            link(v.tensor_copy(iv[:, 2:4, :], r(10)))
            for k in range(MAX_ITEMS - NE):
                link(v.scalar_tensor_tensor(rt[:, 3, 0, :], rt[:, 1, 0, :], float(k + 1), rt[:, 0, 0, :], ALU.is_equal, ALU.mult))
                link(v.tensor_tensor(rt[:, 3, 1, :], rt[:, 3, 0, :], iota_e[:, :], ALU.mult))
                link(v.tensor_reduce(rt[:, 5, 0, k:k + 1], rt[:, 3, 1, :], axis=AX.X, op=ALU.add))
                hot = rt[:, 3, 0:1, :].broadcast_to([P, TB, NE])
                link(v.tensor_scalar(r(7), r(11), -float(P), None, ALU.add))
                link(v.tensor_tensor(r(7), r(7), hot, ALU.mult))
                link(v.tensor_reduce(items[:, NE + k, 0:2].unsqueeze(2), r(7), axis=AX.X, op=ALU.add))
                link(v.tensor_tensor(r(7), r(10), hot, ALU.mult))
                link(v.tensor_reduce(items[:, NE + k, 2:4].unsqueeze(2), r(7), axis=AX.X, op=ALU.add))
            link(v.tensor_copy(over_i[:, 0:3], rt[:, 5, 0, 0:3]))
            v.tensor_scalar(count_i[:, :], rt[:, 1, 0, NE - 1:NE], float(NE), None, ALU.add).then_inc(items_ready, 1)
            v.wait_ge(items_ready, 1)
            v.wait_ge(consts, 6)
            for tb in range(TB):
                v.tensor_scalar(sel[:, tb, :], iota_s[:, :], items[:, 0, tb:tb + 1], None, ALU.is_equal).then_inc(sel_ready, 1)
            for kc in range(KC):
                if kc >= 4:
                    v.wait_ge(g2_done, 1)
                v.tensor_scalar(tmp[:, 0, (kc % 4) * P:(kc % 4) * P + P], ident[:, :], mc(1, G2, kc), None, ALU.mult).then_inc(diag_ready, 1)
            v.memset(selgT[:, :], 0.0).then_inc(selgT_zero, 1)
            for g in range(2):
                v.wait_ge(xh_ready, g + 1)
                v.tensor_tensor(xe_lo[:, 4 * g:4 * g + 4, :].rearrange("p k s -> p (k s)"), psum[7][:, :],
                                xe_hi[:, 4 * g:4 * g + 4, :].rearrange("p k s -> p (k s)").bitcast(F32),
                                ALU.subtract).then_inc(xl_ready, 1)
            v.wait_ge(g2row_ready, 2)

            def evac_y(i):
                v.wait_ge(lo_used, i * NH + LO_SLOTS)
                for h in range(2):
                    v.tensor_tensor(y_exp[:, h * 512:(h + 1) * 512], psum[4 + h][:, :],
                                    g2_row[:, h * 512:(h + 1) * 512], ALU.mult).then_inc(yx_ready, 1)

            def combined(i, m):
                tb, h = m // 2, m % 2
                v.wait_ge(comb_done, i * NCOMB + m + 1)
                v.tensor_tensor(acc[:, tb, h * 512:(h + 1) * 512], acc[:, tb, h * 512:(h + 1) * 512],
                                psum[7][:, :], ALU.add).then_inc(comb_used, 1)

            total = v.value_load(count_i[0:1, 0:1], min_val=NE, max_val=MAX_ITEMS)
            with v.Fori(0, total) as i:
                for n in range(NH):
                    s = n % RAW_SLOTS
                    v.wait_ge(hi_ready, i * NH + n + 1)
                    v.wait_ge(lo_used, i * NH + n + 1)
                    v.tensor_tensor(wlo[:, n % LO_SLOTS, :], ring[:, s * HW:(s + 1) * HW],
                                    whi[:, n % HI_SLOTS, :].bitcast(F32), ALU.subtract).then_inc(lo_ready, 1)
                    if n == 1:
                        evac_y(i)
                    if n >= 2 and n - 2 in COMB_AFTER:
                        combined(i, COMB_AFTER[n - 2])
                    if n >= 3 and HALVES[n - 3][0] == "U" and HALVES[n - 3][2] == 1:
                        j = HALVES[n - 3][1]
                        v.wait_ge(s_ready, i * FT + j + 1)
                        v.tensor_tensor(hid_e[:, :], silu_g[:, :], psum[2 + j % 2][:, :], ALU.mult).then_inc(he_ready, 1)
                    if n - 3 in T_AFTER:
                        j = T_AFTER[n - 3]
                        v.wait_ge(hh_ready, i * FT + j + 1)
                        v.tensor_tensor(hl[:, j % 2, :, :].rearrange("p k s -> p (k s)"), psum[6][:, :],
                                        hh[:, j % 2, :, :].rearrange("p k s -> p (k s)").bitcast(F32),
                                        ALU.subtract).then_inc(hl_ready, 1)
                    if n == AT[("G", 3, 0)]:
                        v.tensor_copy(now[:, 0:4], items[:, bass.ds(i, 1), :].rearrange("p a k -> p (a k)")).then_inc(now_ready, 1)
                        v.tensor_copy(now[:, 4:8], items[:, bass.ds(i + 1, 1), :].rearrange("p a k -> p (a k)")).then_inc(now_ready, 1)
                        v.wait_ge(now_ready, i * 2 + 2)
                        for tb in range(TB):
                            v.tensor_scalar(selg[:, tb, :], sel[:, tb, :], now[:, 2 + tb:3 + tb], None, ALU.mult).then_inc(selg_ready, 1)
                    if n == AT[("G", 4, 0)]:
                        v.wait_ge(selg_ready, i * TB + TB)
                        for tb in range(TB):
                            v.tensor_scalar(sel[:, tb, :], iota_s[:, :], now[:, 4 + tb:5 + tb], None, ALU.is_equal).then_inc(sel_ready, 1)
                    g = GATHER_AFTER.get(n - 2)
                    if g is not None:
                        v.wait_ge(xh_ready, i * 2 + g + 3)
                        v.tensor_tensor(xe_lo[:, 4 * g:4 * g + 4, :].rearrange("p k s -> p (k s)"), psum[7][:, :],
                                        xe_hi[:, 4 * g:4 * g + 4, :].rearrange("p k s -> p (k s)").bitcast(F32),
                                        ALU.subtract).then_inc(xl_ready, 1)
            evac_y(total)
            for m in range(NCOMB):
                tb, h = m // 2, m % 2
                v.wait_ge(comb_done, total * NCOMB + m + 1)
                ins = v.tensor_tensor(acc[:, tb, h * 512:(h + 1) * 512], acc[:, tb, h * 512:(h + 1) * 512],
                                      psum[m][:, :], ALU.add)
                ins.then_inc(acc_half, 1)
            v.wait_ge(act_own, 2 * TILES + TB)
            v.tensor_scalar(now[:, 6:8], now[:, 4:6], 1.0 / D, EPS, ALU.mult, ALU.add).then_inc(fin_var, 1)
            v.wait_ge(fin_std, 1)
            v.wait_ge(fin_var, 1)
            link(v.reciprocal(now[:, 0:2], now[:, 2:4]))
            link(v.tensor_tensor(now[:, 2:4], now[:, 6:8], now[:, 0:2], ALU.mult))
            link(v.scalar_tensor_tensor(now[:, 2:4], now[:, 2:4], -0.5, now[:, 0:2], ALU.mult, ALU.mult))
            link(v.scalar_tensor_tensor(now[:, 2:4], now[:, 2:4], 1.5, now[:, 0:2], ALU.add, ALU.mult))
            v.wait_ge(fg_in, 16)
            for tb in range(TB):
                v.scalar_tensor_tensor(acc[:, tb, :], acc[:, tb, :], now[:, 2 + tb:3 + tb], fin_g[:, :],
                                       ALU.mult, ALU.mult).then_inc(fin_ready, 1)

        @block.tensor
        def _(pe):
            mm = nc.tensor.matmul
            pe.wait_ge(consts, 2)
            pe.wait_ge(rows_ready, 1)
            for n, k in enumerate(ROW_TILES):
                nc.tensor.transpose(psum[0 if n < 4 else 1][:, (n % 4) * P:(n % 4) * P + k], rows[0:k, n, :],
                                    ident[0:k, 0:k]).then_inc(rows_t, 1)
            pe.wait_ge(x_in, 32)
            for n in range(4):
                if n >= 2:
                    pe.wait_ge(h_ready, n - 1)
                for k in range(2):
                    for tb in range(TB):
                        kc = 2 * n + k
                        ins = nc.tensor.transpose(psum[2 + n % 2][:, k * T + tb * P:k * T + (tb + 1) * P],
                                                  x_tok[:, tb, kc * P:(kc + 1) * P], ident[:, :])
                ins.then_inc(x_t, 1)

            def sums(base, ready, src, done):
                for kc in range(KC):
                    pe.wait_ge(ready, base + kc + 1)
                    ins = mm(psum[7][:, 0:T], ones[:, :], src[:, kc, :], start=kc == 0, stop=kc == KC - 1)
                ins.then_inc(done, 1)

            def pairs(kind, k0, ready):
                for n in range(KC):
                    t = WHERE[(kind, n // 2)]
                    if n % 2 == 0:
                        pe.wait_ge(arr[slot_of(t)], arrived_count(t))
                    w = early(t, KC)
                    if k0 + n >= 2:
                        pe.wait_ge(pair_used, k0 + n - 1)
                    for kc in range(KC):
                        if n == 0:
                            pe.wait_ge(ready, kc + 1 if k0 == 0 else KC)
                        mm(psum[4 + n % 2][:, 0:T], w[:, kc, (n % 2) * P:(n % 2) * P + P], yT[:, kc, :],
                           start=kc == 0, stop=kc == KC - 1)
                    for kc in range(KC):
                        o = 256 + (n % 2) * P
                        ins = mm(psum[4 + n % 2][:, T:2 * T], w[:, kc, o:o + P], yT[:, kc, :],
                                 start=kc == 0, stop=kc == KC - 1)
                    ins.then_inc(pair_done, 1)

            def mod_columns(k):
                l, m = MOD_ORDER[k]
                for h in range(2):
                    n = WHERE[("mod", (l, m, h))]
                    pe.wait_ge(arr[slot_of(n)], arrived_count(n))
                    w = early(n, KC)
                    for o in range(4):
                        for kc in range(KC):
                            ins = mm(psum[MOD_BANK[k]][:, 4 * h + o:4 * h + o + 1],
                                     w[:, kc, o * P:(o + 1) * P], cond[:, kc:kc + 1],
                                     start=kc == 0, stop=kc == KC - 1)
                    ins.then_inc(modp, 1)

            def mod_sums(m):
                k, h = PE_MODS + m // 2, m % 2
                if h == 0:
                    pe.wait_ge(modc_ready, k - 1)
                pe.wait_ge(modacc_ready, m + 1)
                for o in range(4):
                    ins = mm(psum[MOD_BANK[k]][:, 4 * h + o:4 * h + o + 1], modacc[:, h, o * P:(o + 1) * P],
                             ones[:, 0:1], start=True, stop=True)
                ins.then_inc(modp, 1)

            sums(0, sq_ready, sq, sum_ready)
            pe.wait_ge(cond_ready, 1)
            mod_columns(0)
            pe.wait_ge(h_ready, 4)
            mod_columns(1)
            pairs("pw1", 0, y_ready)
            pe.wait_ge(modc_ready, 2)
            for k in (2, 3, 4):
                mod_columns(k)
            pe.wait_ge(blk_ready, 8)
            for n in range(8):
                if n >= 2:
                    pe.wait_ge(blk_c, n - 1)
                src = bblk[n // 2] if n < 4 else cblk[n // 2 - 2]
                for k in range(4):
                    kc = (n % 2) * 4 + k
                    a = src[:, 4 * kc:4 * kc + 4, :].rearrange("p i c -> p (i c)") if n < 4 else src[:, kc, :]
                    ins = nc.tensor.transpose(psum[n % 2][:, k * P:(k + 1) * P], a, ident[:, :])
                ins.then_inc(blk_t, 1)

            sums(0, conv_ready, conv, mean_sum)
            pe.wait_ge(cent_ready, 1)
            sums(KC, sq_ready, sq, sum_ready)
            for n in range(KC):
                t = WHERE[("pw2", n // 4)]
                if n % 4 == 0:
                    pe.wait_ge(arr[slot_of(t)], arrived_count(t))
                if n >= 2:
                    pe.wait_ge(pw2_tmp, n - 1)
                w = early(t, KC)
                for kc in range(KC):
                    if n == 0:
                        pe.wait_ge(y_ready, KC + kc + 1)
                    ins = mm(psum[4 + n % 2][:, 0:T], w[:, kc, (n % 4) * P:(n % 4) * P + P], yT[:, kc, :],
                             start=kc == 0, stop=kc == KC - 1)
                ins.then_inc(pw2_done, 1)
            sums(2 * KC, sq_ready, sq, sum_ready)

            def down(b):
                t = WHERE[("down", b)]
                pe.wait_ge(arr[slot_of(t)], arrived_count(t))
                w = early(t, 4)
                for k in range(2):
                    f = 2 * b + k
                    if f == 0:
                        pe.wait_ge(modc_ready, PE_MODS)
                    pe.wait_ge(hid_ready, f + 1)
                    for n in range(KC):
                        ins = mm(psum[n // 2][:, (n % 2) * T:(n % 2) * T + T], w[:, k, n * P:(n + 1) * P],
                                 hid[:, f % 4, :], start=f == 0 and n % 2 == 0, stop=f == 2 * FBLOCKS - 1,
                                 skip_group_check=True)
                    ins.then_inc(down_used, 1)

            for b in range(FBLOCKS):
                t = WHERE[("gu", b)]
                pe.wait_ge(arr[slot_of(t)], arrived_count(t))
                w = early(t, KC)
                for k in range(2):
                    f = 2 * b + k
                    if f >= 2:
                        pe.wait_ge(hid_ready, f - 1)
                    for g in range(2):
                        for kc in range(KC):
                            if f == 0 and g == 0:
                                pe.wait_ge(y_ready, 2 * KC + kc + 1)
                            o = g * 256 + k * P
                            ins = mm(psum[4 + f % 2][:, g * T:(g + 1) * T], w[:, kc, o:o + P], yT[:, kc, :],
                                     start=kc == 0, stop=kc == KC - 1)
                    ins.then_inc(gu_done, 1)
                for m in range(sum(MODS_AT[:max(b - 1, 0)]), sum(MODS_AT[:b])):
                    mod_sums(m)
                if b:
                    down(b - 1)
            mod_sums(sum(MODS_AT) - 1)
            down(FBLOCKS - 1)
            sums(3 * KC, sq_ready, sq, sum_ready)

            def b_products(b):
                m, qq = b // 4, b % 4
                if b >= 2:
                    pe.wait_ge(bu_used, b - 1)
                for k in range(2):
                    kc = 2 * m + k
                    pe.wait_ge(y_ready, 3 * KC + kc + 1)
                    rows_q = slice(32 * qq, 32 * qq + 32)
                    for c2 in range(2):
                        ins = mm(psum[(b % 2) * 2 + c2][:, k * T:(k + 1) * T], bbT[c2][rows_q, kc, :],
                                 yT[rows_q, kc, :], start=True, stop=True)
                ins.then_inc(bu_done, 1)

            def c_products(b):
                m, qq = b // 4, b % 4
                if qq == 0 and m >= 2:
                    pe.wait_ge(ys_pre, 2 * (m - 1))
                pe.wait_ge(prod_d, 2 * b + 2)
                pe.wait_ge(prod_p, 2 * b + 2)
                for k in range(2):
                    kc = 2 * m + k
                    for t in range(4):
                        ins = mm(psum[4 + m % 2][32 * qq:32 * qq + 32, k * T:(k + 1) * T],
                                 cT[t // 2][:, kc, 32 * qq:32 * qq + 32], prod[:, t, k, :],
                                 start=t == 0, stop=t == 3)
                ins.then_inc(prod_used, 1)

            b_products(0)
            for b in range(NB):
                if b + 1 < NB:
                    b_products(b + 1)
                c_products(b)
            pairs("glu", KC, z_ready)
            sums(4 * KC, sq_ready, sq_late, sum_ready)

            pe.wait_ge(wr_in, 32)
            for tb in range(TB):
                for kc in range(KC):
                    pe.wait_ge(y_ready, 4 * KC + kc + 1)
                    mm(psum[6][:, 64 * tb:64 * tb + NE], yT[:, kc, tb * P:(tb + 1) * P], wr[:, kc, :],
                       start=kc == 0, stop=False)
                mm(psum[6][:, 64 * tb:64 * tb + NE], ones[0:1, :], brow[0:1, :], start=False, stop=True).then_inc(log_done, 1)
            for n in range(8):
                if n >= 4:
                    pe.wait_ge(tok_c, n - 3)
                src, tb, h = (hT if n < 4 else yT), (n // 2) % 2, n % 2
                for k in range(4):
                    ins = nc.tensor.transpose(psum[n % 4][:, k * P:(k + 1) * P],
                                              src[:, 4 * h + k, tb * P:(tb + 1) * P], ident[:, :])
                ins.then_inc(tok_t, 1)
            pe.wait_ge(mask_ready, 1)
            pe.wait_ge(consts, 6)
            mm(psum[6][:, 128:128 + NE], tri[:, :], rt[:, 2, 0, :], start=True, stop=True)
            mm(psum[6][:, 192:192 + NE], tri[:, :], rt[:, 2, 1, :], start=True, stop=False)
            mm(psum[6][:, 192:192 + NE], ones[:, :], rt[:, 2, 0, :], start=False, stop=True)
            mm(psum[6][:, 256:256 + NE], ones[:, :], rt[:, 2, 0, :], start=True, stop=False)
            mm(psum[6][:, 256:256 + NE], ones[:, :], rt[:, 2, 1, :], start=False, stop=True).then_inc(rank_done, 1)

            def gather(k, g):
                pe.wait_ge(sel_ready, k)
                for c4 in range(4):
                    kc = 4 * g + c4
                    for tb in range(TB):
                        ins = mm(psum[7][:, c4 * P:(c4 + 1) * P], y_tok[:, tb, kc * P:(kc + 1) * P], sel[:, tb, :],
                                 start=tb == 0, stop=tb == TB - 1)
                ins.then_inc(gath_done, 1)

            for kc in range(KC):
                pe.wait_ge(diag_ready, kc + 1)
                ins = mm(psum[4 + kc // 4][:, (kc % 4) * P:(kc % 4) * P + P], ones[:, :],
                         tmp[:, 0, (kc % 4) * P:(kc % 4) * P + P], start=True, stop=True)
                if kc % 4 == 3:
                    ins.then_inc(g2_done, 1)
            pe.wait_ge(tok_c, 8)
            gather(TB, 0)
            pe.wait_ge(xl_ready, 1)
            gather(TB, 1)
            pe.wait_ge(g2row_ready, 2)
            pe.wait_ge(selgT_zero, 1)
            for bank, free, slots in ((4, hi_used, HI_SLOTS), (5, lo_used, LO_SLOTS)):
                for k in range(4):
                    ins = mm(psum[bank][:, k * P:(k + 1) * P], selgT[:, 0:P], ones[:, :], start=True, stop=True)
                ins.then_inc(free, slots)

            pe.wait_ge(items_ready, 1)
            total = pe.value_load(count_i[0:1, 0:1], min_val=NE, max_val=MAX_ITEMS)

            def product(i, n):
                kind, j, h = HALVES[n]
                pe.wait_ge(hi_ready, i * NH + n + 1)
                hi, lo = whi[:, n % HI_SLOTS, :], wlo[:, n % LO_SLOTS, :]
                if kind == "D":
                    if h == 0:
                        pe.wait_ge(hl_ready, i * FT + j + 1)
                        if j == 0:
                            pe.wait_ge(yx_ready, (i + 1) * 2)
                    steps = [(hh[:, j % 2, 2 * h + k, :], hl[:, j % 2, 2 * h + k, :], psum[4 + s],
                              (k * D + s * 512), j == 0 and h == 0 and k == 0, j == FT - 1 and h == 1 and k == 1)
                             for k in range(2) for s in range(2)]
                else:
                    if n == 0:
                        pe.wait_ge(xl_ready, i * 2 + 2)
                    bank = psum[(0 if kind == "G" else 2) + j % 2]
                    steps = [(xe_hi[:, 4 * h + k, :], xe_lo[:, 4 * h + k, :], bank, k * 512,
                              h == 0 and k == 0, h == 1 and k == 3) for k in range(4)]
                for k, (xh, xl, o, w, first, last) in enumerate(steps):
                    mm(o[:, :], xh, hi[:, w:w + 512], start=first, stop=False)
                    if k == len(steps) - 1:
                        pe.wait_ge(lo_ready, i * NH + n + 1)
                    ins = mm(o[:, :], xl, hi[:, w:w + 512], start=False, stop=False)
                ins.then_inc(hi_used, 1)
                for xh, xl, o, w, first, last in steps:
                    ins = mm(o[:, :], xh, lo[:, w:w + 512], start=False, stop=last)
                ins.then_inc(lo_used, 1)

            def combine(i, m, bank):
                tb, h = m // 2, m % 2
                if m == 0:
                    pe.wait_ge(yx_ready, (i + 1) * 2)
                mm(bank[:, :], selgT[:, tb * P:(tb + 1) * P], y_exp[:, h * 512:(h + 1) * 512],
                   start=True, stop=True).then_inc(comb_done, 1)

            with pe.Fori(0, total) as i:
                for n in range(NH):
                    product(i, n)
                    if n in COMB_AFTER:
                        m = COMB_AFTER[n]
                        if m:
                            pe.wait_ge(comb_used, i * NCOMB + m)
                        combine(i, m, psum[7])
                    if n == SGT_AFTER:
                        pe.wait_ge(comb_used, (i + 1) * NCOMB)
                        pe.wait_ge(selg_ready, (i + 1) * TB)
                        for tb in range(TB):
                            ins = nc.tensor.transpose(psum[7][:, tb * P:(tb + 1) * P], selg[:, tb, :], ident[:, :])
                        ins.then_inc(selg_t, 1)
                    if n in GATHER_AFTER:
                        g = GATHER_AFTER[n]
                        if g == 0:
                            pe.wait_ge(selgT_ready, i + 1)
                            gather(i * TB + 2 * TB, 0)
                        else:
                            pe.wait_ge(xl_ready, i * 2 + 3)
                            gather(i * TB + 2 * TB, 1)
                    if n in T_AFTER:
                        j = T_AFTER[n]
                        pe.wait_ge(he_ready, i * FT + j + 1)
                        if j:
                            pe.wait_ge(hl_ready, i * FT + j)
                        for k in range(4):
                            ins = nc.tensor.transpose(psum[6][:, k * P:(k + 1) * P], hid_e[:, k * P:(k + 1) * P], ident[:, :])
                        ins.then_inc(t_done, 1)
            pe.wait_ge(selgT_ready, total)
            for m in range(NCOMB):
                combine(total, m, psum[m])


_INS = ["x", "c", "mod_w", "mod_b", "norm1_g", "norm2_g", "conv_w_pw1", "conv_b_pw1", "conv_w_dw",
        "conv_b_dw", "conv_ln_g", "conv_ln_b", "conv_w_pw2", "conv_b_pw2", "ssm_a_re", "ssm_a_im",
        "ssm_log_dt", "ssm_b_re", "ssm_b_im", "ssm_c_re", "ssm_c_im", "ssm_d", "ssm_w_glu",
        "ssm_b_glu", "ffn_w_gate", "ffn_w_up", "ffn_w_down", "moe_w_router", "moe_b_router",
        "moe_w_gate", "moe_w_up", "moe_w_down", "final_norm_g"]


def kernel(**inputs):
    import numpy as _np
    import concourse.bacc as _bacc
    from concourse import mybir as _mybir
    from concourse.bass_utils import run_bass_kernel_spmd as _run

    nc = _bacc.Bacc("TRN2", target_bir_lowering=False, num_devices=1)
    arrays, args = {}, []
    for name in _INS:
        a = _np.ascontiguousarray(inputs[name])
        arrays[f"in_{name}_dram"] = a
        args.append(nc.dram_tensor(f"in_{name}_dram", a.shape, _mybir.dt.from_np(a.dtype),
                                   kind="ExternalInput").ap())
    o = nc.dram_tensor("out_dram", (1, T, D), F32, kind="ExternalOutput").ap()
    trunk(nc, *args, o)
    r = _run(nc, [arrays], core_ids=[0])
    return r.results[0]["out_dram"]
```

```python
from contextlib import ExitStack

import numpy as np
import concourse.bass as bass
from concourse import mybir

F32 = mybir.dt.float32
F32R = mybir.dt.float32r
I32 = mybir.dt.int32
ACT = mybir.ActivationFunctionType
ALU = mybir.AluOpType
AX = mybir.AxisListType

P = 128
D, T, DEPTH = 1024, 256, 2
KC = D // P
TB = T // P
TAPS = 31
PE_TAPS = 5
GROUPS, GC, NS = 64, 16, 64
TILES = GROUPS * NS // P
FD, FE, NE = 2816, 3584, 8
FBLOCKS = FD // 256
EPS = 1e-6

EARLY_SLOTS = 4
SH1, SC1, G1, SH2, SC2, G2 = range(6)
MOD_ORDER = [(0, SC1), (0, SH1), (0, SC2), (0, SH2), (0, G1), (0, G2),
             (1, SC1), (1, SH1), (1, G1), (1, SC2), (1, SH2), (1, G2)]
CONV_MODS, NORM_MODS, FFN_MODS, S5_MODS = 2, 4, 6, 8
FFN_MOD_BLOCKS = (2, 4, 6, 8)


def early_stream():
    mods = [("mod", 2 * k + h) for k in range(len(MOD_ORDER)) for h in range(2)]
    tiles = mods[:2 * CONV_MODS]
    for q in range(4):
        tiles += [("pw1", q), mods[2 * CONV_MODS + q]]
    tiles += mods[2 * NORM_MODS:2 * NORM_MODS + 2] + [("pw2", q) for q in range(2)]
    late = mods[2 * FFN_MODS:2 * S5_MODS]
    for b in range(FBLOCKS):
        tiles.append(("gu", b))
        if b == 0:
            tiles += mods[2 * NORM_MODS + 2:2 * FFN_MODS]
        if b in FFN_MOD_BLOCKS:
            tiles.append(late.pop(0))
        if b:
            tiles.append(("down", b - 1))
    tiles.append(("down", FBLOCKS - 1))
    tiles += mods[2 * S5_MODS:]
    tiles += [("glu", q) for q in range(4)]
    assert not late
    return tiles


STREAM = early_stream()
SHIFT = -len(STREAM) % EARLY_SLOTS
WHERE = {(k, i): n for n, (k, i) in enumerate(STREAM)}
DMAS_OF = {"mod": 1, "pw1": 2, "pw2": 1, "gu": 2, "down": 1, "glu": 2}


def slot_of(n):
    return (n + SHIFT) % EARLY_SLOTS


def arrived_count(n):
    return 16 * sum(DMAS_OF[STREAM[m][0]] for m in range(n + 1) if slot_of(m) == slot_of(n))


def consumed(n):
    kind, i = STREAM[n]
    return {"mod": ("mod_part", i + 1),
            "pw1": ("pair_done", 2 * i + 2), "glu": ("pair_done", KC + 2 * i + 2),
            "pw2": ("pw2_done", 4 * i + 4), "gu": ("gu_done", 2 * i + 2),
            "down": ("down_used", 2 * i + 2)}[kind]


def split_units():
    out = [("pw2", q, h) for q in range(2) for h in range(2)]
    for b in range(FBLOCKS):
        out += [("gu", b, k) for k in range(2)]
        if b:
            out.append(("down", b - 1, 0))
    out.append(("down", FBLOCKS - 1, 0))
    return out + [("glu", q, k) for q in range(4) for k in range(2)]


UNITS = split_units()
UNIT = {x: n for n, x in enumerate(UNITS)}


def unit_used(u):
    kind, i, k = UNITS[u]
    return {"pw2": ("pw2_done", 4 * i + 2 * k + 2), "gu": ("gu_done", 2 * i + k + 1),
            "down": ("down_used", 2 * i + 2), "glu": ("pair_done", KC + 2 * i + k + 1)}[kind]


FT = FE // 512


def expert_halves():
    out = []
    for j in range(FT):
        out += [("G", j, h) for h in range(2)] + [("U", j, h) for h in range(2)]
        if j >= 2:
            out += [("D", j - 2, h) for h in range(2)]
    return out + [("D", j, h) for j in (FT - 2, FT - 1) for h in range(2)]


HALVES = expert_halves()
NH = len(HALVES)
AT = {x: n for n, x in enumerate(HALVES)}
RAW_SLOTS = 14
HI_SLOTS, LO_SLOTS = 3, 2
assert NH % RAW_SLOTS == 0 and NH % HI_SLOTS == 0 and NH % LO_SLOTS == 0
HW = 2048
T_AFTER = {AT[("U", j + 1, 1)]: j for j in range(FT - 1)}
T_AFTER[AT[("D", FT - 3, 1)]] = FT - 1
NCOMB = 2 * TB
COMB_AFTER = {AT[("U", m, 1)]: m for m in range(NCOMB)}
SGT_AFTER = AT[("U", 4, 1)]
GATHER_AFTER = {AT[("D", FT - 3, 1)]: 0, AT[("D", FT - 2, 1)]: 1}
MAX_ITEMS = NE + 3

MAGIC = 1.5 * 2.0 ** 23
LOG2E = 1.4426950408889634
LN2_HI, LN2_LO = 0.693359375, -2.12194440e-4
TWO_PI = [6.28125, 0.0019350051879882812, 3.0199159819567e-7]
EXP_COEF = [1.0 / 5040, 1.0 / 720, 1.0 / 120, 1.0 / 24, 1.0 / 6, 0.5, 1.0]

ROWS = {}
for _tile, _names in enumerate([
        [("mod_b", 96)],
        [("dw_lo", 128)],
        [("dw_hi", TAPS * KC - 128)],
        [("c", 8), ("norm1_g", 16), ("norm2_g", 16), ("b_pw1", 16), ("b_dw", 8), ("ln_g", 8),
         ("ln_b", 8), ("b_pw2", 8), ("ssm_d", 8), ("b_glu", 16)],
        [("a_re", 32), ("a_im", 32), ("log_dt", 32)]]):
    _r = 0
    for _n, _k in _names:
        ROWS[_n] = (_tile, _r, _k)
        _r += _k
ROW_TILES = [96, 128, TAPS * KC - 128, 112, 96]


def trunk(nc, x, c, mod_w, mod_b, norm1_g, norm2_g, w_pw1, b_pw1, w_dw, b_dw, ln_g, ln_b, w_pw2,
          b_pw2, a_re, a_im, log_dt, b_re, b_im, c_re, c_im, ssm_d, w_glu, b_glu, w_gate, w_up,
          w_down, w_router, b_router, e_gate, e_up, e_down, final_g, out):
    ctx = ExitStack()
    with ctx:
        BASE = 16512

        def at(name, shape, offset, dtype=F32):
            return nc.alloc_sbuf_tensor_at(name, shape, dtype, offset=BASE + offset)

        def sem(name):
            return ctx.enter_context(nc.semaphore(name))

        KB = 1024
        ring = at("ring", [P, RAW_SLOTS * HW], 0)
        ring_lo = at("ring_lo", [P, EARLY_SLOTS * 4096], 0, F32R)
        ehi = at("ehi", [P, 2, 2048], 64 * KB, F32R)
        LOW = 80 * KB
        bbT = [at(f"bbT_{n}", [P, KC, P], LOW + 4 * KB * n) for n, _ in enumerate("ri")]
        cT = [at(f"cT_{n}", [P, KC, P], LOW + 8 * KB + 4 * KB * n) for n, _ in enumerate("ri")]
        modacc = at("modacc", [P, 2, 512], LOW + 16 * KB)
        diag = at("diag", [P, 2, PE_TAPS, P], LOW + 24 * KB)
        hid = at("hid", [P, 4, T], LOW + 20 * KB)
        hid_lo = at("hid_lo", [P, 4, T], LOW + 20 * KB, F32R)
        hid_hi = at("hid_hi", [P, 4, T], LOW + 16 * KB, F32R)
        xrot = at("xrot", [P, 2, 2, 2, T], LOW + 16 * KB)
        sq = at("sq", [P, KC, T], LOW + 24 * KB)
        y_hi = at("y_hi", [P, KC, T], LOW + 24 * KB, F32R)
        prod = at("prod", [P, 4, 2, T], LOW + 24 * KB)
        B = 112 * KB
        x_tok = at("x_tok", [P, TB, D], B)
        PAD = T + TAPS - 1
        upad = at("upad", [P, KC, PAD], B + 8 * KB)
        conv = at("conv", [P, KC, T], B + 17 * KB + 512)
        rows = at("rows", [P, len(ROW_TILES), P], B + 26 * KB)
        braw = [at(f"braw_{n}", [P, TILES, GC], B + 29 * KB + 2 * KB * n) for n in range(2)]
        bblk = [at(f"bblk_{n}", [P, TILES, 2 * GC], B + 33 * KB + 4 * KB * n) for n in range(2)]
        craw = [at(f"craw_{n}", [P, KC, NS], B + 41 * KB + 2 * KB * n) for n in range(2)]
        cblk = [at(f"cblk_{n}", [P, KC, P], B + 45 * KB + 4 * KB * n) for n in range(2)]
        btmp = [at(f"btmp_{n}", [P, TILES, GC], B + 53 * KB + 2 * KB * n) for n in range(4)]
        tabc = at("tabc", [P, TILES, T], B)
        tabs = at("tabs", [P, TILES, T], B + 32 * KB)
        cT_neg = at("cT_neg", [P, KC, P], 64 * KB)
        z_hi = at("z_hi", [P, KC, T], B, F32R)
        whi = at("whi", [P, HI_SLOTS, HW], B, F32R)
        wlo = at("wlo", [P, LO_SLOTS, HW], B + 24 * KB, F32R)
        acc = at("acc", [P, TB, D], B + 40 * KB)
        sq_late = at("sq_late", [P, KC, T], B + 40 * KB)
        y_tok = at("y_tok", [P, TB, D], B + 48 * KB)
        g2_row = at("g2_row", [P, D], B + 56 * KB)
        y_exp = at("y_exp", [P, D], B + 60 * KB)
        fin_g = at("fin_g", [P, D], 0)
        fin_sq = at("fin_sq", [P, D], 4 * KB)
        hT = at("hT", [P, KC, T], 176 * KB)
        yT = at("yT", [P, KC, T], 184 * KB)
        y_lo = at("y_lo", [P, KC, T], 184 * KB, F32R)
        xe_hi = at("xe_hi", [P, KC, P], 176 * KB, F32R)
        xe_lo = at("xe_lo", [P, KC, P], 180 * KB, F32R)
        hh = at("hh", [P, 2, 4, P], 184 * KB, F32R)
        hl = at("hl", [P, 2, 4, P], 188 * KB, F32R)
        M = 192 * KB
        ident = at("ident", [P, P], M)
        ones = at("ones", [P, P], M + 512)
        cols = at("cols", [P, len(ROW_TILES), P], M + 1024)
        modc = at("modc", [P, DEPTH * 6, KC], M + 3584)
        ab = at("ab", [P, 8, KC], M + 3968)
        cond = at("cond", [P, KC, 32], B + 61 * KB)
        cond_late = at("cond_late", [P, KC, 32], M + 1024 + 512)
        zeros = at("zeros", [P, P], M + 1024 + 512)
        sum_col = at("sum_col", [P, 1], M + 4224)
        modraw = at("modraw", [P, DEPTH * 6, KC], M + 15616)
        sp5 = at("sp5", [P, 20, TILES], M + 4256)
        sp5i = at("sp5i", [P, TILES], M + 6816, I32)
        masks = at("masks", [P, 4], M + 6944)
        iota_t = at("iota_t", [P, T], M + 6976)
        nrm = at("nrm", [P, 3, T], M + 8000)
        modacc_s5 = at("modacc_s5", [P, 512], M + 8000)
        sel = at("sel", [P, TB, P], M + 8000)
        selg = at("selg", [P, TB, P], M + 9024)
        selgT = at("selgT", [P, T], M + 10048)
        tmp = at("tmp", [P, 2, 512], M + 11072)
        silu_g = at("silu_g", [P, 512], M + 11072)
        hid_e = at("hid_e", [P, 512], M + 13120)
        rt = at("rt", [P, 12, TB, NE], M + 4256)
        tri = at("tri", [P, P], M + 6976)
        iota_s = at("iota_s", [P, P], M + 6976 + 512)
        wr = at("wr", [P, KC, NE], B)
        logT = at("logT", [NE, T], B + 24 * KB)
        R = M + 15168
        logit = at("logit", [P, TB, NE], R)
        items = at("items", [P, MAX_ITEMS + 1, 4], R + 64)
        now = at("now", [P, 8], R + 256)
        count_i = at("count_i", [P, 1], R + 288, I32)
        iota_e = at("iota_e", [P, NE], R + 320)
        bcol = at("bcol", [NE, 1], R + 352)
        over_i = at("over_i", [P, 4], R + 384, I32)
        ldt_rows = at("ldt_rows", [P, 4], R + 416)

        psum = [ctx.enter_context(nc.psum_tensor(f"bank{n}", [P, 512], F32)) for n in range(8)]

        def col(name, i=0):
            tile, r, _ = ROWS[name]
            return cols[:, tile, r + i:r + i + 1]

        def colv(name, i, n):
            tile, r, _ = ROWS[name]
            return cols[:, tile, r + i:r + i + n]

        def dw(tap, kc):
            r = tap * KC + kc
            return cols[:, 1 + r // P, r % P:r % P + 1]

        def early(n, parts):
            s = slot_of(n)
            return ring[:, s * 4096:(s + 1) * 4096].rearrange("p (k n) -> p k n", k=parts)

        def unit_views(u):
            kind, i, k = UNITS[u]
            s = slot_of(WHERE[(kind, i)])
            hi = ehi[:, u % 2, :]
            if kind == "down":
                w, lo = (t[:, s * 4096:s * 4096 + 2048].rearrange("p (k g n) -> p k g n", k=2, g=2)
                         for t in (ring, ring_lo))
                return w, lo, hi.rearrange("p (k g n) -> p k g n", k=2, g=2)
            w, lo = (t[:, s * 4096:(s + 1) * 4096].rearrange("p (k n) -> p k n", k=KC)
                     for t in (ring, ring_lo))
            if kind == "pw2":
                w, lo = (t[:, :, k * 256:(k + 1) * 256].rearrange("p k (g n) -> p k g n", g=2) for t in (w, lo))
            else:
                w, lo = (t.rearrange("p k (g n) -> p k g n", g=2)[:, :, :, k * P:(k + 1) * P] for t in (w, lo))
            return w, lo, hi.rearrange("p (k g n) -> p k g n", k=KC, g=2)

        x_in, rows_in, s5_in, wr_in, fg_in, out_done = (
            sem(n) for n in ("x_in", "rows_in", "s5_in", "wr_in", "fg_in", "out_done"))
        arr = [sem(f"arr{n}") for n in range(EARLY_SLOTS)]
        consts = sem("consts")
        rows_ready = sem("rows_ready")
        rows_t, cols_ready = sem("rows_t"), sem("cols_ready")
        cond_ready, sum_col_ready = sem("cond_ready"), sem("sum_col_ready")
        x_t, h_ready = sem("x_t"), sem("h_ready")
        mod_part, mod_acc, mod_sum, mod_raw, modc_ready = (
            sem(n) for n in ("mod_part", "mod_acc", "mod_sum", "mod_raw", "modc_ready"))
        ab_ready = sem("ab_ready")
        sq_ready, sum_ready, var_ready, std_ready = (sem(n) for n in ("sq_ready", "sum_ready", "var_ready", "std_ready"))
        raw_ready, y_ready = sem("raw_ready"), sem("y_ready")
        pair_done, sig_ready, pair_used = sem("pair_done"), sem("sig_ready"), sem("pair_used")
        conv_ready, mean_sum, cent_ready = sem("conv_ready"), sem("mean_sum"), sem("cent_ready")
        pw2_done, pw2_tmp, h2_ready = sem("pw2_done"), sem("pw2_tmp"), sem("h2_ready")
        gu_done, gsil, hid_ready, down_used = (sem(n) for n in ("gu_done", "gsil", "hid_ready", "down_used"))
        h3_ready, h4_ready = sem("h3_ready"), sem("h4_ready")
        ehi_ready, elo_ready = sem("ehi_ready"), sem("elo_ready")
        yhi_ready, ylo_ready = sem("yhi_ready"), sem("ylo_ready")
        hidhi_ready, hidlo_ready = sem("hidhi_ready"), sem("hidlo_ready")
        diag_made, taps_done = sem("diag_made"), sem("taps_done")
        chain, tap = sem("chain"), sem("tap")
        blk_ready, blk_t, blk_c = sem("blk_ready"), sem("blk_t"), sem("blk_c")
        trig_in, trig, trig_out = sem("trig_in"), sem("trig"), sem("trig_out")
        rnd_ready, frac_ready, sin_ready, tab_ready = (sem(n) for n in ("rnd_ready", "frac_ready", "sin_ready", "tab_ready"))
        act_own, pool_own = sem("act_own"), sem("pool_own")
        ones_pad = sem("ones_pad")
        bu_done, bu_used, scan_ready, prod_p, prod_used, ys_pre, z_ready = (
            sem(n) for n in ("bu_done", "bu_used", "scan_ready", "prod_p", "prod_used",
                             "ys_pre", "z_ready"))
        cneg_ready = sem("cneg_ready")
        log_done, rank_done, mask_ready, diag_ready, g2_done = (
            sem(n) for n in ("log_done", "rank_done", "mask_ready", "diag_ready", "g2_done"))
        logT_ready, logit_t = sem("logT_ready"), sem("logit_t")
        tok_t, tok_c, exp2_in, exp2 = sem("tok_t"), sem("tok_c"), sem("exp2_in"), sem("exp2")
        items_ready, g2row_ready, over_ready = sem("items_ready"), sem("g2row_ready"), sem("over_ready")
        raw_in = [sem(f"raw_in{n}") for n in range(RAW_SLOTS)]
        hi_ready, lo_ready, hi_used, lo_used = (sem(n) for n in ("hi_ready", "lo_ready", "hi_used", "lo_used"))
        s_ready, he_ready, t_done, hh_ready, hl_ready = (
            sem(n) for n in ("s_ready", "he_ready", "t_done", "hh_ready", "hl_ready"))
        yx_ready, comb_done, comb_used = (sem(n) for n in ("yx_ready", "comb_done", "comb_used"))
        sel_ready, selg_ready, selg_t, selgT_ready = (sem(n) for n in ("sel_ready", "selg_ready", "selg_t", "selgT_ready"))
        gath_done, xh_ready, xl_ready = sem("gath_done"), sem("xh_ready"), sem("xl_ready")
        fin_var, fin_std, fin_ready = (sem(n) for n in ("fin_var", "fin_std", "fin_ready"))
        selgT_zero, now_ready, acc_half = sem("selgT_zero"), sem("now_ready"), sem("acc_half")

        block = ctx.enter_context(nc.Block())
        S5_TABLE_ORDER = [(2 * m + k) * 4 + q for m in range(4) for q in range(4) for k in range(2)]
        TABLES_AT = [0, 4, 4] + [3] * 8
        NB = 16

        def mod_place(m):
            if m < 2 * FFN_MODS:
                return psum[3 + 3 * (m % 2)], psum[2], modacc[:, m % 2, :].rearrange("p (a n) -> p a n", a=2)
            if m < 2 * S5_MODS:
                return psum[6], psum[7], tmp[:, :, T:2 * T]
            return psum[6], psum[7], modacc_s5[:, :].rearrange("p (a n) -> p a n", a=2)

        def mc(l, v, kc=None):
            a = modc[:, l * 6 + v, :]
            return a if kc is None else a[:, kc:kc + 1]

        CONSUMED = {"mod_part": mod_part, "pair_done": pair_done,
                    "pw2_done": pw2_done, "gu_done": gu_done, "down_used": down_used}

        dwr = w_dw[0].rearrange("t (k p) -> (t k) p", p=P)
        row_srcs = {
            "mod_b": mod_b.rearrange("l (k p) -> (l k) p", p=P),
            "dw_lo": dwr[0:P, :], "dw_hi": dwr[P:TAPS * KC, :],
            "c": c.rearrange("a (k p) -> (a k) p", p=P),
            "norm1_g": norm1_g.rearrange("l (k p) -> (l k) p", p=P),
            "norm2_g": norm2_g.rearrange("l (k p) -> (l k) p", p=P),
            "b_pw1": b_pw1.rearrange("a (k p) -> (a k) p", p=P),
            "b_dw": b_dw.rearrange("a (k p) -> (a k) p", p=P),
            "ln_g": ln_g.rearrange("a (k p) -> (a k) p", p=P),
            "ln_b": ln_b.rearrange("a (k p) -> (a k) p", p=P),
            "b_pw2": b_pw2.rearrange("a (k p) -> (a k) p", p=P),
            "ssm_d": ssm_d.rearrange("a (k p) -> (a k) p", p=P),
            "b_glu": b_glu.rearrange("a (k p) -> (a k) p", p=P),
            "a_re": a_re[0].rearrange("(i g) s -> i (g s)", g=2),
            "a_im": a_im[0].rearrange("(i g) s -> i (g s)", g=2),
            "log_dt": log_dt[0].rearrange("(i g) -> i g", g=2),
        }
        ROW_NAMES = sorted(ROWS, key=lambda name: name != "c")

        def load_rows(eng, names):
            for name in names:
                tile, r, k = ROWS[name]
                dst = ldt_rows[r:r + k, 0:2] if name == "log_dt" else rows[r:r + k, tile, :]
                eng.dma_start(dst, row_srcs[name]).then_inc(rows_in, 16)

        @block.sync
        def _(sp):
            sp.dma_start(x_tok[:, 0, :], x[0, 0:P, :]).then_inc(x_in, 16)
            load_rows(sp, ROW_NAMES[1::2])
            for n, (kind, i) in enumerate(STREAM):
                prev = n - EARLY_SLOTS
                if n == WHERE[("pw1", 0)] + 1:
                    for n, w in enumerate((b_re, b_im)):
                        sp.dma_start(braw[n][:, :, :], w[0].rearrange("g s c -> (g s) c").rearrange("(i p) c -> p i c", p=P)).then_inc(s5_in, 16)
                    for n, w in enumerate((c_re, c_im)):
                        sp.dma_start(craw[n][:, :, :], w[0].rearrange("g c s -> (g c) s").rearrange("(k p) s -> p k s", p=P)).then_inc(s5_in, 16)
                if prev >= 0:
                    name, count = consumed(prev)
                    sp.wait_ge(CONSUMED[name], count)
                a = arr[slot_of(n)]
                if kind == "mod":
                    (l, v), h = MOD_ORDER[i // 2], i % 2
                    src = mod_w[l, :, v * D + h * 512:v * D + (h + 1) * 512]
                    sp.dma_start(early(n, KC), src.rearrange("(k p) n -> p k n", p=P)).then_inc(a, 16)
                elif kind in ("pw1", "glu"):
                    w = w_pw1 if kind == "pw1" else w_glu
                    for g in range(2):
                        src = w[0, :, g * D + i * 256:g * D + (i + 1) * 256]
                        sp.dma_start(early(n, KC)[:, :, g * 256:(g + 1) * 256],
                                     src.rearrange("(k p) n -> p k n", p=P)).then_inc(a, 16)
                elif kind == "gu":
                    for g, w in enumerate((w_gate, w_up)):
                        src = w[0, :, i * 256:(i + 1) * 256]
                        sp.dma_start(early(n, KC)[:, :, g * 256:(g + 1) * 256],
                                     src.rearrange("(k p) n -> p k n", p=P)).then_inc(a, 16)
                elif kind == "pw2":
                    src = w_pw2[0, :, i * 512:(i + 1) * 512]
                    sp.dma_start(early(n, KC), src.rearrange("(k p) n -> p k n", p=P)).then_inc(a, 16)
                else:
                    src = w_down[0, i * 256:(i + 1) * 256, :]
                    sp.dma_start(early(n, 4)[:, 0:2, :], src.rearrange("(k p) n -> p k n", p=P)).then_inc(a, 16)

            def half(e, n):
                kind, j, h = HALVES[n]
                s = n % RAW_SLOTS
                e1 = bass.ds(e, 1)
                if kind == "D":
                    src = e_down[0, e1, j * 512 + h * 256:j * 512 + (h + 1) * 256, :]
                    src = src.rearrange("e (k p) n -> p (e k) n", p=P)
                    dst = ring[:, s * HW:(s + 1) * HW].rearrange("p (k n) -> p k n", k=2)
                else:
                    w = e_gate if kind == "G" else e_up
                    src = w[0, e1, h * 512:(h + 1) * 512, j * 512:(j + 1) * 512]
                    src = src.rearrange("e (k p) n -> p (e k) n", p=P)
                    dst = ring[:, s * HW:(s + 1) * HW].rearrange("p (k n) -> p k n", k=4)
                sp.dma_start(dst, src).then_inc(raw_in[s], 16)

            for n in range(NH):
                if n < 2 * EARLY_SLOTS:
                    if n % 2 == 0:
                        m = len(STREAM) - EARLY_SLOTS + n // 2
                        name, count = consumed(m)
                        sp.wait_ge(CONSUMED[name], count)
                elif n >= RAW_SLOTS:
                    sp.wait_ge(lo_ready, n - RAW_SLOTS + 1)
                half(0, n)
            with sp.Fori(1, NE) as e:
                for n in range(NH):
                    sp.wait_ge(lo_ready, e * NH + (n - RAW_SLOTS + 1))
                    half(e, n)
            sp.wait_ge(items_ready, 1)
            total = sp.value_load(count_i[0:1, 0:1], min_val=NE, max_val=MAX_ITEMS)
            sp.wait_ge(over_ready, 1)
            with sp.If(total > NE):
                with sp.Fori(NE, total) as i:
                    e = sp.value_load(over_i[0:1, bass.ds(i - NE, 1)], min_val=0, max_val=NE - 1)
                    for n in range(NH):
                        sp.wait_ge(lo_ready, i * NH + (n - RAW_SLOTS + 1))
                        half(e, n)
            sp.wait_ge(lo_ready, total * NH)
            sp.dma_start(fin_g[:, :], final_g.rearrange("(a n) -> a n", a=1).broadcast_to([P, D])).then_inc(fg_in, 16)
            for tb in range(TB):
                sp.wait_ge(fin_ready, tb + 1)
                sp.dma_start(out[0, tb * P:(tb + 1) * P, :], acc[:, tb, :]).then_inc(out_done, 16)
            sp.wait_ge(out_done, 16 * TB)

        @block.gpsimd
        def _(pool):
            pool.memset(ident[:, :], 0.0).then_inc(pool_own, 1)
            pool.memset(ones[:, :], 1.0).then_inc(consts, 1)
            pool.wait_ge(pool_own, 1)
            pool.affine_select(out=ident[:, :], in_=ident[:, :], compare_op=ALU.not_equal, fill=1.0,
                               base=0, pattern=[[-1, P]], channel_multiplier=1).then_inc(consts, 1)
            pool.iota(iota_t[:, :], pattern=[[1, T]], base=0, channel_multiplier=0,
                      allow_small_or_imprecise_dtypes=True).then_inc(consts, 1)
            pool.memset(upad[:, :, 0:TAPS - 1], 0.0).then_inc(ones_pad, 1)
            for n in range(2):
                pool.memset(bblk[n][:, :, :], 0.0).then_inc(ones_pad, 1)
            pool.iota(iota_e[:, :], pattern=[[1, NE]], base=0, channel_multiplier=0,
                      allow_small_or_imprecise_dtypes=True).then_inc(consts, 1)

            pool.wait_ge(trig_out, 1)
            pool.wait_ge(y_ready, 2 * KC)
            pool.wait_ge(blk_c, 8)
            own = 1
            for n, i in enumerate(S5_TABLE_ORDER):
                pool.tensor_scalar(tabs[:, n, :], iota_t[:, :], sp5[:, 10, i:i + 1], MAGIC,
                                   ALU.mult, ALU.add).then_inc(pool_own, 1)
                own += 1
                pool.wait_ge(pool_own, own)
                pool.tensor_scalar(tabs[:, n, :], tabs[:, n, :], MAGIC, None, ALU.subtract).then_inc(rnd_ready, 1)
                if n >= 2:
                    pool.wait_ge(sin_ready, n - 1)
                    pool.tensor_scalar(tabc[:, n - 2, :], tabc[:, n - 2, :], -2.0, 1.0,
                                       ALU.mult, ALU.add).then_inc(tab_ready, 1)
            for n in (TILES - 2, TILES - 1):
                pool.wait_ge(sin_ready, n + 1)
                pool.tensor_scalar(tabc[:, n, :], tabc[:, n, :], -2.0, 1.0,
                                   ALU.mult, ALU.add).then_inc(tab_ready, 1)
            pool.wait_ge(tab_ready, TILES)
            for b in range(NB):
                pool.wait_ge(scan_ready, b + 1)
                xr, xi = xrot[:, b % 2, 0, :, :], xrot[:, b % 2, 1, :, :]
                tc, ts = tabc[:, 2 * b:2 * b + 2, :], tabs[:, 2 * b:2 * b + 2, :]
                for t, (tab, x_) in enumerate(((tc, xr), (ts, xi), (ts, xr), (tc, xi))):
                    if b:
                        pool.wait_ge(prod_used, 4 * (b - 1) + t + 1)
                    pool.tensor_tensor(prod[:, t, :, :], tab, x_, ALU.mult).then_inc(prod_p, 1)
            pool.iota(iota_s[:, :], pattern=[[1, P]], base=0, channel_multiplier=0,
                      allow_small_or_imprecise_dtypes=True).then_inc(consts, 1)
            pool.memset(tri[:, :], 1.0).then_inc(pool_own, 1)
            pool.wait_ge(pool_own, own + 1)
            pool.affine_select(out=tri[:, :], in_=tri[:, :], compare_op=ALU.is_ge, fill=0.0,
                               base=0, pattern=[[1, P]], channel_multiplier=-1).then_inc(consts, 1)

        @block.scalar
        def _(act):
            load_rows(act, ROW_NAMES[0::2])
            act.dma_start(x_tok[:, 1, :], x[0, P:2 * P, :]).then_inc(x_in, 16)
            for n, k in enumerate(ROW_TILES):
                act.wait_ge(rows_t, 4 if n < 4 else 5)
                act.activation(cols[:, n, 0:k], psum[0 if n < 4 else 1][:, (n % 4) * P:(n % 4) * P + k],
                               ACT.Copy).then_inc(cols_ready, 1)
            act.wait_ge(cols_ready, 4)
            act.activation(cond[:, :, :], colv("c", 0, KC).unsqueeze(2).broadcast_to([P, KC, 32]),
                           ACT.Silu).then_inc(cond_ready, 1)
            for n in range(4):
                act.wait_ge(x_t, n + 1)
                act.activation(hT[:, 2 * n:2 * n + 2, :], psum[4 + n % 2][:, :].rearrange("p (k t) -> p k t", k=2),
                               ACT.Copy).then_inc(h_ready, 1)

            def squares(src, dst, ready, first):
                for kc in range(KC):
                    act.wait_ge(ready, first(kc))
                    act.activation(dst[:, kc, :], src[:, kc, :], ACT.Square).then_inc(sq_ready, 1)

            def root(k):
                act.wait_ge(var_ready, k + 1)
                act.activation(nrm[:, 1, :], nrm[:, 0, :], ACT.Sqrt).then_inc(std_ready, 1)

            def split_hi(u):
                t = WHERE[UNITS[u][:2]]
                act.wait_ge(arr[slot_of(t)], arrived_count(t))
                if u >= 2:
                    name, count = unit_used(u - 2)
                    act.wait_ge(CONSUMED[name], count)
                w, _, hi = unit_views(u)
                act.activation(hi, w, ACT.Copy).then_inc(ehi_ready, 1)

            def y_split_hi(dst, g, ready, count):
                act.wait_ge(ready, count)
                act.activation(dst[:, 4 * g:4 * g + 4, :], yT[:, 4 * g:4 * g + 4, :], ACT.Copy).then_inc(yhi_ready, 1)

            def shifted(k, func, gain, shift, src, split=False):
                for kc in range(KC):
                    act.wait_ge(raw_ready, k * KC + kc + 1)
                    act.activation(yT[:, kc, :], src[:, kc, :], func, scale=gain(kc),
                                   bias=shift(kc)).then_inc(y_ready, 1)
                    if split and kc % 4 == 3:
                        y_split_hi(y_hi, kc // 4, y_ready, k * KC + kc + 1)

            def mod_copy(m):
                act.wait_ge(mod_part, m + 1)
                bank, _, dst = mod_place(m)
                if m >= 2:
                    act.wait_ge(mod_sum, m - 1)
                act.activation(dst, bank[:, :].rearrange("p (a n) -> p a n", a=2), ACT.Copy).then_inc(mod_acc, 1)

            def mod_vector(k):
                act.wait_ge(mod_sum, 2 * k + 2)
                act.activation(modraw[:, k, :], mod_place(2 * k)[1][:, 0:KC], ACT.Copy).then_inc(mod_raw, 1)

            def s5_copies():
                for n in range(8):
                    act.wait_ge(blk_t, n + 1)
                    src = psum[3 + 3 * (n % 2)][:, :].rearrange("p (k s) -> p k s", k=4)
                    dst = (bbT[n // 2] if n < 4 else cT[n // 2 - 2])[:, (n % 2) * 4:(n % 2) * 4 + 4, :]
                    act.activation(dst, src, ACT.Copy).then_inc(blk_c, 1)

            squares(hT, sq, h_ready, lambda kc: kc // 2 + 1)
            root(0)
            act.wait_ge(trig_in, 1)
            act.activation(sp5[:, 11, :], sp5[:, 8, :], ACT.Sin).then_inc(trig, 1)
            act.activation(sp5[:, 12, :], sp5[:, 8, :], ACT.Sin, scale=0.5).then_inc(trig, 1)
            for k in range(CONV_MODS):
                mod_copy(2 * k)
                mod_copy(2 * k + 1)
                mod_vector(k)
            act.wait_ge(modc_ready, 2)
            act.wait_ge(ab_ready, 1)
            shifted(0, ACT.Identity, lambda kc: ab[:, 0, kc:kc + 1], lambda kc: mc(0, SH1, kc), yT)

            def diagonals(n):
                if n >= 2:
                    act.wait_ge(taps_done, n - 1)
                for k in range(PE_TAPS):
                    ins = act.activation(diag[:, n % 2, k, :], ident[:, :], ACT.Copy, scale=dw(k, n))
                ins.then_inc(diag_made, 1)

            def sigmoids(k0, bias):
                if k0 == 0:
                    act.wait_ge(var_ready, 1)
                    diagonals(0)
                for n in range(KC):
                    act.wait_ge(pair_done, k0 + n + 1)
                    if k0 + n >= 2:
                        act.wait_ge(pair_used, k0 + n - 1)
                    act.activation(tmp[:, n % 2, 0:T], psum[4 + n % 2][:, T:2 * T], ACT.Sigmoid,
                                   bias=bias(n)).then_inc(sig_ready, 1)
                    if k0 == 0 and n % 2:
                        m = 2 * CONV_MODS + n // 2
                        mod_copy(m)
                    if k0 == 0 and n + 1 < KC:
                        diagonals(n + 1)
                    if k0 == 0 and n % 4 == 3:
                        mod_vector(m // 2)
                    if k0 and n + 2 < KC:
                        split_hi(UNIT[("glu", 0, 0)] + n + 2)

            sigmoids(0, lambda n: col("b_pw1", KC + n))
            s5_copies()
            split_hi(0)
            split_hi(1)
            squares(conv, sq, cent_ready, lambda kc: kc + 1)
            root(1)
            mod_copy(2 * NORM_MODS)
            mod_copy(2 * NORM_MODS + 1)
            shifted(1, ACT.Silu, lambda kc: col("ln_g", kc), lambda kc: col("ln_b", kc), conv, split=True)
            mod_vector(NORM_MODS)
            act.activation(cond_late[:, :, :], cond[:, :, :], ACT.Copy).then_inc(cond_ready, 1)
            act.wait_ge(ab_ready, 3)
            for n in range(KC):
                act.wait_ge(pw2_done, n + 1)
                if n >= 2:
                    act.wait_ge(h2_ready, n - 1)
                act.activation(tmp[:, n % 2, 0:T], psum[4 + n % 2][:, 0:T], ACT.Identity,
                               scale=mc(0, G1, n), bias=ab[:, 2, n:n + 1]).then_inc(pw2_tmp, 1)
                if n in (1, 3, 5):
                    split_hi(n // 2 + 2)
            squares(hT, conv, h2_ready, lambda kc: kc + 1)
            split_hi(5)
            root(2)
            mod_copy(2 * NORM_MODS + 2)
            mod_copy(2 * NORM_MODS + 3)
            shifted(2, ACT.Identity, lambda kc: ab[:, 1, kc:kc + 1], lambda kc: mc(0, SH2, kc), yT, split=True)
            mod_vector(NORM_MODS + 1)

            def sin_tables(n):
                act.wait_ge(frac_ready, n + 1)
                act.activation(tabs[:, n, :], tabc[:, n, :], ACT.Sin, scale=6.2831840).then_inc(act_own, 1)
                if n >= 2:
                    act.wait_ge(sin_ready, n - 1)
                act.activation(nrm[:, n % 2, :], tabc[:, n, :], ACT.Sin, scale=3.14159265).then_inc(act_own, 1)
                act.wait_ge(act_own, 2 * n + 2)
                act.activation(tabc[:, n, :], nrm[:, n % 2, :], ACT.Square).then_inc(sin_ready, 1)

            made = 0
            for b in range(FBLOCKS):
                for f in (2 * b, 2 * b + 1):
                    act.wait_ge(gu_done, f + 1)
                    if f >= 2:
                        act.wait_ge(hid_ready, f - 1)
                    act.activation(tmp[:, f % 2, 0:T], psum[4 + f % 2][:, 0:T], ACT.Silu).then_inc(gsil, 1)
                    split_hi(UNIT[("gu", b, f % 2)] + 2)
                    act.wait_ge(hid_ready, f + 1)
                    if f >= 4:
                        act.wait_ge(down_used, f - 3)
                    act.activation(hid_hi[:, f % 4, :], hid[:, f % 4, :], ACT.Copy).then_inc(hidhi_ready, 1)
                if b in FFN_MOD_BLOCKS:
                    m = 2 * FFN_MODS + FFN_MOD_BLOCKS.index(b)
                    mod_copy(m)
                for _ in range(TABLES_AT[b]):
                    sin_tables(made)
                    made += 1
                if b in FFN_MOD_BLOCKS and m % 2:
                    mod_vector(m // 2)
                if 0 < b < FBLOCKS - 1:
                    split_hi(UNIT[("down", b - 1, 0)] + 2)
            squares(hT, sq, h3_ready, lambda kc: kc + 1)
            root(3)
            act.wait_ge(ab_ready, 4)
            shifted(3, ACT.Identity, lambda kc: ab[:, 3, kc:kc + 1], lambda kc: mc(1, SH1, kc), yT)
            act.wait_ge(blk_c, 8)
            act.activation(cT_neg[:, :, :], cT[0][:, :, :], ACT.Copy, scale=-1.0).then_inc(cneg_ready, 1)
            kc = 0
            for b in range(NB):
                if b % 2 == 0:
                    mod_copy(2 * S5_MODS + b // 2)
                    if b % 4 == 2:
                        mod_vector(S5_MODS + b // 4)
                for _ in range(2 * (b in (5, 9, 13)) + 2 * (b == NB - 1)):
                    act.wait_ge(ys_pre, kc + 1)
                    act.activation(yT[:, kc, :], yT[:, kc, :], ACT.Gelu_apprx_tanh).then_inc(z_ready, 1)
                    kc += 1
                    if kc % 4 == 0:
                        y_split_hi(z_hi, kc // 4 - 1, z_ready, kc)
                if b == NB - 2:
                    split_hi(UNIT[("glu", 0, 0)])
            assert UNIT[("glu", 0, 1)] % 2 == 0
            split_hi(UNIT[("glu", 0, 1)])
            sigmoids(KC, lambda n: col("b_glu", KC + n))
            act.dma_start(wr[:, :, :], w_router[0].rearrange("(k p) e -> p k e", p=P)).then_inc(wr_in, 16)
            act.dma_start(bcol[:, :], b_router.rearrange("a e -> e a")).then_inc(wr_in, 16)
            squares(hT, sq_late, h4_ready, lambda kc: kc + 1)
            root(4)
            for n in range(2):
                act.wait_ge(g2_done, n + 1)
                act.activation(g2_row[:, n * 512:(n + 1) * 512], psum[4 + n][:, :], ACT.Copy).then_inc(g2row_ready, 1)
            act.wait_ge(ab_ready, 5)
            shifted(4, ACT.Identity, lambda kc: ab[:, 4, kc:kc + 1], lambda kc: mc(1, SH2, kc), yT)
            for n in range(8):
                if n == 4:
                    act.wait_ge(log_done, 1)
                    act.activation(logT[:, :], psum[6][0:NE, 0:T], ACT.Identity, bias=bcol[:, :]).then_inc(logT_ready, 1)
                act.wait_ge(tok_t, n + 1)
                src = psum[n % 4][:, :]
                dst = (acc if n < 4 else y_tok)[:, (n // 2) % 2, (n % 2) * 512:(n % 2) * 512 + 512]
                act.activation(dst, src, ACT.Copy).then_inc(tok_c, 1)
            act.wait_ge(exp2_in, 1)
            act.activation(rt[:, 4, :, 1], rt[:, 4, :, 0], ACT.Exp).then_inc(exp2, 1)
            act.wait_ge(items_ready, 1)
            total = act.value_load(count_i[0:1, 0:1], min_val=NE, max_val=MAX_ITEMS)
            with act.Fori(0, total) as i:
                for n in range(NH):
                    s = n % RAW_SLOTS
                    act.wait_ge(raw_in[s], (i * (NH // RAW_SLOTS) + (n // RAW_SLOTS + 1)) * 16)
                    act.wait_ge(hi_used, i * NH + n + 1)
                    act.activation(whi[:, n % HI_SLOTS, :], ring[:, s * HW:(s + 1) * HW],
                                   ACT.Copy).then_inc(hi_ready, 1)
                    if n >= 3 and HALVES[n - 3][0] == "U" and HALVES[n - 3][2] == 1:
                        j = HALVES[n - 3][1]
                        act.wait_ge(lo_used, i * NH + (AT[("U", j, 1)] + 1 + LO_SLOTS))
                        act.activation(silu_g[:, :], psum[j % 2][:, :], ACT.Silu).then_inc(s_ready, 1)
                    if n - 3 in T_AFTER:
                        j = T_AFTER[n - 3]
                        act.wait_ge(t_done, i * FT + j + 1)
                        act.activation(hh[:, j % 2, :, :], psum[6][:, :].rearrange("p (k s) -> p k s", k=4),
                                       ACT.Copy).then_inc(hh_ready, 1)
                    if n - 3 == SGT_AFTER:
                        act.wait_ge(selg_t, i + 1)
                        act.activation(selgT[:, :], psum[7][:, 0:T], ACT.Copy).then_inc(selgT_ready, 1)
                    g = GATHER_AFTER.get(n - 2)
                    if g is not None:
                        act.wait_ge(gath_done, i * 2 + g + 3)
                        act.activation(xe_hi[:, 4 * g:4 * g + 4, :],
                                       psum[7][:, :].rearrange("p (k s) -> p k s", k=4),
                                       ACT.Copy).then_inc(xh_ready, 1)
            act.wait_ge(fg_in, 16)
            for tb in range(TB):
                act.wait_ge(acc_half, 2 * tb + 2)
                if tb:
                    act.wait_ge(act_own, 2 * TILES + tb)
                act.activation(fin_sq[:, :], acc[:, tb, :], ACT.Square,
                               accum_out=now[:, 4 + tb:5 + tb]).then_inc(act_own, 1)
                act.wait_ge(act_own, 2 * TILES + tb + 1)
            act.wait_ge(fin_var, 1)
            act.activation(now[:, 2:4], now[:, 6:8], ACT.Sqrt).then_inc(fin_std, 1)

        @block.vector
        def _(v):
            links = [0]

            def link(ins):
                links[0] += 1
                ins.then_inc(chain, 1)
                v.wait_ge(chain, links[0])

            v.wait_ge(rows_in, 16 * len(ROWS))
            for g in range(2):
                ins = v.tensor_copy(rows[64:96, 4, g * NS:(g + 1) * NS],
                                    ldt_rows[64:96, g:g + 1].broadcast_to([32, NS]))
            ins.then_inc(rows_ready, 1)
            v.memset(sum_col[:, :], 1.0 / 32).then_inc(sum_col_ready, 1)
            v.wait_ge(consts, 2)
            idv = ident[:, :].rearrange("p (a g c) -> p g a c", g=2, c=GC)
            for g in range(2):
                link(v.tensor_reduce(masks[:, g:g + 1], idv[:, g], axis=AX.XY, op=ALU.add))
            for g in range(2):
                link(v.tensor_scalar(masks[:, 2 + g:3 + g], masks[:, g:g + 1], -1.0, None, ALU.mult))

            def q(n):
                return sp5[:, n, :]

            def exponential(o, src, t):
                xx, k, r = t
                link(v.tensor_scalar(q(xx), src, -87.0, 88.7, ALU.max, ALU.min))
                link(v.tensor_scalar(q(k), q(xx), LOG2E, MAGIC, ALU.mult, ALU.add))
                link(v.tensor_scalar(q(k), q(k), MAGIC, None, ALU.subtract))
                link(v.scalar_tensor_tensor(q(r), q(k), -LN2_HI, q(xx), ALU.mult, ALU.add))
                link(v.scalar_tensor_tensor(q(r), q(k), -LN2_LO, q(r), ALU.mult, ALU.add))
                link(v.tensor_scalar(q(xx), q(r), EXP_COEF[0], None, ALU.mult))
                for cf in EXP_COEF[1:]:
                    link(v.scalar_tensor_tensor(q(xx), q(xx), cf, q(r), ALU.add, ALU.mult))
                link(v.tensor_scalar(sp5i[:, :], q(k), 127.0, 2.0 ** 23, ALU.add, ALU.mult))
                link(v.scalar_tensor_tensor(q(o), q(xx), 1.0, sp5i[:, :].bitcast(F32), ALU.add, ALU.mult))

            v.wait_ge(cols_ready, 5)
            are, aim, ldt = (cols[:, 4, 32 * n:32 * n + 32] for n in range(3))
            exponential(3, ldt, (0, 1, 2))
            link(v.tensor_tensor(q(4), q(3), are, ALU.mult))
            exponential(5, q(4), (0, 1, 2))
            link(v.tensor_tensor(q(6), q(3), aim, ALU.mult))
            link(v.tensor_scalar(q(7), q(6), 1.0 / (2 * np.pi), MAGIC, ALU.mult, ALU.add))
            link(v.tensor_scalar(q(7), q(7), MAGIC, None, ALU.subtract))
            link(v.scalar_tensor_tensor(q(8), q(7), -TWO_PI[0], q(6), ALU.mult, ALU.add))
            link(v.scalar_tensor_tensor(q(8), q(7), -TWO_PI[1], q(8), ALU.mult, ALU.add))
            link(v.scalar_tensor_tensor(q(8), q(7), -TWO_PI[2], q(8), ALU.mult, ALU.add))
            link(v.tensor_scalar(q(8), q(8), -3.1415925, 3.1415925, ALU.max, ALU.min))
            v.tensor_scalar(q(10), q(8), 1.0 / (2 * np.pi), None, ALU.mult).then_inc(trig_in, 1)
            v.wait_ge(trig_in, 1)
            link(v.tensor_scalar(q(13), q(10), 384.0, None, ALU.add))
            link(v.tensor_scalar(q(13), q(13), 384.0, None, ALU.subtract))
            v.tensor_tensor(q(14), q(10), q(13), ALU.subtract).then_inc(trig_out, 1)

            def variance(k):
                v.wait_ge(sum_ready, k + 1)
                v.tensor_scalar(nrm[:, 0, :], psum[7][:, 0:T], 1.0 / D, EPS, ALU.mult, ALU.add).then_inc(var_ready, 1)

            def rsqrt(k):
                v.wait_ge(std_ready, k + 1)
                link(v.reciprocal(nrm[:, 2, :], nrm[:, 1, :]))
                link(v.tensor_tensor(nrm[:, 1, :], nrm[:, 0, :], nrm[:, 2, :], ALU.mult))
                link(v.scalar_tensor_tensor(nrm[:, 1, :], nrm[:, 1, :], -0.5, nrm[:, 2, :], ALU.mult, ALU.mult))
                link(v.scalar_tensor_tensor(nrm[:, 1, :], nrm[:, 1, :], 1.5, nrm[:, 2, :], ALU.add, ALU.mult))

            def split_lo(u):
                v.wait_ge(ehi_ready, u + 1)
                w, lo, hi = unit_views(u)
                v.tensor_tensor(lo, w, hi.bitcast(F32), ALU.subtract).then_inc(elo_ready, 1)

            def y_split_lo(high, k):
                v.wait_ge(yhi_ready, k + 1)
                g = slice(4 * (k % 2), 4 * (k % 2) + 4)
                v.tensor_tensor(y_lo[:, g, :], yT[:, g, :], high[:, g, :].bitcast(F32), ALU.subtract).then_inc(ylo_ready, 1)

            def scaled(dst, src):
                for kc in range(KC):
                    v.tensor_tensor(dst[:, kc, :], src[:, kc, :], nrm[:, 1, :], ALU.mult).then_inc(raw_ready, 1)

            def mod_bias(k):
                l, m = MOD_ORDER[k]
                v.wait_ge(mod_raw, k + 1)
                v.tensor_tensor(mc(l, m), modraw[:, k, :], colv("mod_b", (l * 6 + m) * KC, KC),
                                ALU.add).then_inc(modc_ready, 1)
                v.wait_ge(modc_ready, k + 1)

            def gain_cols(o, l, m, name):
                v.scalar_tensor_tensor(ab[:, o, :], mc(l, m), 1.0, colv(name, l * KC, KC),
                                       ALU.add, ALU.mult).then_inc(ab_ready, 1)

            variance(0)
            rsqrt(0)
            scaled(yT, hT)
            v.wait_ge(trig, 2)
            link(v.tensor_tensor(q(15), q(12), q(12), ALU.mult))
            link(v.tensor_scalar(q(15), q(15), -2.0, 1.0, ALU.mult, ALU.add))
            link(v.tensor_tensor(q(15), q(15), q(5), ALU.mult))
            link(v.tensor_scalar(q(15), q(15), -1.0, None, ALU.add))
            link(v.tensor_tensor(q(16), q(11), q(5), ALU.mult))
            link(v.tensor_tensor(q(0), are, are, ALU.mult))
            link(v.tensor_tensor(q(1), aim, aim, ALU.mult))
            link(v.tensor_tensor(q(0), q(0), q(1), ALU.add))
            link(v.reciprocal(q(0), q(0)))
            link(v.tensor_tensor(q(1), q(15), are, ALU.mult))
            link(v.tensor_tensor(q(2), q(16), aim, ALU.mult))
            link(v.tensor_tensor(q(1), q(1), q(2), ALU.add))
            link(v.tensor_tensor(q(17), q(1), q(0), ALU.mult))
            link(v.tensor_tensor(q(1), q(16), are, ALU.mult))
            link(v.tensor_tensor(q(2), q(15), aim, ALU.mult))
            link(v.tensor_tensor(q(1), q(1), q(2), ALU.subtract))
            link(v.tensor_tensor(q(18), q(1), q(0), ALU.mult))
            mod_bias(0)
            gain_cols(0, 0, SC1, "norm1_g")
            mod_bias(1)
            v.wait_ge(s5_in, 64)
            fr, fi = (q(n).unsqueeze(2).broadcast_to([P, TILES, GC]) for n in (17, 18))
            for t, (f, w) in enumerate(((fr, 0), (fi, 1), (fr, 1), (fi, 0))):
                link(v.tensor_tensor(btmp[t][:, :, :], f, braw[w][:, :, :], ALU.mult))
            v.wait_ge(ones_pad, 3)
            for g in range(2):
                pr, cr = slice(64 * g, 64 * g + 64), slice(GC * g, GC * g + GC)
                v.tensor_tensor(bblk[0][pr, :, cr], btmp[0][pr, :, :], btmp[1][pr, :, :], ALU.subtract).then_inc(blk_ready, 1)
                v.tensor_tensor(bblk[1][pr, :, cr], btmp[2][pr, :, :], btmp[3][pr, :, :], ALU.add).then_inc(blk_ready, 1)
            for n in range(2):
                for g in range(2):
                    v.tensor_scalar(cblk[n][:, :, g * NS:(g + 1) * NS], craw[n][:, :, :],
                                    masks[:, 2 * n + g:2 * n + g + 1], None, ALU.mult).then_inc(blk_ready, 1)
            DVE_STEPS = TAPS - PE_TAPS + 1
            v.wait_ge(ones_pad, 1)
            v.wait_ge(x_t, 4)
            for n in range(KC):
                v.wait_ge(sig_ready, n + 1)
                v.scalar_tensor_tensor(upad[:, n, TAPS - 1:PAD], psum[4 + n % 2][:, 0:T], col("b_pw1", n),
                                       tmp[:, n % 2, 0:T], ALU.add, ALU.mult).then_inc(pair_used, 1)
                v.wait_ge(pair_used, n + 1)
                even, odd = conv[:, n, :], tmp[:, n % 2, T:2 * T]
                for k in range(PE_TAPS, TAPS):
                    o = odd if (k - PE_TAPS) % 2 else even
                    u = upad[:, n, k:k + T]
                    if k == PE_TAPS:
                        ins = v.tensor_scalar(o, u, dw(k, n), col("b_dw", n), ALU.mult, ALU.add)
                    elif k == PE_TAPS + 1:
                        ins = v.tensor_scalar(o, u, dw(k, n), None, ALU.mult)
                    else:
                        v.wait_ge(tap, n * DVE_STEPS + k - PE_TAPS - 1)
                        ins = v.scalar_tensor_tensor(o, u, dw(k, n), o, ALU.mult, ALU.add)
                    ins.then_inc(tap, 1)
                v.wait_ge(taps_done, n + 1)
                v.wait_ge(tap, (n + 1) * DVE_STEPS - 2)
                v.tensor_tensor(even, even, psum[n % 2][:, 0:T], ALU.add).then_inc(tap, 1)
                v.wait_ge(tap, (n + 1) * DVE_STEPS)
                v.tensor_tensor(even, even, odd, ALU.add).then_inc(conv_ready, 1)
            v.wait_ge(mean_sum, 1)
            link(v.tensor_scalar(nrm[:, 2, :], psum[7][:, 0:T], 1.0 / D, None, ALU.mult))
            for kc in range(KC):
                v.tensor_tensor(conv[:, kc, :], conv[:, kc, :], nrm[:, 2, :], ALU.subtract).then_inc(cent_ready, 1)
            split_lo(0)
            split_lo(1)
            variance(1)
            rsqrt(1)
            scaled(conv, conv)
            for g in range(2):
                y_split_lo(y_hi, g)
            for k in range(CONV_MODS, NORM_MODS + 1):
                mod_bias(k)
            gain_cols(1, 0, SC2, "norm2_g")
            v.tensor_tensor(ab[:, 2, :], mc(0, G1), colv("b_pw2", 0, KC), ALU.mult).then_inc(ab_ready, 1)
            for n in range(KC):
                v.wait_ge(pw2_tmp, n + 1)
                v.tensor_tensor(hT[:, n, :], hT[:, n, :], tmp[:, n % 2, 0:T], ALU.add).then_inc(h2_ready, 1)
                if n in (1, 3, 5):
                    split_lo(n // 2 + 2)
            variance(2)
            rsqrt(2)
            scaled(yT, hT)
            for g in range(2):
                y_split_lo(y_hi, 2 + g)
            split_lo(5)
            mod_bias(NORM_MODS + 1)

            made = 0
            for b in range(FBLOCKS):
                for f in (2 * b, 2 * b + 1):
                    v.wait_ge(gsil, f + 1)
                    if f >= 4:
                        v.wait_ge(down_used, f - 3)
                    v.tensor_tensor(hid[:, f % 4, :], psum[4 + f % 2][:, T:2 * T], tmp[:, f % 2, 0:T],
                                    ALU.mult).then_inc(hid_ready, 1)
                    split_lo(UNIT[("gu", b, f % 2)] + 2)
                    v.wait_ge(hidhi_ready, f + 1)
                    v.tensor_tensor(hid_lo[:, f % 4, :], hid[:, f % 4, :], hid_hi[:, f % 4, :].bitcast(F32),
                                    ALU.subtract).then_inc(hidlo_ready, 1)
                for _ in range(TABLES_AT[b]):
                    i = S5_TABLE_ORDER[made]
                    v.wait_ge(rnd_ready, made + 1)
                    link(v.scalar_tensor_tensor(tabc[:, made, :], iota_t[:, :], sp5[:, 13, i:i + 1],
                                                tabs[:, made, :], ALU.mult, ALU.subtract))
                    link(v.scalar_tensor_tensor(tabc[:, made, :], iota_t[:, :], sp5[:, 14, i:i + 1],
                                                tabc[:, made, :], ALU.mult, ALU.add))
                    v.tensor_scalar(tabc[:, made, :], tabc[:, made, :], -0.5, 0.5, ALU.max, ALU.min).then_inc(frac_ready, 1)
                    made += 1
                if 0 < b < FBLOCKS - 1:
                    split_lo(UNIT[("down", b - 1, 0)] + 2)
            for k in range(FFN_MODS, S5_MODS):
                mod_bias(k)
            gain_cols(3, 1, SC1, "norm1_g")
            v.wait_ge(down_used, 2 * FBLOCKS)
            for n in range(KC):
                v.scalar_tensor_tensor(hT[:, n, :], psum[n // 2][:, (n % 2) * T:(n % 2) * T + T], mc(0, G2, n),
                                       hT[:, n, :], ALU.mult, ALU.add).then_inc(h3_ready, 1)
            variance(3)
            rsqrt(3)
            scaled(yT, hT)

            v.wait_ge(tab_ready, TILES)
            ta, tb_ = tmp[:, 0, :], tmp[:, 1, :]
            for b in range(NB):
                m, qq = b // 4, b % 4
                ur, ui = psum[(b % 2) * 2][:, :], psum[(b % 2) * 2 + 1][:, :]
                tc = tabc[:, 2 * b:2 * b + 2, :].rearrange("p a t -> p (a t)")
                ts = tabs[:, 2 * b:2 * b + 2, :].rearrange("p a t -> p (a t)")
                xr = xrot[:, b % 2, 0, :, :].rearrange("p a t -> p (a t)")
                xi = xrot[:, b % 2, 1, :, :].rearrange("p a t -> p (a t)")
                v.wait_ge(bu_done, b + 1)
                if b >= 2:
                    v.wait_ge(prod_p, 4 * (b - 1))
                link(v.tensor_tensor(ta, ur, tc, ALU.mult))
                link(v.tensor_tensor(tb_, ui, ts, ALU.mult))
                link(v.tensor_tensor(xr, ta, tb_, ALU.add))
                link(v.tensor_tensor(ta, ui, tc, ALU.mult))
                v.tensor_tensor(tb_, ur, ts, ALU.mult).then_inc(bu_used, 1)
                v.wait_ge(bu_used, b + 1)
                link(v.tensor_tensor(xi, ta, tb_, ALU.subtract))
                for k in range(2):
                    i = (2 * m + k) * 4 + qq
                    mag = sp5[:, 5, i:i + 1].broadcast_to([P, T])
                    for c2 in range(2):
                        s = xrot[:, b % 2, c2, k, :]
                        ins = v.tensor_tensor_scan(s, mag, s, 0.0, ALU.mult, ALU.add)
                        if k == 0 or c2 == 0:
                            link(ins)
                ins.then_inc(scan_ready, 1)
                if b % 4 == 1 and b > 1:
                    mm = b // 4 - 1
                    v.wait_ge(prod_used, 16 * (mm + 1))
                    for k in range(2):
                        kc = 2 * mm + k
                        v.scalar_tensor_tensor(yT[:, kc, :], yT[:, kc, :], col("ssm_d", kc),
                                               psum[4 + mm % 2][:, k * T:(k + 1) * T], ALU.mult, ALU.add).then_inc(ys_pre, 1)
            y_split_lo(z_hi, 4)
            split_lo(UNIT[("glu", 0, 0)])
            for k in range(S5_MODS, len(MOD_ORDER)):
                mod_bias(k)
            gain_cols(4, 1, SC2, "norm2_g")
            v.wait_ge(prod_used, 4 * NB)
            for k in range(2):
                kc = 6 + k
                v.scalar_tensor_tensor(yT[:, kc, :], yT[:, kc, :], col("ssm_d", kc),
                                       psum[5][:, k * T:(k + 1) * T], ALU.mult, ALU.add).then_inc(ys_pre, 1)
            y_split_lo(z_hi, 5)
            split_lo(UNIT[("glu", 0, 1)])
            for n in range(KC):
                v.wait_ge(sig_ready, KC + n + 1)
                v.scalar_tensor_tensor(tmp[:, n % 2, T:2 * T], psum[4 + n % 2][:, 0:T], col("b_glu", n),
                                       tmp[:, n % 2, 0:T], ALU.add, ALU.mult).then_inc(pair_used, 1)
                v.wait_ge(pair_used, KC + n + 1)
                v.scalar_tensor_tensor(hT[:, n, :], tmp[:, n % 2, T:2 * T], mc(1, G1, n), hT[:, n, :],
                                       ALU.mult, ALU.add).then_inc(h4_ready, 1)
                if n + 2 < KC:
                    split_lo(UNIT[("glu", 0, 0)] + n + 2)
            v.wait_ge(h4_ready, KC)
            for kc in range(KC):
                v.tensor_scalar(tmp[:, kc // 4, (kc % 4) * P:(kc % 4) * P + P], ident[:, :], mc(1, G2, kc), None, ALU.mult).then_inc(diag_ready, 1)
            v.memset(zeros[:, :], 0.0).then_inc(selgT_zero, 1)
            variance(4)
            rsqrt(4)
            scaled(yT, hT)
            v.wait_ge(raw_ready, 5 * KC)
            v.memset(selgT[:, :], 0.0).then_inc(selgT_zero, 1)

            def r(n):
                return rt[:, n, :, :]

            def rb(n, c0):
                return rt[:, n, :, c0:c0 + 1].broadcast_to([P, TB, NE])

            v.wait_ge(logit_t, 1)
            for tb in range(TB):
                link(v.tensor_copy(logit[:, tb, :], psum[7][:, tb * P:tb * P + NE]))
            ie = iota_e[:, :].unsqueeze(1).broadcast_to([P, TB, NE])
            for k in range(2):
                src = logit[:, :, :] if k == 0 else r(3)
                link(v.tensor_reduce(rt[:, 5 + k, :, 0:1], src, axis=AX.X, op=ALU.max))
                link(v.tensor_tensor(r(7), src, rb(5 + k, 0), ALU.is_equal))
                link(v.tensor_scalar(r(8), ie, -1.0, float(NE), ALU.mult, ALU.add))
                link(v.tensor_tensor(r(7), r(7), r(8), ALU.mult))
                link(v.tensor_reduce(rt[:, 9, :, 0:1], r(7), axis=AX.X, op=ALU.max))
                link(v.tensor_tensor(r(k), r(8), rb(9, 0), ALU.is_equal))
                if k == 0:
                    link(v.tensor_scalar(r(3), r(0), -3.0e38, None, ALU.mult))
                    link(v.tensor_tensor(r(3), r(3), logit[:, :, :], ALU.add))
            v.tensor_tensor(r(2), r(0), r(1), ALU.add).then_inc(mask_ready, 1)
            v.tensor_tensor(rt[:, 4, :, 0], rt[:, 6, :, 0], rt[:, 5, :, 0], ALU.subtract).then_inc(exp2_in, 1)
            v.wait_ge(exp2, 1)
            link(v.tensor_scalar(rt[:, 4, :, 2], rt[:, 4, :, 1], 1.0, None, ALU.add))
            link(v.reciprocal(rt[:, 4, :, 3], rt[:, 4, :, 2]))
            link(v.tensor_tensor(rt[:, 4, :, 4], rt[:, 4, :, 3], rt[:, 4, :, 1], ALU.mult))
            link(v.tensor_tensor(r(0), r(0), rb(4, 3), ALU.mult))
            link(v.tensor_tensor(r(1), r(1), rb(4, 4), ALU.mult))
            link(v.tensor_tensor(r(10), r(0), r(1), ALU.add))
            v.wait_ge(rank_done, 1)
            for tb in range(TB):
                link(v.tensor_scalar(rt[:, 11, tb, :], psum[6][:, 128 + 64 * tb:128 + 64 * tb + NE], 999.0, None, ALU.add))
            link(v.tensor_tensor(r(11), r(11), r(2), ALU.mult))
            link(v.tensor_scalar(r(11), r(11), -1000.0, None, ALU.add))
            link(v.tensor_scalar(rt[:, 0, 0, :], psum[6][:, 256:256 + NE], float(P), None, ALU.is_gt))
            link(v.memset(rt[:, 0, 1, :], 1.0))
            link(v.tensor_tensor_scan(rt[:, 1, 0, :], rt[:, 0, 1, :], rt[:, 0, 0, :], 0.0, ALU.mult, ALU.add))
            link(v.memset(items[:, :, :], -1000.0))
            iv = items[:, 0:NE, :].rearrange("p e k -> p k e")
            link(v.tensor_copy(iv[:, 0:2, :], r(11)))
            link(v.tensor_copy(iv[:, 2:4, :], r(10)))
            v.tensor_scalar(count_i[:, :], rt[:, 1, 0, NE - 1:NE], float(NE), None, ALU.add).then_inc(items_ready, 1)

            def overflow_items():
                for k in range(MAX_ITEMS - NE):
                    link(v.scalar_tensor_tensor(rt[:, 3, 0, :], rt[:, 1, 0, :], float(k + 1), rt[:, 0, 0, :], ALU.is_equal, ALU.mult))
                    link(v.tensor_tensor(rt[:, 3, 1, :], rt[:, 3, 0, :], iota_e[:, :], ALU.mult))
                    link(v.tensor_reduce(rt[:, 5, 0, k:k + 1], rt[:, 3, 1, :], axis=AX.X, op=ALU.add))
                    hot = rt[:, 3, 0:1, :].broadcast_to([P, TB, NE])
                    link(v.tensor_scalar(r(7), r(11), -float(P), None, ALU.add))
                    link(v.tensor_tensor(r(7), r(7), hot, ALU.mult))
                    link(v.tensor_reduce(items[:, NE + k, 0:2].unsqueeze(2), r(7), axis=AX.X, op=ALU.add))
                    link(v.tensor_tensor(r(7), r(10), hot, ALU.mult))
                    link(v.tensor_reduce(items[:, NE + k, 2:4].unsqueeze(2), r(7), axis=AX.X, op=ALU.add))
                v.tensor_copy(over_i[:, 0:3], rt[:, 5, 0, 0:3]).then_inc(over_ready, 1)

            v.wait_ge(items_ready, 1)
            v.wait_ge(consts, 6)
            for tb in range(TB):
                v.tensor_scalar(sel[:, tb, :], iota_s[:, :], items[:, 0, tb:tb + 1], None, ALU.is_equal).then_inc(sel_ready, 1)
            overflow_items()
            for g in range(2):
                bank = psum[7 - g]
                v.wait_ge(gath_done, g + 1)
                v.tensor_copy(xe_hi[:, 4 * g:4 * g + 4, :], bank[:, :].rearrange("p (k s) -> p k s", k=4)).then_inc(xh_ready, 1)
                v.wait_ge(xh_ready, g + 1)
                v.tensor_tensor(xe_lo[:, 4 * g:4 * g + 4, :].rearrange("p k s -> p (k s)"), bank[:, :],
                                xe_hi[:, 4 * g:4 * g + 4, :].rearrange("p k s -> p (k s)").bitcast(F32),
                                ALU.subtract).then_inc(xl_ready, 1)
            v.wait_ge(g2row_ready, 2)

            def evac_y(i):
                v.wait_ge(lo_used, i * NH + LO_SLOTS)
                for h in range(2):
                    v.tensor_tensor(y_exp[:, h * 512:(h + 1) * 512], psum[4 + h][:, :],
                                    g2_row[:, h * 512:(h + 1) * 512], ALU.mult).then_inc(yx_ready, 1)

            def combined(i, m):
                tb, h = m // 2, m % 2
                v.wait_ge(comb_done, i * NCOMB + m + 1)
                v.tensor_tensor(acc[:, tb, h * 512:(h + 1) * 512], acc[:, tb, h * 512:(h + 1) * 512],
                                psum[7][:, :], ALU.add).then_inc(comb_used, 1)

            total = v.value_load(count_i[0:1, 0:1], min_val=NE, max_val=MAX_ITEMS)
            with v.Fori(0, total) as i:
                for n in range(NH):
                    s = n % RAW_SLOTS
                    v.wait_ge(hi_ready, i * NH + n + 1)
                    v.wait_ge(lo_used, i * NH + n + 1)
                    v.tensor_tensor(wlo[:, n % LO_SLOTS, :], ring[:, s * HW:(s + 1) * HW],
                                    whi[:, n % HI_SLOTS, :].bitcast(F32), ALU.subtract).then_inc(lo_ready, 1)
                    if n == 1:
                        evac_y(i)
                    if n >= 2 and n - 2 in COMB_AFTER:
                        combined(i, COMB_AFTER[n - 2])
                    if n >= 3 and HALVES[n - 3][0] == "U" and HALVES[n - 3][2] == 1:
                        j = HALVES[n - 3][1]
                        v.wait_ge(s_ready, i * FT + j + 1)
                        v.tensor_tensor(hid_e[:, :], silu_g[:, :], psum[2 + j % 2][:, :], ALU.mult).then_inc(he_ready, 1)
                    if n - 3 in T_AFTER:
                        j = T_AFTER[n - 3]
                        v.wait_ge(hh_ready, i * FT + j + 1)
                        v.tensor_tensor(hl[:, j % 2, :, :].rearrange("p k s -> p (k s)"), psum[6][:, :],
                                        hh[:, j % 2, :, :].rearrange("p k s -> p (k s)").bitcast(F32),
                                        ALU.subtract).then_inc(hl_ready, 1)
                    if n == AT[("G", 3, 0)]:
                        v.tensor_copy(now[:, 0:4], items[:, bass.ds(i, 1), :].rearrange("p a k -> p (a k)")).then_inc(now_ready, 1)
                        v.tensor_copy(now[:, 4:8], items[:, bass.ds(i + 1, 1), :].rearrange("p a k -> p (a k)")).then_inc(now_ready, 1)
                        v.wait_ge(now_ready, i * 2 + 2)
                        for tb in range(TB):
                            v.tensor_scalar(selg[:, tb, :], sel[:, tb, :], now[:, 2 + tb:3 + tb], None, ALU.mult).then_inc(selg_ready, 1)
                    if n == AT[("G", 4, 0)]:
                        v.wait_ge(selg_ready, i * TB + TB)
                        for tb in range(TB):
                            v.tensor_scalar(sel[:, tb, :], iota_s[:, :], now[:, 4 + tb:5 + tb], None, ALU.is_equal).then_inc(sel_ready, 1)
                    g = GATHER_AFTER.get(n - 2)
                    if g is not None:
                        v.wait_ge(xh_ready, i * 2 + g + 3)
                        v.tensor_tensor(xe_lo[:, 4 * g:4 * g + 4, :].rearrange("p k s -> p (k s)"), psum[7][:, :],
                                        xe_hi[:, 4 * g:4 * g + 4, :].rearrange("p k s -> p (k s)").bitcast(F32),
                                        ALU.subtract).then_inc(xl_ready, 1)
            evac_y(total)
            for m in range(NCOMB):
                tb, h = m // 2, m % 2
                v.wait_ge(comb_done, total * NCOMB + m + 1)
                ins = v.tensor_tensor(acc[:, tb, h * 512:(h + 1) * 512], acc[:, tb, h * 512:(h + 1) * 512],
                                      psum[m][:, :], ALU.add)
                ins.then_inc(acc_half, 1)
            v.wait_ge(act_own, 2 * TILES + TB)
            v.tensor_scalar(now[:, 6:8], now[:, 4:6], 1.0 / D, EPS, ALU.mult, ALU.add).then_inc(fin_var, 1)
            v.wait_ge(fin_std, 1)
            v.wait_ge(fin_var, 1)
            link(v.reciprocal(now[:, 0:2], now[:, 2:4]))
            link(v.tensor_tensor(now[:, 2:4], now[:, 6:8], now[:, 0:2], ALU.mult))
            link(v.scalar_tensor_tensor(now[:, 2:4], now[:, 2:4], -0.5, now[:, 0:2], ALU.mult, ALU.mult))
            link(v.scalar_tensor_tensor(now[:, 2:4], now[:, 2:4], 1.5, now[:, 0:2], ALU.add, ALU.mult))
            v.wait_ge(fg_in, 16)
            for tb in range(TB):
                v.scalar_tensor_tensor(acc[:, tb, :], acc[:, tb, :], now[:, 2 + tb:3 + tb], fin_g[:, :],
                                       ALU.mult, ALU.mult).then_inc(fin_ready, 1)

        @block.tensor
        def _(pe):
            mm = nc.tensor.matmul
            pe.wait_ge(consts, 2)
            pe.wait_ge(rows_ready, 1)
            for n, k in enumerate(ROW_TILES):
                nc.tensor.transpose(psum[0 if n < 4 else 1][:, (n % 4) * P:(n % 4) * P + k], rows[0:k, n, :],
                                    ident[0:k, 0:k]).then_inc(rows_t, 1)
            pe.wait_ge(x_in, 32)
            for n in range(4):
                if n >= 2:
                    pe.wait_ge(h_ready, n - 1)
                for k in range(2):
                    for tb in range(TB):
                        kc = 2 * n + k
                        ins = nc.tensor.transpose(psum[4 + n % 2][:, k * T + tb * P:k * T + (tb + 1) * P],
                                                  x_tok[:, tb, kc * P:(kc + 1) * P], ident[:, :])
                ins.then_inc(x_t, 1)

            def sums(base, ready, src, done):
                for kc in range(KC):
                    pe.wait_ge(ready, base + kc + 1)
                    ins = mm(psum[7][:, 0:T], ones[:, :], src[:, kc, :], start=kc == 0, stop=kc == KC - 1)
                ins.then_inc(done, 1)

            def split_product(out, u, high, k):
                _, lo, hi = unit_views(u)
                for p in range(3):
                    if p == 2:
                        pe.wait_ge(elo_ready, u + 1)
                    for kc in range(KC):
                        ins = mm(out, (lo if p == 2 else hi)[:, kc, k, :], (y_lo if p == 1 else high)[:, kc, :],
                                 start=p == 0 and kc == 0, stop=p == 2 and kc == KC - 1)
                return ins

            def split_pairs():
                for n in range(KC):
                    u = UNIT[("glu", n // 2, n % 2)]
                    pe.wait_ge(ehi_ready, u + 1)
                    pe.wait_ge(pair_used, KC + n - 1)
                    if n == 0:
                        pe.wait_ge(ylo_ready, 6)
                    for g in range(2):
                        ins = split_product(psum[4 + n % 2][:, g * T:(g + 1) * T], u, z_hi, g)
                    ins.then_inc(pair_done, 1)

            def s5_transposes():
                pe.wait_ge(mod_acc, 2 * NORM_MODS)
                pe.wait_ge(blk_ready, 8)
                for n in range(8):
                    if n >= 2:
                        pe.wait_ge(blk_c, n - 1)
                    src = bblk[n // 2] if n < 4 else cblk[n // 2 - 2]
                    for k in range(4):
                        kc = (n % 2) * 4 + k
                        a = src[:, 4 * kc:4 * kc + 4, :].rearrange("p i c -> p (i c)") if n < 4 else src[:, kc, :]
                        ins = nc.tensor.transpose(psum[3 + 3 * (n % 2)][:, k * P:(k + 1) * P], a, ident[:, :])
                    ins.then_inc(blk_t, 1)

            def pairs():
                for n in range(KC):
                    t = WHERE[("pw1", n // 2)]
                    if n % 2 == 0:
                        pe.wait_ge(arr[slot_of(t)], arrived_count(t))
                    w = early(t, KC)
                    if n >= 2:
                        pe.wait_ge(pair_used, n - 1)
                    for g in range(2):
                        for kc in range(KC):
                            if n == 0:
                                pe.wait_ge(y_ready, kc + 1)
                            o = g * 256 + (n % 2) * P
                            ins = mm(psum[4 + n % 2][:, g * T:(g + 1) * T], w[:, kc, o:o + P], yT[:, kc, :],
                                     start=kc == 0, stop=kc == KC - 1)
                    ins.then_inc(pair_done, 1)
                    m = 2 * CONV_MODS + n // 2
                    if n % 2:
                        mod_partial(m)
                    if n:
                        taps(n - 1)
                    if n % 2:
                        mod_sums(m)
                s5_transposes()
                taps(KC - 1)

            def taps(n):
                pe.wait_ge(diag_made, n + 1)
                pe.wait_ge(pair_used, n + 1)
                if n < 2:
                    pe.wait_ge(cols_ready, 5)
                else:
                    pe.wait_ge(conv_ready, n - 1)
                for k in range(PE_TAPS):
                    ins = mm(psum[n % 2][:, 0:T], diag[:, n % 2, k, :], upad[:, n, k:k + T],
                             start=k == 0, stop=k == PE_TAPS - 1)
                ins.then_inc(taps_done, 1)

            def mod_partial(m):
                n = WHERE[("mod", m)]
                bank = mod_place(m)[0]
                pe.wait_ge(arr[slot_of(n)], arrived_count(n))
                if m >= 2:
                    pe.wait_ge(mod_acc, m - 1 if 2 <= m < 2 * FFN_MODS else m)
                w, cc = early(n, KC), cond if m < 2 * FFN_MODS else cond_late
                for first in (True, False):
                    for j in range(4):
                        kc = 2 * j + (not first)
                        ins = mm(bank[32 * j:32 * j + 32, :], cc[:, kc, :], w[:, kc, :],
                                 start=first, stop=not first)
                ins.then_inc(mod_part, 1)

            def mod_sums(m):
                _, bank, part = mod_place(m)
                k, h = m // 2, m % 2
                if k and h == 0:
                    pe.wait_ge(mod_raw, k)
                pe.wait_ge(mod_acc, m + 1)
                for o in range(4):
                    ins = mm(bank[:, 4 * h + o:4 * h + o + 1], part[:, o // 2, (o % 2) * P:(o % 2) * P + P],
                             sum_col[:, :], start=True, stop=True)
                ins.then_inc(mod_sum, 1)

            def mod_tiles(first, last):
                mod_partial(first)
                for m in range(first, last):
                    if m + 1 < last:
                        mod_partial(m + 1)
                    mod_sums(m)

            sums(0, sq_ready, sq, sum_ready)
            pe.wait_ge(cond_ready, 1)
            pe.wait_ge(sum_col_ready, 1)
            mod_tiles(0, 2 * CONV_MODS)
            pe.wait_ge(h_ready, 4)
            pairs()
            sums(0, conv_ready, conv, mean_sum)
            pe.wait_ge(cent_ready, 1)
            sums(KC, sq_ready, sq, sum_ready)
            pe.wait_ge(blk_c, 8)
            mod_tiles(2 * NORM_MODS, 2 * NORM_MODS + 2)
            for n in range(KC):
                u = UNIT[("pw2", n // 4, n // 2 % 2)]
                pe.wait_ge(ehi_ready, u + 1)
                if n >= 2:
                    pe.wait_ge(pw2_tmp, n - 1)
                if n == 0:
                    pe.wait_ge(ylo_ready, 2)
                ins = split_product(psum[4 + n % 2][:, 0:T], u, y_hi, n % 2)
                ins.then_inc(pw2_done, 1)
            sums(2 * KC, sq_ready, conv, sum_ready)
            mod_tiles(2 * NORM_MODS + 2, 2 * FFN_MODS)

            def down(b):
                u = UNIT[("down", b, 0)]
                _, lo, hi = unit_views(u)
                pe.wait_ge(elo_ready, u + 1)
                for k in range(2):
                    f = 2 * b + k
                    if f == 0:
                        pe.wait_ge(mod_raw, FFN_MODS)
                    pe.wait_ge(hidlo_ready, f + 1)
                    for n in range(KC):
                        for p in range(3):
                            w = (lo if p == 2 else hi)[:, k, n // 4, (n % 4) * P:(n % 4) * P + P]
                            ins = mm(psum[n // 2][:, (n % 2) * T:(n % 2) * T + T], w,
                                     (hid_lo if p == 1 else hid_hi)[:, f % 4, :],
                                     start=f == 0 and n % 2 == 0 and p == 0,
                                     stop=f == 2 * FBLOCKS - 1 and p == 2, skip_group_check=True)
                    ins.then_inc(down_used, 1)

            for b in range(FBLOCKS):
                for k in range(2):
                    f = 2 * b + k
                    u = UNIT[("gu", b, k)]
                    pe.wait_ge(ehi_ready, u + 1)
                    if f >= 2:
                        pe.wait_ge(hid_ready, f - 1)
                    if f == 0:
                        pe.wait_ge(ylo_ready, 4)
                    for g in range(2):
                        ins = split_product(psum[4 + f % 2][:, g * T:(g + 1) * T], u, y_hi, g)
                    ins.then_inc(gu_done, 1)
                if b in FFN_MOD_BLOCKS:
                    m = 2 * FFN_MODS + FFN_MOD_BLOCKS.index(b)
                    pe.wait_ge(cond_ready, 2)
                    pe.wait_ge(var_ready, 3)
                    mod_partial(m)
                if b:
                    down(b - 1)
                if b in FFN_MOD_BLOCKS:
                    mod_sums(m)
            down(FBLOCKS - 1)
            pe.wait_ge(mod_raw, S5_MODS)
            sums(3 * KC, sq_ready, sq, sum_ready)

            def b_products(b):
                m, qq = b // 4, b % 4
                if b >= 2:
                    pe.wait_ge(bu_used, b - 1)
                for k in range(2):
                    kc = 2 * m + k
                    pe.wait_ge(y_ready, 3 * KC + kc + 1)
                    rows_q = slice(32 * qq, 32 * qq + 32)
                    for c2 in range(2):
                        ins = mm(psum[(b % 2) * 2 + c2][:, k * T:(k + 1) * T], bbT[c2][rows_q, kc, :],
                                 yT[rows_q, kc, :], start=True, stop=True)
                ins.then_inc(bu_done, 1)

            def c_products(b):
                m, qq = b // 4, b % 4
                if qq == 0 and m >= 2:
                    pe.wait_ge(ys_pre, 2 * (m - 1))
                for t, c_ in enumerate((cT[0], cT_neg, cT[1], cT[1])):
                    pe.wait_ge(prod_p, 4 * b + t + 1)
                    for k in range(2):
                        ins = mm(psum[4 + m % 2][32 * qq:32 * qq + 32, k * T:(k + 1) * T],
                                 c_[:, 2 * m + k, 32 * qq:32 * qq + 32], prod[:, t, k, :],
                                 start=t == 0 and k == 0, stop=t == 3, skip_group_check=True)
                    ins.then_inc(prod_used, 1)

            b_products(0)
            b_products(1)
            pe.wait_ge(cneg_ready, 1)
            for b in range(NB):
                if b + 2 < NB:
                    b_products(b + 2)
                if b % 2 == 0:
                    if b == 0:
                        pe.wait_ge(y_ready, 4 * KC)
                    mod_partial(2 * S5_MODS + b // 2)
                c_products(b)
                if b % 2 == 0:
                    mod_sums(2 * S5_MODS + b // 2)
            def token_major(n):
                if n >= 4:
                    pe.wait_ge(tok_c, n - 3)
                src, tb, h = (hT if n < 4 else yT), (n // 2) % 2, n % 2
                for k in range(4):
                    ins = nc.tensor.transpose(psum[n % 4][:, k * P:(k + 1) * P],
                                              src[:, 4 * h + k, tb * P:(tb + 1) * P], ident[:, :])
                ins.then_inc(tok_t, 1)

            split_pairs()
            pe.wait_ge(mod_raw, len(MOD_ORDER))
            sums(4 * KC, sq_ready, sq_late, sum_ready)

            pe.wait_ge(pair_used, 2 * KC)
            for kc in range(KC):
                pe.wait_ge(diag_ready, kc + 1)
                ins = mm(psum[4 + kc // 4][:, (kc % 4) * P:(kc % 4) * P + P], ones[:, :],
                         tmp[:, kc // 4, (kc % 4) * P:(kc % 4) * P + P], start=True, stop=True)
                if kc % 4 == 3:
                    ins.then_inc(g2_done, 1)
            for n in range(4):
                token_major(n)

            pe.wait_ge(g2row_ready, 2)
            pe.wait_ge(selgT_zero, 1)
            for bank, free, slots in ((4, hi_used, HI_SLOTS), (5, lo_used, LO_SLOTS)):
                for k in range(4):
                    ins = mm(psum[bank][:, k * P:(k + 1) * P], zeros[:, :], ones[:, :], start=True, stop=True)
                ins.then_inc(free, slots)

            pe.wait_ge(wr_in, 32)
            for kc in range(KC):
                pe.wait_ge(y_ready, 4 * KC + kc + 1)
                ins = mm(psum[6][0:NE, 0:T], wr[:, kc, :], yT[:, kc, :], start=kc == 0, stop=kc == KC - 1)
            ins.then_inc(log_done, 1)
            token_major(4)
            pe.wait_ge(logT_ready, 1)
            for tb in range(TB):
                ins = nc.tensor.transpose(psum[7][:, tb * P:tb * P + NE], logT[:, tb * P:(tb + 1) * P], ident[0:NE, 0:NE])
            ins.then_inc(logit_t, 1)
            for n in range(5, 8):
                token_major(n)
            pe.wait_ge(mask_ready, 1)
            pe.wait_ge(consts, 6)
            mm(psum[6][:, 128:128 + NE], tri[:, :], rt[:, 2, 0, :], start=True, stop=True)
            mm(psum[6][:, 192:192 + NE], tri[:, :], rt[:, 2, 1, :], start=True, stop=False)
            mm(psum[6][:, 192:192 + NE], ones[:, :], rt[:, 2, 0, :], start=False, stop=True)
            mm(psum[6][:, 256:256 + NE], ones[:, :], rt[:, 2, 0, :], start=True, stop=False)
            mm(psum[6][:, 256:256 + NE], ones[:, :], rt[:, 2, 1, :], start=False, stop=True).then_inc(rank_done, 1)

            def gather(k, g, bank=psum[7]):
                pe.wait_ge(sel_ready, k)
                for c4 in range(4):
                    kc = 4 * g + c4
                    for tb in range(TB):
                        ins = mm(bank[:, c4 * P:(c4 + 1) * P], y_tok[:, tb, kc * P:(kc + 1) * P], sel[:, tb, :],
                                 start=tb == 0, stop=tb == TB - 1)
                ins.then_inc(gath_done, 1)

            pe.wait_ge(tok_c, 8)
            pe.wait_ge(items_ready, 1)
            gather(TB, 0)
            gather(TB, 1, psum[6])

            pe.wait_ge(items_ready, 1)
            total = pe.value_load(count_i[0:1, 0:1], min_val=NE, max_val=MAX_ITEMS)

            def product(i, n):
                kind, j, h = HALVES[n]
                pe.wait_ge(hi_ready, i * NH + n + 1)
                hi, lo = whi[:, n % HI_SLOTS, :], wlo[:, n % LO_SLOTS, :]
                if kind == "D":
                    if h == 0:
                        pe.wait_ge(hl_ready, i * FT + j + 1)
                        if j == 0:
                            pe.wait_ge(yx_ready, (i + 1) * 2)
                    steps = [(hh[:, j % 2, 2 * h + k, :], hl[:, j % 2, 2 * h + k, :], psum[4 + s],
                              (k * D + s * 512), j == 0 and h == 0 and k == 0, j == FT - 1 and h == 1 and k == 1)
                             for k in range(2) for s in range(2)]
                else:
                    if n == 0:
                        pe.wait_ge(xl_ready, i * 2 + 2)
                    bank = psum[(0 if kind == "G" else 2) + j % 2]
                    steps = [(xe_hi[:, 4 * h + k, :], xe_lo[:, 4 * h + k, :], bank, k * 512,
                              h == 0 and k == 0, h == 1 and k == 3) for k in range(4)]
                for k, (xh, xl, o, w, first, last) in enumerate(steps):
                    mm(o[:, :], xh, hi[:, w:w + 512], start=first, stop=False)
                    if k == len(steps) - 1:
                        pe.wait_ge(lo_ready, i * NH + n + 1)
                    ins = mm(o[:, :], xl, hi[:, w:w + 512], start=False, stop=False)
                ins.then_inc(hi_used, 1)
                for xh, xl, o, w, first, last in steps:
                    ins = mm(o[:, :], xh, lo[:, w:w + 512], start=False, stop=last)
                ins.then_inc(lo_used, 1)

            def combine(i, m, bank):
                tb, h = m // 2, m % 2
                if m == 0:
                    pe.wait_ge(yx_ready, (i + 1) * 2)
                mm(bank[:, :], selgT[:, tb * P:(tb + 1) * P], y_exp[:, h * 512:(h + 1) * 512],
                   start=True, stop=True).then_inc(comb_done, 1)

            with pe.Fori(0, total) as i:
                for n in range(NH):
                    product(i, n)
                    if n in COMB_AFTER:
                        m = COMB_AFTER[n]
                        if m:
                            pe.wait_ge(comb_used, i * NCOMB + m)
                        combine(i, m, psum[7])
                    if n == SGT_AFTER:
                        pe.wait_ge(comb_used, (i + 1) * NCOMB)
                        pe.wait_ge(selg_ready, (i + 1) * TB)
                        for tb in range(TB):
                            ins = nc.tensor.transpose(psum[7][:, tb * P:(tb + 1) * P], selg[:, tb, :], ident[:, :])
                        ins.then_inc(selg_t, 1)
                    if n in GATHER_AFTER:
                        g = GATHER_AFTER[n]
                        if g == 0:
                            pe.wait_ge(selgT_ready, i + 1)
                            gather(i * TB + 2 * TB, 0)
                        else:
                            pe.wait_ge(xl_ready, i * 2 + 3)
                            gather(i * TB + 2 * TB, 1)
                    if n in T_AFTER:
                        j = T_AFTER[n]
                        pe.wait_ge(he_ready, i * FT + j + 1)
                        if j:
                            pe.wait_ge(hl_ready, i * FT + j)
                        for k in range(4):
                            ins = nc.tensor.transpose(psum[6][:, k * P:(k + 1) * P], hid_e[:, k * P:(k + 1) * P], ident[:, :])
                        ins.then_inc(t_done, 1)
            pe.wait_ge(selgT_ready, total)
            for m in range(NCOMB):
                combine(total, m, psum[m])


_INS = ["x", "c", "mod_w", "mod_b", "norm1_g", "norm2_g", "conv_w_pw1", "conv_b_pw1", "conv_w_dw",
        "conv_b_dw", "conv_ln_g", "conv_ln_b", "conv_w_pw2", "conv_b_pw2", "ssm_a_re", "ssm_a_im",
        "ssm_log_dt", "ssm_b_re", "ssm_b_im", "ssm_c_re", "ssm_c_im", "ssm_d", "ssm_w_glu",
        "ssm_b_glu", "ffn_w_gate", "ffn_w_up", "ffn_w_down", "moe_w_router", "moe_b_router",
        "moe_w_gate", "moe_w_up", "moe_w_down", "final_norm_g"]


def kernel(**inputs):
    import numpy as _np
    import concourse.bacc as _bacc
    from concourse import mybir as _mybir
    from concourse.bass_utils import run_bass_kernel_spmd as _run

    nc = _bacc.Bacc("TRN2", target_bir_lowering=False, num_devices=1)
    arrays, args = {}, []
    for name in _INS:
        a = _np.ascontiguousarray(inputs[name])
        arrays[f"in_{name}_dram"] = a
        args.append(nc.dram_tensor(f"in_{name}_dram", a.shape, _mybir.dt.from_np(a.dtype),
                                   kind="ExternalInput").ap())
    o = nc.dram_tensor("out_dram", (1, T, D), F32, kind="ExternalOutput").ap()
    trunk(nc, *args, o)
    r = _run(nc, [arrays], core_ids=[0])
    return r.results[0]["out_dram"]
```

```python
from contextlib import ExitStack

import numpy as np
import concourse.bass as bass
from concourse import mybir

F32 = mybir.dt.float32
F32R = mybir.dt.float32r
I32 = mybir.dt.int32
ACT = mybir.ActivationFunctionType
ALU = mybir.AluOpType
AX = mybir.AxisListType

P = 128
D, T, DEPTH = 1024, 256, 2
KC = D // P
TB = T // P
TAPS = 31
PE_TAPS, POOL_TAPS = 2, 8
S5_TURNS = {2: (0, 1), 4: (2, 3, 4), 6: (5, 6, 7)}
TAP_RING = 4
GROUPS, GC, NS = 64, 16, 64
TILES = GROUPS * NS // P
FD, FE, NE = 2816, 3584, 8
FBLOCKS = FD // 256
EPS = 1e-6

EARLY_SLOTS = 4
SH1, SC1, G1, SH2, SC2, G2 = range(6)
MOD_ORDER = [(0, SC1), (0, SH1), (0, SC2), (0, SH2), (0, G1), (0, G2),
             (1, SC1), (1, SH1), (1, G1), (1, SC2), (1, SH2), (1, G2)]
CONV_MODS, NORM_MODS, FFN_MODS, S5_MODS = 2, 4, 6, 8
FFN_MOD_BLOCKS = (2, 4, 6, 8)


def early_stream():
    mods = [("mod", 2 * k + h) for k in range(len(MOD_ORDER)) for h in range(2)]
    tiles = mods[:2 * CONV_MODS]
    for q in range(4):
        tiles += [("pw1", q), mods[2 * CONV_MODS + q]]
    tiles += mods[2 * NORM_MODS:2 * NORM_MODS + 2] + [("pw2", q) for q in range(2)]
    late = mods[2 * FFN_MODS:2 * S5_MODS]
    for b in range(FBLOCKS):
        tiles.append(("gu", b))
        if b == 0:
            tiles += mods[2 * NORM_MODS + 2:2 * FFN_MODS]
        if b in FFN_MOD_BLOCKS:
            tiles.append(late.pop(0))
        if b:
            tiles.append(("down", b - 1))
    tiles.append(("down", FBLOCKS - 1))
    tiles += mods[2 * S5_MODS:]
    tiles += [("glu", q) for q in range(4)]
    assert not late
    return tiles


STREAM = early_stream()
SHIFT = -len(STREAM) % EARLY_SLOTS
WHERE = {(k, i): n for n, (k, i) in enumerate(STREAM)}
DMAS_OF = {"mod": 1, "pw1": 2, "pw2": 1, "gu": 2, "down": 1, "glu": 2}


def slot_of(n):
    return (n + SHIFT) % EARLY_SLOTS


def arrived_count(n):
    return 16 * sum(DMAS_OF[STREAM[m][0]] for m in range(n + 1) if slot_of(m) == slot_of(n))


def consumed(n):
    kind, i = STREAM[n]
    return {"mod": ("mod_part", i + 1),
            "pw1": ("pair_done", 2 * i + 2), "glu": ("pair_done", KC + 2 * i + 2),
            "pw2": ("pw2_done", 4 * i + 4), "gu": ("gu_done", 2 * i + 2),
            "down": ("down_used", 2 * i + 2)}[kind]


def split_units():
    out = [("pw2", q, h) for q in range(2) for h in range(2)]
    for b in range(FBLOCKS):
        out += [("gu", b, k) for k in range(2)]
        if b:
            out.append(("down", b - 1, 0))
    out.append(("down", FBLOCKS - 1, 0))
    return out + [("glu", q, k) for q in range(4) for k in range(2)]


UNITS = split_units()
UNIT = {x: n for n, x in enumerate(UNITS)}


def unit_used(u):
    kind, i, k = UNITS[u]
    return {"pw2": ("pw2_done", 4 * i + 2 * k + 2), "gu": ("gu_done", 2 * i + k + 1),
            "down": ("down_used", 2 * i + 2), "glu": ("pair_done", KC + 2 * i + k + 1)}[kind]


FT = FE // 512


def expert_halves():
    out = []
    for j in range(FT):
        out += [("G", j, h) for h in range(2)] + [("U", j, h) for h in range(2)]
        if j >= 2:
            out += [("D", j - 2, h) for h in range(2)]
    return out + [("D", j, h) for j in (FT - 2, FT - 1) for h in range(2)]


HALVES = expert_halves()
NH = len(HALVES)
AT = {x: n for n, x in enumerate(HALVES)}
RAW_SLOTS = 14
HI_SLOTS, LO_SLOTS = 3, 2
assert NH % RAW_SLOTS == 0 and NH % HI_SLOTS == 0 and NH % LO_SLOTS == 0
HW = 2048
T_AFTER = {AT[("U", j + 1, 1)]: j for j in range(FT - 1)}
T_AFTER[AT[("D", FT - 3, 1)]] = FT - 1
NCOMB = 2 * TB
COMB_AFTER = {AT[("U", m, 1)]: m for m in range(NCOMB)}
COMB_SLOTS = list(COMB_AFTER)
SEL_T_AFTER = AT[("U", 4, 1)]
GATHER_AFTER = {AT[("D", FT - 3, 1)]: 0, AT[("D", FT - 2, 1)]: 1}
MAX_WIDE = 3
MAX_ITEMS = NE + 1
MAX_ROWS = NE + MAX_WIDE + 1

MAGIC = 1.5 * 2.0 ** 23
LOG2E = 1.4426950408889634
LN2_HI, LN2_LO = 0.693359375, -2.12194440e-4
TWO_PI = [6.28125, 0.0019350051879882812, 3.0199159819567e-7]
EXP_COEF = [1.0 / 5040, 1.0 / 720, 1.0 / 120, 1.0 / 24, 1.0 / 6, 0.5, 1.0]

ROWS = {}
for _tile, _names in enumerate([
        [("mod_b", 96)],
        [("dw_lo", 128)],
        [("dw_hi", TAPS * KC - 128)],
        [("c", 8), ("norm1_g", 16), ("norm2_g", 16), ("b_pw1", 16), ("b_dw", 8), ("ln_g", 8),
         ("ln_b", 8), ("b_pw2", 8), ("ssm_d", 8), ("b_glu", 16)],
        [("a_re", 32), ("a_im", 32), ("log_dt", 32)]]):
    _r = 0
    for _n, _k in _names:
        ROWS[_n] = (_tile, _r, _k)
        _r += _k
ROW_TILES = [96, 128, TAPS * KC - 128, 112, 96]


def trunk(nc, x, c, mod_w, mod_b, norm1_g, norm2_g, w_pw1, b_pw1, w_dw, b_dw, ln_g, ln_b, w_pw2,
          b_pw2, a_re, a_im, log_dt, b_re, b_im, c_re, c_im, ssm_d, w_glu, b_glu, w_gate, w_up,
          w_down, w_router, b_router, e_gate, e_up, e_down, final_g, out):
    ctx = ExitStack()
    with ctx:
        BASE = 16512

        def at(name, shape, offset, dtype=F32):
            return nc.alloc_sbuf_tensor_at(name, shape, dtype, offset=BASE + offset)

        def sem(name):
            return ctx.enter_context(nc.semaphore(name))

        KB = 1024
        ring = at("ring", [P, RAW_SLOTS * HW], 0)
        ring_lo = at("ring_lo", [P, EARLY_SLOTS * 4096], 0, F32R)
        ehi = at("ehi", [P, 2, 2048], 64 * KB, F32R)
        LOW = 80 * KB
        bbT = [at(f"bbT_{n}", [P, KC, P], LOW + 4 * KB * n) for n, _ in enumerate("ri")]
        cT = [at(f"cT_{n}", [P, KC, P], LOW + 8 * KB + 4 * KB * n) for n, _ in enumerate("ri")]
        modacc = at("modacc", [P, 2, 512], LOW + 16 * KB)
        diag = at("diag", [P, 2, PE_TAPS, P], LOW + 24 * KB)
        tapped = at("tapped", [P, TAP_RING, T], LOW + 20 * KB)
        tapsum = at("tapsum", [P, 2, T], LOW + 28 * KB)
        hid = at("hid", [P, 4, T], LOW + 20 * KB)
        hid_lo = at("hid_lo", [P, 4, T], LOW + 20 * KB, F32R)
        hid_hi = at("hid_hi", [P, 4, T], LOW + 16 * KB, F32R)
        xrot = at("xrot", [P, 2, 2, 2, T], LOW + 16 * KB)
        sq = at("sq", [P, KC, T], LOW + 24 * KB)
        y_hi = at("y_hi", [P, KC, T], LOW + 24 * KB, F32R)
        prod = at("prod", [P, 4, 2, T], LOW + 24 * KB)
        B = 112 * KB
        x_tok = at("x_tok", [P, TB, D], B)
        PAD = T + TAPS - 1
        upad = at("upad", [P, KC, PAD], B + 8 * KB)
        conv = at("conv", [P, KC, T], B + 17 * KB + 512)
        rows = at("rows", [P, len(ROW_TILES), P], B + 26 * KB)
        braw = [at(f"braw_{n}", [P, TILES, GC], B + 29 * KB + 2 * KB * n) for n in range(2)]
        bblk = [at(f"bblk_{n}", [P, TILES, 2 * GC], B + 33 * KB + 4 * KB * n) for n in range(2)]
        craw = [at(f"craw_{n}", [P, KC, NS], B + 41 * KB + 2 * KB * n) for n in range(2)]
        cblk = [at(f"cblk_{n}", [P, KC, P], B + 45 * KB + 4 * KB * n) for n in range(2)]
        btmp = [at(f"btmp_{n}", [P, TILES, GC], B + 53 * KB + 2 * KB * n) for n in range(4)]
        tabc = at("tabc", [P, TILES, T], B)
        tabs = at("tabs", [P, TILES, T], B + 32 * KB)
        cT_neg = at("cT_neg", [P, KC, P], 64 * KB)
        z_hi = at("z_hi", [P, KC, T], B, F32R)
        whi = at("whi", [P, HI_SLOTS, HW], B, F32R)
        wlo = at("wlo", [P, LO_SLOTS, HW], B + 24 * KB, F32R)
        acc = at("acc", [P, TB, D], B + 40 * KB)
        sq_late = at("sq_late", [P, KC, T], B + 40 * KB)
        y_tok = at("y_tok", [P, TB, D], B + 48 * KB)
        g2_row = at("g2_row", [P, D], B + 56 * KB)
        y_exp = at("y_exp", [P, D], B + 60 * KB)
        yx_lo = at("yx_lo", [P, D], B + 60 * KB, F32R)
        fin_g = at("fin_g", [P, D], 0)
        fin_sq = at("fin_sq", [P, D], 4 * KB)
        hT = at("hT", [P, KC, T], 176 * KB)
        yT = at("yT", [P, KC, T], 184 * KB)
        y_lo = at("y_lo", [P, KC, T], 184 * KB, F32R)
        xe_hi = at("xe_hi", [P, KC, P], 176 * KB, F32R)
        xe_lo = at("xe_lo", [P, KC, P], 180 * KB, F32R)
        hh = at("hh", [P, 2, 4, P], 184 * KB, F32R)
        hl = at("hl", [P, 2, 4, P], 188 * KB, F32R)
        M = 192 * KB
        ident = at("ident", [P, P], M)
        ones = at("ones", [P, P], M + 512)
        cols = at("cols", [P, len(ROW_TILES), P], M + 1024)
        modc = at("modc", [P, DEPTH * 6, KC], M + 3584)
        ab = at("ab", [P, 8, KC], M + 3968)
        cond = at("cond", [P, KC, 32], B + 61 * KB)
        cond_late = at("cond_late", [P, KC, 32], M + 1024 + 512)
        zeros = at("zeros", [P, P], M + 1024 + 512)
        sum_col = at("sum_col", [P, 1], M + 4224)
        modraw = at("modraw", [P, DEPTH * 6, KC], M + 15616)
        sp5 = at("sp5", [P, 20, TILES], M + 4256)
        sp5i = at("sp5i", [P, TILES], M + 6816, I32)
        masks = at("masks", [P, 4], M + 6944)
        iota_t = at("iota_t", [P, T], M + 6976)
        nrm = at("nrm", [P, 3, T], M + 8000)
        modacc_s5 = at("modacc_s5", [P, 512], M + 8000)
        sel = at("sel", [P, TB, P], M + 8000)
        selT = at("selT", [P, T], M + 10048, F32R)
        yx_hi = at("yx_hi", [P, 512], M + 4256, F32R)
        tmp = at("tmp", [P, 2, 512], M + 11072)
        silu_g = at("silu_g", [P, 512], M + 11072)
        hid_e = at("hid_e", [P, 512], M + 13120)
        rt = at("rt", [P, 12, TB, NE], M + 4256)
        tri = at("tri", [P, P], M + 6976)
        iota_s = at("iota_s", [P, P], M + 6976 + 512)
        wr = at("wr", [P, KC, NE], B)
        logT = at("logT", [NE, T], B + 24 * KB)
        R = M + 15168
        logit = at("logit", [P, TB, NE], R)
        items = at("items", [P, MAX_ROWS, 4], R + 64)
        now = at("now", [P, 8], R + 256)
        iota_e = at("iota_e", [P, NE], R + 320)
        bcol = at("bcol", [NE, 1], R + 352)
        counts_i = at("counts_i", [P, 4], R + 384, I32)
        place = at("place", [P, MAX_ROWS, NE], M + 5056)
        placed = at("placed", [P, MAX_ROWS, NE], M + 5440)
        order_i = at("order_i", [P, MAX_ROWS], M + 16000, I32)
        picked = at("picked", [P, MAX_ROWS, 4, NE], M + 5888)
        xw_hi = at("xw_hi", [P, KC, T], 176 * KB, F32R)
        xw_lo = at("xw_lo", [P, KC, T], 184 * KB, F32R)
        wide_at = [B + 48 * KB, B + 56 * KB, M + 6976]
        hw_hi = [at(f"hw_hi{n}", [P, 4, T], o, F32R) for n, o in enumerate(wide_at)]
        hw = [at(f"hw{n}", [P, 4, T], o + 4 * KB) for n, o in enumerate(wide_at)]
        hw_lo = [at(f"hw_lo{n}", [P, 4, T], o + 4 * KB, F32R) for n, o in enumerate(wide_at)]
        out_w = at("out_w", [P, KC, T], B + 56 * KB)
        ldt_rows = at("ldt_rows", [P, 4], R + 416)

        psum = [ctx.enter_context(nc.psum_tensor(f"bank{n}", [P, 512], F32)) for n in range(8)]

        def col(name, i=0):
            tile, r, _ = ROWS[name]
            return cols[:, tile, r + i:r + i + 1]

        def colv(name, i, n):
            tile, r, _ = ROWS[name]
            return cols[:, tile, r + i:r + i + n]

        def dw(tap, kc):
            r = tap * KC + kc
            return cols[:, 1 + r // P, r % P:r % P + 1]

        def early(n, parts):
            s = slot_of(n)
            return ring[:, s * 4096:(s + 1) * 4096].rearrange("p (k n) -> p k n", k=parts)

        def unit_views(u):
            kind, i, k = UNITS[u]
            s = slot_of(WHERE[(kind, i)])
            hi = ehi[:, u % 2, :]
            if kind == "down":
                w, lo = (t[:, s * 4096:s * 4096 + 2048].rearrange("p (k g n) -> p k g n", k=2, g=2)
                         for t in (ring, ring_lo))
                return w, lo, hi.rearrange("p (k g n) -> p k g n", k=2, g=2)
            w, lo = (t[:, s * 4096:(s + 1) * 4096].rearrange("p (k n) -> p k n", k=KC)
                     for t in (ring, ring_lo))
            if kind == "pw2":
                w, lo = (t[:, :, k * 256:(k + 1) * 256].rearrange("p k (g n) -> p k g n", g=2) for t in (w, lo))
            else:
                w, lo = (t.rearrange("p k (g n) -> p k g n", g=2)[:, :, :, k * P:(k + 1) * P] for t in (w, lo))
            return w, lo, hi.rearrange("p (k g n) -> p k g n", k=KC, g=2)

        x_in, rows_in, s5_in, wr_in, fg_in, out_done = (
            sem(n) for n in ("x_in", "rows_in", "s5_in", "wr_in", "fg_in", "out_done"))
        arr = [sem(f"arr{n}") for n in range(EARLY_SLOTS)]
        consts = sem("consts")
        rows_ready = sem("rows_ready")
        rows_t, cols_ready = sem("rows_t"), sem("cols_ready")
        cond_ready, sum_col_ready = sem("cond_ready"), sem("sum_col_ready")
        x_t, h_ready = sem("x_t"), sem("h_ready")
        mod_part, mod_acc, mod_sum, mod_raw, modc_ready = (
            sem(n) for n in ("mod_part", "mod_acc", "mod_sum", "mod_raw", "modc_ready"))
        ab_ready = sem("ab_ready")
        sq_ready, sum_ready, var_ready, std_ready = (sem(n) for n in ("sq_ready", "sum_ready", "var_ready", "std_ready"))
        raw_ready, y_ready = sem("raw_ready"), sem("y_ready")
        pair_done, sig_ready, pair_used = sem("pair_done"), sem("sig_ready"), sem("pair_used")
        conv_ready, mean_sum, cent_ready = sem("conv_ready"), sem("mean_sum"), sem("cent_ready")
        pw2_done, pw2_tmp, h2_ready = sem("pw2_done"), sem("pw2_tmp"), sem("h2_ready")
        gu_done, gsil, hid_ready, down_used = (sem(n) for n in ("gu_done", "gsil", "hid_ready", "down_used"))
        h3_ready, h4_ready = sem("h3_ready"), sem("h4_ready")
        ehi_ready, elo_ready = sem("ehi_ready"), sem("elo_ready")
        yhi_ready, ylo_ready = sem("yhi_ready"), sem("ylo_ready")
        hidhi_ready, hidlo_ready = sem("hidhi_ready"), sem("hidlo_ready")
        tapped_ready, tapsum_ready = sem("tapped_ready"), sem("tapsum_ready")
        diag_made, taps_done = sem("diag_made"), sem("taps_done")
        chain, tap = sem("chain"), sem("tap")
        blk_ready, blk_t, blk_c = sem("blk_ready"), sem("blk_t"), sem("blk_c")
        trig_in, trig, trig_out = sem("trig_in"), sem("trig"), sem("trig_out")
        rnd_ready, frac_ready, sin_ready, tab_ready = (sem(n) for n in ("rnd_ready", "frac_ready", "sin_ready", "tab_ready"))
        act_own, pool_own = sem("act_own"), sem("pool_own")
        ones_pad = sem("ones_pad")
        bu_done, bu_used, scan_ready, prod_p, prod_used, ys_pre, z_ready = (
            sem(n) for n in ("bu_done", "bu_used", "scan_ready", "prod_p", "prod_used",
                             "ys_pre", "z_ready"))
        cneg_ready, prod_v = sem("cneg_ready"), sem("prod_v")
        log_done, rank_done, mask_ready, diag_ready, g2_done = (
            sem(n) for n in ("log_done", "rank_done", "mask_ready", "diag_ready", "g2_done"))
        logT_ready, logit_t = sem("logT_ready"), sem("logit_t")
        tok_t, tok_c, exp2_in, exp2 = sem("tok_t"), sem("tok_c"), sem("exp2_in"), sem("exp2")
        items_ready, g2row_ready = sem("items_ready"), sem("g2row_ready")
        xw_t, xwh_ready, xwl_ready = sem("xw_t"), sem("xwh_ready"), sem("xwl_ready")
        sw_ready, hw_ready, hwh_ready, hwl_ready = (
            sem(n) for n in ("sw_ready", "hw_ready", "hwh_ready", "hwl_ready"))
        outw_ready, outw_t = sem("outw_ready"), sem("outw_t")
        raw_in = [sem(f"raw_in{n}") for n in range(RAW_SLOTS)]
        hi_ready, lo_ready, hi_used, lo_used = (sem(n) for n in ("hi_ready", "lo_ready", "hi_used", "lo_used"))
        s_ready, he_ready, t_done, hh_ready, hl_ready = (
            sem(n) for n in ("s_ready", "he_ready", "t_done", "hh_ready", "hl_ready"))
        yx_ready, comb_done, comb_used = (sem(n) for n in ("yx_ready", "comb_done", "comb_used"))
        sel_ready, sel_t, selT_ready = (sem(n) for n in ("sel_ready", "sel_t", "selT_ready"))
        yxh_ready, yxl_ready = sem("yxh_ready"), sem("yxl_ready")
        gath_done, xh_ready, xl_ready = sem("gath_done"), sem("xh_ready"), sem("xl_ready")
        fin_var, fin_std, fin_ready = (sem(n) for n in ("fin_var", "fin_std", "fin_ready"))
        zeros_ready, now_ready, acc_half = sem("zeros_ready"), sem("now_ready"), sem("acc_half")

        block = ctx.enter_context(nc.Block())
        S5_TABLE_ORDER = [(2 * m + k) * 4 + q for m in range(4) for q in range(4) for k in range(2)]
        TABLES_AT = [0, 4, 4] + [3] * 8
        NB = 16

        def mod_place(m):
            if m < 2 * FFN_MODS:
                return psum[3 + 3 * (m % 2)], psum[2], modacc[:, m % 2, :].rearrange("p (a n) -> p a n", a=2)
            if m < 2 * S5_MODS:
                return psum[6], psum[7], tmp[:, :, T:2 * T]
            return psum[6], psum[7], modacc_s5[:, :].rearrange("p (a n) -> p a n", a=2)

        def mc(l, v, kc=None):
            a = modc[:, l * 6 + v, :]
            return a if kc is None else a[:, kc:kc + 1]

        CONSUMED = {"mod_part": mod_part, "pair_done": pair_done,
                    "pw2_done": pw2_done, "gu_done": gu_done, "down_used": down_used}

        def tap_adds(q):
            return q // POOL_TAPS * (POOL_TAPS - 1) + max(q % POOL_TAPS, 1)

        DVE_FROM = PE_TAPS + POOL_TAPS

        dwr = w_dw[0].rearrange("t (k p) -> (t k) p", p=P)
        row_srcs = {
            "mod_b": mod_b.rearrange("l (k p) -> (l k) p", p=P),
            "dw_lo": dwr[0:P, :], "dw_hi": dwr[P:TAPS * KC, :],
            "c": c.rearrange("a (k p) -> (a k) p", p=P),
            "norm1_g": norm1_g.rearrange("l (k p) -> (l k) p", p=P),
            "norm2_g": norm2_g.rearrange("l (k p) -> (l k) p", p=P),
            "b_pw1": b_pw1.rearrange("a (k p) -> (a k) p", p=P),
            "b_dw": b_dw.rearrange("a (k p) -> (a k) p", p=P),
            "ln_g": ln_g.rearrange("a (k p) -> (a k) p", p=P),
            "ln_b": ln_b.rearrange("a (k p) -> (a k) p", p=P),
            "b_pw2": b_pw2.rearrange("a (k p) -> (a k) p", p=P),
            "ssm_d": ssm_d.rearrange("a (k p) -> (a k) p", p=P),
            "b_glu": b_glu.rearrange("a (k p) -> (a k) p", p=P),
            "a_re": a_re[0].rearrange("(i g) s -> i (g s)", g=2),
            "a_im": a_im[0].rearrange("(i g) s -> i (g s)", g=2),
            "log_dt": log_dt[0].rearrange("(i g) -> i g", g=2),
        }
        ROW_NAMES = sorted(ROWS, key=lambda name: name != "c")

        def load_rows(eng, names):
            for name in names:
                tile, r, k = ROWS[name]
                dst = ldt_rows[r:r + k, 0:2] if name == "log_dt" else rows[r:r + k, tile, :]
                eng.dma_start(dst, row_srcs[name]).then_inc(rows_in, 16)

        @block.sync
        def _(sp):
            sp.dma_start(x_tok[:, 0, :], x[0, 0:P, :]).then_inc(x_in, 16)
            load_rows(sp, ROW_NAMES[1::2])
            for n, (kind, i) in enumerate(STREAM):
                prev = n - EARLY_SLOTS
                if n == WHERE[("pw1", 0)] + 1:
                    for n, w in enumerate((b_re, b_im)):
                        sp.dma_start(braw[n][:, :, :], w[0].rearrange("g s c -> (g s) c").rearrange("(i p) c -> p i c", p=P)).then_inc(s5_in, 16)
                    for n, w in enumerate((c_re, c_im)):
                        sp.dma_start(craw[n][:, :, :], w[0].rearrange("g c s -> (g c) s").rearrange("(k p) s -> p k s", p=P)).then_inc(s5_in, 16)
                if prev >= 0:
                    name, count = consumed(prev)
                    sp.wait_ge(CONSUMED[name], count)
                a = arr[slot_of(n)]
                if kind == "mod":
                    (l, v), h = MOD_ORDER[i // 2], i % 2
                    src = mod_w[l, :, v * D + h * 512:v * D + (h + 1) * 512]
                    sp.dma_start(early(n, KC), src.rearrange("(k p) n -> p k n", p=P)).then_inc(a, 16)
                elif kind in ("pw1", "glu"):
                    w = w_pw1 if kind == "pw1" else w_glu
                    for g in range(2):
                        src = w[0, :, g * D + i * 256:g * D + (i + 1) * 256]
                        sp.dma_start(early(n, KC)[:, :, g * 256:(g + 1) * 256],
                                     src.rearrange("(k p) n -> p k n", p=P)).then_inc(a, 16)
                elif kind == "gu":
                    for g, w in enumerate((w_gate, w_up)):
                        src = w[0, :, i * 256:(i + 1) * 256]
                        sp.dma_start(early(n, KC)[:, :, g * 256:(g + 1) * 256],
                                     src.rearrange("(k p) n -> p k n", p=P)).then_inc(a, 16)
                elif kind == "pw2":
                    src = w_pw2[0, :, i * 512:(i + 1) * 512]
                    sp.dma_start(early(n, KC), src.rearrange("(k p) n -> p k n", p=P)).then_inc(a, 16)
                else:
                    src = w_down[0, i * 256:(i + 1) * 256, :]
                    sp.dma_start(early(n, 4)[:, 0:2, :], src.rearrange("(k p) n -> p k n", p=P)).then_inc(a, 16)

            def half(e, n):
                kind, j, h = HALVES[n]
                s = n % RAW_SLOTS
                e1 = bass.ds(e, 1)
                if kind == "D":
                    src = e_down[0, e1, j * 512 + h * 256:j * 512 + (h + 1) * 256, :]
                    src = src.rearrange("e (k p) n -> p (e k) n", p=P)
                    dst = ring[:, s * HW:(s + 1) * HW].rearrange("p (k n) -> p k n", k=2)
                else:
                    w = e_gate if kind == "G" else e_up
                    src = w[0, e1, h * 512:(h + 1) * 512, j * 512:(j + 1) * 512]
                    src = src.rearrange("e (k p) n -> p (e k) n", p=P)
                    dst = ring[:, s * HW:(s + 1) * HW].rearrange("p (k n) -> p k n", k=4)
                sp.dma_start(dst, src).then_inc(raw_in[s], 16)

            for n in range(NH):
                if n < 2 * EARLY_SLOTS:
                    if n % 2 == 0:
                        m = len(STREAM) - EARLY_SLOTS + n // 2
                        name, count = consumed(m)
                        sp.wait_ge(CONSUMED[name], count)
                elif n >= RAW_SLOTS:
                    sp.wait_ge(lo_ready, n - RAW_SLOTS + 1)
                half(0, n)
            sp.wait_ge(items_ready, 1)
            total = sp.value_load(counts_i[0:1, 2:3], min_val=NE, max_val=MAX_ITEMS)
            with sp.Fori(1, total) as i:
                e = sp.value_load(order_i[0:1, bass.ds(i, 1)], min_val=0, max_val=NE - 1)
                for n in range(NH):
                    sp.wait_ge(lo_ready, i * NH + (n - RAW_SLOTS + 1))
                    half(e, n)
            sp.wait_ge(lo_ready, total * NH)
            sp.dma_start(fin_g[:, :], final_g.rearrange("(a n) -> a n", a=1).broadcast_to([P, D])).then_inc(fg_in, 16)
            for tb in range(TB):
                sp.wait_ge(fin_ready, tb + 1)
                sp.dma_start(out[0, tb * P:(tb + 1) * P, :], acc[:, tb, :]).then_inc(out_done, 16)
            sp.wait_ge(out_done, 16 * TB)

        @block.gpsimd
        def _(pool):
            pool.memset(ident[:, :], 0.0).then_inc(pool_own, 1)
            pool.memset(ones[:, :], 1.0).then_inc(consts, 1)
            pool.wait_ge(pool_own, 1)
            pool.affine_select(out=ident[:, :], in_=ident[:, :], compare_op=ALU.not_equal, fill=1.0,
                               base=0, pattern=[[-1, P]], channel_multiplier=1).then_inc(consts, 1)
            pool.iota(iota_t[:, :], pattern=[[1, T]], base=0, channel_multiplier=0,
                      allow_small_or_imprecise_dtypes=True).then_inc(consts, 1)
            pool.memset(upad[:, :, 0:TAPS - 1], 0.0).then_inc(ones_pad, 1)
            for n in range(2):
                pool.memset(bblk[n][:, :, :], 0.0).then_inc(ones_pad, 1)
            pool.iota(iota_e[:, :], pattern=[[1, NE]], base=0, channel_multiplier=0,
                      allow_small_or_imprecise_dtypes=True).then_inc(consts, 1)

            for q in range(KC * POOL_TAPS):
                n, k = q // POOL_TAPS, q % POOL_TAPS
                if k == 0:
                    continue
                if k == 1 and n >= 2:
                    pool.wait_ge(conv_ready, n - 1)
                pool.wait_ge(tapped_ready, q + 1)
                o = tapsum[:, n % 2, :]
                if k > 1:
                    pool.wait_ge(tapsum_ready, tap_adds(q) - 1)
                pool.tensor_tensor(o, tapped[:, (q - 1) % TAP_RING, :] if k == 1 else o,
                                   tapped[:, q % TAP_RING, :], ALU.add).then_inc(tapsum_ready, 1)

            pool.wait_ge(trig_out, 1)
            pool.wait_ge(y_ready, 2 * KC)
            pool.wait_ge(blk_c, 8)
            own = 1
            for n, i in enumerate(S5_TABLE_ORDER):
                pool.tensor_scalar(tabs[:, n, :], iota_t[:, :], sp5[:, 10, i:i + 1], MAGIC,
                                   ALU.mult, ALU.add).then_inc(pool_own, 1)
                own += 1
                pool.wait_ge(pool_own, own)
                pool.tensor_scalar(tabs[:, n, :], tabs[:, n, :], MAGIC, None, ALU.subtract).then_inc(rnd_ready, 1)
                if n >= 2:
                    pool.wait_ge(sin_ready, n - 1)
                    pool.tensor_scalar(tabc[:, n - 2, :], tabc[:, n - 2, :], -2.0, 1.0,
                                       ALU.mult, ALU.add).then_inc(tab_ready, 1)
            for n in (TILES - 2, TILES - 1):
                pool.wait_ge(sin_ready, n + 1)
                pool.tensor_scalar(tabc[:, n, :], tabc[:, n, :], -2.0, 1.0,
                                   ALU.mult, ALU.add).then_inc(tab_ready, 1)
            pool.wait_ge(tab_ready, TILES)
            for b in range(NB):
                pool.wait_ge(scan_ready, b + 1)
                xr, xi = xrot[:, b % 2, 0, :, :], xrot[:, b % 2, 1, :, :]
                tc, ts = tabc[:, 2 * b:2 * b + 2, :], tabs[:, 2 * b:2 * b + 2, :]
                for t, (tab, x_) in enumerate(((tc, xr), (ts, xi), (ts, xr), (tc, xi))):
                    if b == NB - 1 and t >= 2:
                        break
                    if b:
                        pool.wait_ge(prod_used, 4 * (b - 1) + t + 1)
                    pool.tensor_tensor(prod[:, t, :, :], tab, x_, ALU.mult).then_inc(prod_p, 1)
            pool.iota(iota_s[:, :], pattern=[[1, P]], base=0, channel_multiplier=0,
                      allow_small_or_imprecise_dtypes=True).then_inc(consts, 1)
            pool.memset(tri[:, :], 1.0).then_inc(pool_own, 1)
            pool.wait_ge(pool_own, own + 1)
            pool.affine_select(out=tri[:, :], in_=tri[:, :], compare_op=ALU.is_ge, fill=0.0,
                               base=0, pattern=[[1, P]], channel_multiplier=-1).then_inc(consts, 1)

        @block.scalar
        def _(act):
            load_rows(act, ROW_NAMES[0::2])
            act.dma_start(x_tok[:, 1, :], x[0, P:2 * P, :]).then_inc(x_in, 16)
            for n, k in enumerate(ROW_TILES):
                act.wait_ge(rows_t, 4 if n < 4 else 5)
                act.activation(cols[:, n, 0:k], psum[0 if n < 4 else 1][:, (n % 4) * P:(n % 4) * P + k],
                               ACT.Copy).then_inc(cols_ready, 1)
            act.wait_ge(cols_ready, 4)
            act.activation(cond[:, :, :], colv("c", 0, KC).unsqueeze(2).broadcast_to([P, KC, 32]),
                           ACT.Silu).then_inc(cond_ready, 1)
            for n in range(4):
                act.wait_ge(x_t, n + 1)
                act.activation(hT[:, 2 * n:2 * n + 2, :], psum[4 + n % 2][:, :].rearrange("p (k t) -> p k t", k=2),
                               ACT.Copy).then_inc(h_ready, 1)

            def squares(src, dst, ready, first):
                for kc in range(KC):
                    act.wait_ge(ready, first(kc))
                    act.activation(dst[:, kc, :], src[:, kc, :], ACT.Square).then_inc(sq_ready, 1)

            def root(k):
                act.wait_ge(var_ready, k + 1)
                act.activation(nrm[:, 1, :], nrm[:, 0, :], ACT.Sqrt).then_inc(std_ready, 1)

            def split_hi(u):
                t = WHERE[UNITS[u][:2]]
                act.wait_ge(arr[slot_of(t)], arrived_count(t))
                if u >= 2:
                    name, count = unit_used(u - 2)
                    act.wait_ge(CONSUMED[name], count)
                w, _, hi = unit_views(u)
                act.activation(hi, w, ACT.Copy).then_inc(ehi_ready, 1)

            def y_split_hi(dst, g, ready, count):
                act.wait_ge(ready, count)
                act.activation(dst[:, 4 * g:4 * g + 4, :], yT[:, 4 * g:4 * g + 4, :], ACT.Copy).then_inc(yhi_ready, 1)

            def shifted(k, func, gain, shift, src, split=False):
                for kc in range(KC):
                    act.wait_ge(raw_ready, k * KC + kc + 1)
                    act.activation(yT[:, kc, :], src[:, kc, :], func, scale=gain(kc),
                                   bias=shift(kc)).then_inc(y_ready, 1)
                    if split and kc % 4 == 3:
                        y_split_hi(y_hi, kc // 4, y_ready, k * KC + kc + 1)

            def mod_copy(m):
                act.wait_ge(mod_part, m + 1)
                bank, _, dst = mod_place(m)
                if m >= 2:
                    act.wait_ge(mod_sum, m - 1)
                act.activation(dst, bank[:, :].rearrange("p (a n) -> p a n", a=2), ACT.Copy).then_inc(mod_acc, 1)

            def mod_vector(k):
                act.wait_ge(mod_sum, 2 * k + 2)
                act.activation(modraw[:, k, :], mod_place(2 * k)[1][:, 0:KC], ACT.Copy).then_inc(mod_raw, 1)

            def s5_copies(ns):
                for n in ns:
                    act.wait_ge(blk_t, n + 1)
                    src = psum[3 + 3 * (n % 2)][:, :].rearrange("p (k s) -> p k s", k=4)
                    dst = (bbT[n // 2] if n < 4 else cT[n // 2 - 2])[:, (n % 2) * 4:(n % 2) * 4 + 4, :]
                    act.activation(dst, src, ACT.Copy).then_inc(blk_c, 1)

            squares(hT, sq, h_ready, lambda kc: kc // 2 + 1)
            root(0)
            act.wait_ge(trig_in, 1)
            act.activation(sp5[:, 11, :], sp5[:, 8, :], ACT.Sin).then_inc(trig, 1)
            act.activation(sp5[:, 12, :], sp5[:, 8, :], ACT.Sin, scale=0.5).then_inc(trig, 1)
            for k in range(CONV_MODS):
                mod_copy(2 * k)
                mod_copy(2 * k + 1)
                mod_vector(k)
            act.wait_ge(modc_ready, 2)
            act.wait_ge(ab_ready, 1)
            shifted(0, ACT.Identity, lambda kc: ab[:, 0, kc:kc + 1], lambda kc: mc(0, SH1, kc), yT)

            def diagonals(n):
                if n >= 2:
                    act.wait_ge(taps_done, n - 1)
                for k in range(PE_TAPS):
                    ins = act.activation(diag[:, n % 2, k, :], ident[:, :], ACT.Copy, scale=dw(k, n))
                ins.then_inc(diag_made, 1)

            def products(n):
                act.wait_ge(pair_used, n + 1)
                for k in range(POOL_TAPS):
                    q = n * POOL_TAPS + k
                    if q >= TAP_RING:
                        act.wait_ge(tapsum_ready, tap_adds(q - TAP_RING))
                    act.activation(tapped[:, q % TAP_RING, :], upad[:, n, PE_TAPS + k:PE_TAPS + k + T],
                                   ACT.Copy, scale=dw(PE_TAPS + k, n)).then_inc(tapped_ready, 1)

            def sigmoids(k0, bias):
                if k0 == 0:
                    act.wait_ge(var_ready, 1)
                    diagonals(0)
                for n in range(KC):
                    act.wait_ge(pair_done, k0 + n + 1)
                    if k0 + n >= 2:
                        act.wait_ge(pair_used, k0 + n - 1)
                    act.activation(tmp[:, n % 2, 0:T], psum[4 + n % 2][:, T:2 * T], ACT.Sigmoid,
                                   bias=bias(n)).then_inc(sig_ready, 1)
                    if k0 == 0 and n % 2:
                        m = 2 * CONV_MODS + n // 2
                        mod_copy(m)
                    if k0 == 0:
                        s5_copies(S5_TURNS.get(n, ()))
                    if k0 == 0 and n + 1 < KC:
                        diagonals(n + 1)
                    if k0 == 0:
                        products(n)
                    if k0 == 0 and n % 4 == 3:
                        mod_vector(m // 2)
                    if k0 and n + 2 < KC:
                        split_hi(UNIT[("glu", 0, 0)] + n + 2)

            sigmoids(0, lambda n: col("b_pw1", KC + n))
            split_hi(0)
            split_hi(1)
            squares(conv, sq, cent_ready, lambda kc: kc + 1)
            root(1)
            mod_copy(2 * NORM_MODS)
            mod_copy(2 * NORM_MODS + 1)
            shifted(1, ACT.Silu, lambda kc: col("ln_g", kc), lambda kc: col("ln_b", kc), conv, split=True)
            mod_vector(NORM_MODS)
            act.activation(cond_late[:, :, :], cond[:, :, :], ACT.Copy).then_inc(cond_ready, 1)
            act.wait_ge(ab_ready, 3)
            for n in range(KC):
                act.wait_ge(pw2_done, n + 1)
                if n >= 2:
                    act.wait_ge(h2_ready, n - 1)
                act.activation(tmp[:, n % 2, 0:T], psum[4 + n % 2][:, 0:T], ACT.Identity,
                               scale=mc(0, G1, n), bias=ab[:, 2, n:n + 1]).then_inc(pw2_tmp, 1)
                if n in (1, 3, 5):
                    split_hi(n // 2 + 2)
            squares(hT, conv, h2_ready, lambda kc: kc + 1)
            split_hi(5)
            root(2)
            mod_copy(2 * NORM_MODS + 2)
            mod_copy(2 * NORM_MODS + 3)
            shifted(2, ACT.Identity, lambda kc: ab[:, 1, kc:kc + 1], lambda kc: mc(0, SH2, kc), yT, split=True)
            mod_vector(NORM_MODS + 1)

            def sin_tables(n):
                act.wait_ge(frac_ready, n + 1)
                act.activation(tabs[:, n, :], tabc[:, n, :], ACT.Sin, scale=6.2831840).then_inc(act_own, 1)
                if n >= 2:
                    act.wait_ge(sin_ready, n - 1)
                act.activation(nrm[:, n % 2, :], tabc[:, n, :], ACT.Sin, scale=3.14159265).then_inc(act_own, 1)
                act.wait_ge(act_own, 2 * n + 2)
                act.activation(tabc[:, n, :], nrm[:, n % 2, :], ACT.Square).then_inc(sin_ready, 1)

            made = 0
            for b in range(FBLOCKS):
                for f in (2 * b, 2 * b + 1):
                    act.wait_ge(gu_done, f + 1)
                    if f >= 2:
                        act.wait_ge(hid_ready, f - 1)
                    act.activation(tmp[:, f % 2, 0:T], psum[4 + f % 2][:, 0:T], ACT.Silu).then_inc(gsil, 1)
                    split_hi(UNIT[("gu", b, f % 2)] + 2)
                    act.wait_ge(hid_ready, f + 1)
                    if f >= 4:
                        act.wait_ge(down_used, f - 3)
                    act.activation(hid_hi[:, f % 4, :], hid[:, f % 4, :], ACT.Copy).then_inc(hidhi_ready, 1)
                if b in FFN_MOD_BLOCKS:
                    m = 2 * FFN_MODS + FFN_MOD_BLOCKS.index(b)
                    mod_copy(m)
                for n in range(TABLES_AT[b]):
                    if 0 < b < FBLOCKS - 1 and n == TABLES_AT[b] - 1:
                        split_hi(UNIT[("down", b - 1, 0)] + 2)
                    sin_tables(made)
                    made += 1
                if b in FFN_MOD_BLOCKS and m % 2:
                    mod_vector(m // 2)
            squares(hT, sq, h3_ready, lambda kc: kc + 1)
            root(3)
            act.wait_ge(ab_ready, 4)
            shifted(3, ACT.Identity, lambda kc: ab[:, 3, kc:kc + 1], lambda kc: mc(1, SH1, kc), yT)
            act.wait_ge(blk_c, 8)
            act.activation(cT_neg[:, :, :], cT[0][:, :, :], ACT.Copy, scale=-1.0).then_inc(cneg_ready, 1)
            kc = 0
            for b in range(NB):
                if b % 2 == 0:
                    mod_copy(2 * S5_MODS + b // 2)
                    if b % 4 == 2:
                        mod_vector(S5_MODS + b // 4)
                for _ in range(2 * (b in (5, 9, 13)) + 2 * (b == NB - 1)):
                    act.wait_ge(ys_pre, kc + 1)
                    act.activation(yT[:, kc, :], yT[:, kc, :], ACT.Gelu_apprx_tanh).then_inc(z_ready, 1)
                    kc += 1
                    if kc % 4 == 0:
                        y_split_hi(z_hi, kc // 4 - 1, z_ready, kc)
                if b == NB - 2:
                    split_hi(UNIT[("glu", 0, 0)])
            assert UNIT[("glu", 0, 1)] % 2 == 0
            split_hi(UNIT[("glu", 0, 1)])
            sigmoids(KC, lambda n: col("b_glu", KC + n))
            act.dma_start(wr[:, :, :], w_router[0].rearrange("(k p) e -> p k e", p=P)).then_inc(wr_in, 16)
            act.dma_start(bcol[:, :], b_router.rearrange("a e -> e a")).then_inc(wr_in, 16)
            squares(hT, sq_late, h4_ready, lambda kc: kc + 1)
            root(4)
            for n in range(2):
                act.wait_ge(g2_done, n + 1)
                act.activation(g2_row[:, n * 512:(n + 1) * 512], psum[4 + n][:, :], ACT.Copy).then_inc(g2row_ready, 1)
            act.wait_ge(ab_ready, 5)
            shifted(4, ACT.Identity, lambda kc: ab[:, 4, kc:kc + 1], lambda kc: mc(1, SH2, kc), yT)
            act.wait_ge(zeros_ready, 1)
            for tb in range(TB):
                act.activation(selT[:, tb * P:(tb + 1) * P], zeros[:, :], ACT.Copy).then_inc(act_own, 1)
            for n in range(8):
                if n == 4:
                    act.wait_ge(log_done, 1)
                    act.activation(logT[:, :], psum[6][0:NE, 0:T], ACT.Identity, bias=bcol[:, :]).then_inc(logT_ready, 1)
                act.wait_ge(tok_t, n + 1)
                src = psum[n % 4][:, :]
                dst = (acc if n < 4 else y_tok)[:, (n // 2) % 2, (n % 2) * 512:(n % 2) * 512 + 512]
                act.activation(dst, src, ACT.Copy).then_inc(tok_c, 1)
            act.wait_ge(exp2_in, 1)
            act.activation(rt[:, 4, :, 1], rt[:, 4, :, 0], ACT.Exp).then_inc(exp2, 1)
            act.wait_ge(items_ready, 1)
            narrow = act.value_load(counts_i[0:1, 0:1], min_val=NE - MAX_WIDE, max_val=NE)
            wide = act.value_load(counts_i[0:1, 1:2], min_val=0, max_val=MAX_WIDE)

            def y_high(i, h):
                act.wait_ge(yx_ready, i * 2 + (h + 1))
                if h:
                    act.wait_ge(comb_done, i * NCOMB + 2)
                act.activation(yx_hi[:, :], y_exp[:, h * 512:(h + 1) * 512], ACT.Copy).then_inc(yxh_ready, 1)

            with act.Fori(0, narrow) as i:
                for n in range(NH):
                    s = n % RAW_SLOTS
                    act.wait_ge(raw_in[s], (i * (NH // RAW_SLOTS) + (n // RAW_SLOTS + 1)) * 16)
                    act.wait_ge(hi_used, i * NH + n + 1)
                    act.activation(whi[:, n % HI_SLOTS, :], ring[:, s * HW:(s + 1) * HW],
                                   ACT.Copy).then_inc(hi_ready, 1)
                    if n >= 3 and HALVES[n - 3][0] == "U" and HALVES[n - 3][2] == 1:
                        j = HALVES[n - 3][1]
                        act.wait_ge(lo_used, i * NH + (AT[("U", j, 1)] + 1 + LO_SLOTS))
                        act.activation(silu_g[:, :], psum[j % 2][:, :], ACT.Silu).then_inc(s_ready, 1)
                    if n - 3 in T_AFTER:
                        j = T_AFTER[n - 3]
                        act.wait_ge(t_done, i * FT + j + 1)
                        act.activation(hh[:, j % 2, :, :], psum[6][:, :].rearrange("p (k s) -> p k s", k=4),
                                       ACT.Copy).then_inc(hh_ready, 1)
                    if n == 2:
                        y_high(i, 0)
                    if n - 3 == COMB_SLOTS[1]:
                        y_high(i, 1)
                    if n - 3 == SEL_T_AFTER:
                        act.wait_ge(sel_t, i + 1)
                        act.activation(selT[:, :], psum[7][:, 0:T], ACT.Copy).then_inc(selT_ready, 1)
                    g = GATHER_AFTER.get(n - 2)
                    if g is not None:
                        act.wait_ge(gath_done, i * 2 + g + 3)
                        act.activation(xe_hi[:, 4 * g:4 * g + 4, :],
                                       psum[7][:, :].rearrange("p (k s) -> p k s", k=4),
                                       ACT.Copy).then_inc(xh_ready, 1)
            y_high(narrow, 0)
            y_high(narrow, 1)
            with act.If(wide > 0):
                for n in range(4):
                    act.wait_ge(xw_t, n + 1)
                    act.activation(xw_hi[:, 2 * n:2 * n + 2, :], psum[4 + n][:, :].rearrange("p (k t) -> p k t", k=2),
                                   ACT.Copy).then_inc(xwh_ready, 1)
                with act.Fori(0, wide) as k:
                    i = narrow + k
                    for n in range(NH):
                        s = n % RAW_SLOTS
                        act.wait_ge(raw_in[s], (i * (NH // RAW_SLOTS) + (n // RAW_SLOTS + 1)) * 16)
                        act.wait_ge(hi_used, i * NH + n + 1)
                        act.activation(whi[:, n % HI_SLOTS, :], ring[:, s * HW:(s + 1) * HW],
                                       ACT.Copy).then_inc(hi_ready, 1)
                        if n < 3:
                            continue
                        kind, j, h = HALVES[n - 3]
                        if kind == "G" and h:
                            act.wait_ge(lo_used, i * NH + (n - 2 + LO_SLOTS))
                            for g in range(2):
                                act.activation(hw[j % 3][:, 2 * g:2 * g + 2, :],
                                               psum[g][:, :].rearrange("p (c t) -> p c t", c=2), ACT.Silu).then_inc(sw_ready, 1)
                        if kind == "U" and h:
                            act.wait_ge(hw_ready, k * 2 * FT + (2 * j + 2))
                            act.activation(hw_hi[j % 3][:, :, :], hw[j % 3][:, :, :], ACT.Copy).then_inc(hwh_ready, 1)
                    act.wait_ge(lo_used, (i + 1) * NH + LO_SLOTS)
                    for kc in range(KC):
                        act.activation(out_w[:, kc, :], psum[4 + kc // 2][:, (kc % 2) * T:(kc % 2) * T + T],
                                       ACT.Copy, scale=mc(1, G2, kc)).then_inc(outw_ready, 1)
            act.wait_ge(acc_half, wide * 4 + NCOMB)
            act.wait_ge(fg_in, 16)
            for tb in range(TB):
                act.wait_ge(acc_half, 2 * tb + 2)
                if tb:
                    act.wait_ge(act_own, 2 * TILES + TB + tb)
                act.activation(fin_sq[:, :], acc[:, tb, :], ACT.Square,
                               accum_out=now[:, 4 + tb:5 + tb]).then_inc(act_own, 1)
                act.wait_ge(act_own, 2 * TILES + TB + tb + 1)
            act.wait_ge(fin_var, 1)
            act.activation(now[:, 2:4], now[:, 6:8], ACT.Sqrt).then_inc(fin_std, 1)

        @block.vector
        def _(v):
            links = [0]

            def link(ins):
                links[0] += 1
                ins.then_inc(chain, 1)
                v.wait_ge(chain, links[0])

            v.wait_ge(rows_in, 16 * len(ROWS))
            for g in range(2):
                ins = v.tensor_copy(rows[64:96, 4, g * NS:(g + 1) * NS],
                                    ldt_rows[64:96, g:g + 1].broadcast_to([32, NS]))
            ins.then_inc(rows_ready, 1)
            v.memset(sum_col[:, :], 1.0 / 32).then_inc(sum_col_ready, 1)
            v.wait_ge(consts, 2)
            idv = ident[:, :].rearrange("p (a g c) -> p g a c", g=2, c=GC)
            for g in range(2):
                link(v.tensor_reduce(masks[:, g:g + 1], idv[:, g], axis=AX.XY, op=ALU.add))
            for g in range(2):
                link(v.tensor_scalar(masks[:, 2 + g:3 + g], masks[:, g:g + 1], -1.0, None, ALU.mult))

            def q(n):
                return sp5[:, n, :]

            def exponential(o, src, t):
                xx, k, r = t
                link(v.tensor_scalar(q(xx), src, -87.0, 88.7, ALU.max, ALU.min))
                link(v.tensor_scalar(q(k), q(xx), LOG2E, MAGIC, ALU.mult, ALU.add))
                link(v.tensor_scalar(q(k), q(k), MAGIC, None, ALU.subtract))
                link(v.scalar_tensor_tensor(q(r), q(k), -LN2_HI, q(xx), ALU.mult, ALU.add))
                link(v.scalar_tensor_tensor(q(r), q(k), -LN2_LO, q(r), ALU.mult, ALU.add))
                link(v.tensor_scalar(q(xx), q(r), EXP_COEF[0], None, ALU.mult))
                for cf in EXP_COEF[1:]:
                    link(v.scalar_tensor_tensor(q(xx), q(xx), cf, q(r), ALU.add, ALU.mult))
                link(v.tensor_scalar(sp5i[:, :], q(k), 127.0, 2.0 ** 23, ALU.add, ALU.mult))
                link(v.scalar_tensor_tensor(q(o), q(xx), 1.0, sp5i[:, :].bitcast(F32), ALU.add, ALU.mult))

            v.wait_ge(cols_ready, 5)
            are, aim, ldt = (cols[:, 4, 32 * n:32 * n + 32] for n in range(3))
            exponential(3, ldt, (0, 1, 2))
            link(v.tensor_tensor(q(4), q(3), are, ALU.mult))
            exponential(5, q(4), (0, 1, 2))
            link(v.tensor_tensor(q(6), q(3), aim, ALU.mult))
            link(v.tensor_scalar(q(7), q(6), 1.0 / (2 * np.pi), MAGIC, ALU.mult, ALU.add))
            link(v.tensor_scalar(q(7), q(7), MAGIC, None, ALU.subtract))
            link(v.scalar_tensor_tensor(q(8), q(7), -TWO_PI[0], q(6), ALU.mult, ALU.add))
            link(v.scalar_tensor_tensor(q(8), q(7), -TWO_PI[1], q(8), ALU.mult, ALU.add))
            link(v.scalar_tensor_tensor(q(8), q(7), -TWO_PI[2], q(8), ALU.mult, ALU.add))
            link(v.tensor_scalar(q(8), q(8), -3.1415925, 3.1415925, ALU.max, ALU.min))
            v.tensor_scalar(q(10), q(8), 1.0 / (2 * np.pi), None, ALU.mult).then_inc(trig_in, 1)
            v.wait_ge(trig_in, 1)
            link(v.tensor_scalar(q(13), q(10), 384.0, None, ALU.add))
            link(v.tensor_scalar(q(13), q(13), 384.0, None, ALU.subtract))
            v.tensor_tensor(q(14), q(10), q(13), ALU.subtract).then_inc(trig_out, 1)

            def variance(k):
                v.wait_ge(sum_ready, k + 1)
                v.tensor_scalar(nrm[:, 0, :], psum[7][:, 0:T], 1.0 / D, EPS, ALU.mult, ALU.add).then_inc(var_ready, 1)

            def rsqrt(k):
                v.wait_ge(std_ready, k + 1)
                link(v.reciprocal(nrm[:, 2, :], nrm[:, 1, :]))
                link(v.tensor_tensor(nrm[:, 1, :], nrm[:, 0, :], nrm[:, 2, :], ALU.mult))
                link(v.scalar_tensor_tensor(nrm[:, 1, :], nrm[:, 1, :], -0.5, nrm[:, 2, :], ALU.mult, ALU.mult))
                link(v.scalar_tensor_tensor(nrm[:, 1, :], nrm[:, 1, :], 1.5, nrm[:, 2, :], ALU.add, ALU.mult))

            def split_lo(u):
                v.wait_ge(ehi_ready, u + 1)
                w, lo, hi = unit_views(u)
                v.tensor_tensor(lo, w, hi.bitcast(F32), ALU.subtract).then_inc(elo_ready, 1)

            def y_split_lo(high, k):
                v.wait_ge(yhi_ready, k + 1)
                g = slice(4 * (k % 2), 4 * (k % 2) + 4)
                v.tensor_tensor(y_lo[:, g, :], yT[:, g, :], high[:, g, :].bitcast(F32), ALU.subtract).then_inc(ylo_ready, 1)

            def scaled(dst, src):
                for kc in range(KC):
                    v.tensor_tensor(dst[:, kc, :], src[:, kc, :], nrm[:, 1, :], ALU.mult).then_inc(raw_ready, 1)

            def mod_bias(k):
                l, m = MOD_ORDER[k]
                v.wait_ge(mod_raw, k + 1)
                v.tensor_tensor(mc(l, m), modraw[:, k, :], colv("mod_b", (l * 6 + m) * KC, KC),
                                ALU.add).then_inc(modc_ready, 1)
                v.wait_ge(modc_ready, k + 1)

            def gain_cols(o, l, m, name):
                v.scalar_tensor_tensor(ab[:, o, :], mc(l, m), 1.0, colv(name, l * KC, KC),
                                       ALU.add, ALU.mult).then_inc(ab_ready, 1)

            variance(0)
            rsqrt(0)
            scaled(yT, hT)
            v.wait_ge(trig, 2)
            link(v.tensor_tensor(q(15), q(12), q(12), ALU.mult))
            link(v.tensor_scalar(q(15), q(15), -2.0, 1.0, ALU.mult, ALU.add))
            link(v.tensor_tensor(q(15), q(15), q(5), ALU.mult))
            link(v.tensor_scalar(q(15), q(15), -1.0, None, ALU.add))
            link(v.tensor_tensor(q(16), q(11), q(5), ALU.mult))
            link(v.tensor_tensor(q(0), are, are, ALU.mult))
            link(v.tensor_tensor(q(1), aim, aim, ALU.mult))
            link(v.tensor_tensor(q(0), q(0), q(1), ALU.add))
            link(v.reciprocal(q(0), q(0)))
            link(v.tensor_tensor(q(1), q(15), are, ALU.mult))
            link(v.tensor_tensor(q(2), q(16), aim, ALU.mult))
            link(v.tensor_tensor(q(1), q(1), q(2), ALU.add))
            link(v.tensor_tensor(q(17), q(1), q(0), ALU.mult))
            link(v.tensor_tensor(q(1), q(16), are, ALU.mult))
            link(v.tensor_tensor(q(2), q(15), aim, ALU.mult))
            link(v.tensor_tensor(q(1), q(1), q(2), ALU.subtract))
            link(v.tensor_tensor(q(18), q(1), q(0), ALU.mult))
            mod_bias(0)
            gain_cols(0, 0, SC1, "norm1_g")
            mod_bias(1)
            v.wait_ge(s5_in, 64)
            fr, fi = (q(n).unsqueeze(2).broadcast_to([P, TILES, GC]) for n in (17, 18))
            for t, (f, w) in enumerate(((fr, 0), (fi, 1), (fr, 1), (fi, 0))):
                link(v.tensor_tensor(btmp[t][:, :, :], f, braw[w][:, :, :], ALU.mult))
            v.wait_ge(ones_pad, 3)
            for g in range(2):
                pr, cr = slice(64 * g, 64 * g + 64), slice(GC * g, GC * g + GC)
                v.tensor_tensor(bblk[0][pr, :, cr], btmp[0][pr, :, :], btmp[1][pr, :, :], ALU.subtract).then_inc(blk_ready, 1)
                v.tensor_tensor(bblk[1][pr, :, cr], btmp[2][pr, :, :], btmp[3][pr, :, :], ALU.add).then_inc(blk_ready, 1)
            for n in range(2):
                for g in range(2):
                    v.tensor_scalar(cblk[n][:, :, g * NS:(g + 1) * NS], craw[n][:, :, :],
                                    masks[:, 2 * n + g:2 * n + g + 1], None, ALU.mult).then_inc(blk_ready, 1)
            DVE_STEPS = TAPS - DVE_FROM + 2
            v.wait_ge(ones_pad, 1)
            v.wait_ge(x_t, 4)
            for n in range(KC):
                v.wait_ge(sig_ready, n + 1)
                v.scalar_tensor_tensor(upad[:, n, TAPS - 1:PAD], psum[4 + n % 2][:, 0:T], col("b_pw1", n),
                                       tmp[:, n % 2, 0:T], ALU.add, ALU.mult).then_inc(pair_used, 1)
                v.wait_ge(pair_used, n + 1)
                even, odd = conv[:, n, :], tmp[:, n % 2, T:2 * T]
                for k in range(DVE_FROM, TAPS):
                    o = odd if (k - DVE_FROM) % 2 else even
                    u = upad[:, n, k:k + T]
                    if k == DVE_FROM:
                        ins = v.tensor_scalar(o, u, dw(k, n), col("b_dw", n), ALU.mult, ALU.add)
                    elif k == DVE_FROM + 1:
                        ins = v.tensor_scalar(o, u, dw(k, n), None, ALU.mult)
                    else:
                        v.wait_ge(tap, n * DVE_STEPS + k - DVE_FROM - 1)
                        ins = v.scalar_tensor_tensor(o, u, dw(k, n), o, ALU.mult, ALU.add)
                    ins.then_inc(tap, 1)
                v.wait_ge(taps_done, n + 1)
                v.wait_ge(tap, (n + 1) * DVE_STEPS - 2)
                v.tensor_tensor(even, even, psum[n % 2][:, 0:T], ALU.add).then_inc(tap, 1)
                v.wait_ge(tapsum_ready, (n + 1) * (POOL_TAPS - 1))
                v.tensor_tensor(odd, odd, tapsum[:, n % 2, :], ALU.add).then_inc(tap, 1)
                v.wait_ge(tap, (n + 1) * DVE_STEPS)
                v.tensor_tensor(even, even, odd, ALU.add).then_inc(conv_ready, 1)
            split_lo(0)
            v.wait_ge(mean_sum, 1)
            link(v.tensor_scalar(nrm[:, 2, :], psum[7][:, 0:T], 1.0 / D, None, ALU.mult))
            for kc in range(KC):
                v.tensor_tensor(conv[:, kc, :], conv[:, kc, :], nrm[:, 2, :], ALU.subtract).then_inc(cent_ready, 1)
            split_lo(1)
            variance(1)
            rsqrt(1)
            scaled(conv, conv)
            for g in range(2):
                y_split_lo(y_hi, g)
            for k in range(CONV_MODS, NORM_MODS + 1):
                mod_bias(k)
            gain_cols(1, 0, SC2, "norm2_g")
            v.tensor_tensor(ab[:, 2, :], mc(0, G1), colv("b_pw2", 0, KC), ALU.mult).then_inc(ab_ready, 1)
            for n in range(KC):
                v.wait_ge(pw2_tmp, n + 1)
                v.tensor_tensor(hT[:, n, :], hT[:, n, :], tmp[:, n % 2, 0:T], ALU.add).then_inc(h2_ready, 1)
                if n in (1, 3, 5):
                    split_lo(n // 2 + 2)
            variance(2)
            rsqrt(2)
            scaled(yT, hT)
            for g in range(2):
                y_split_lo(y_hi, 2 + g)
            split_lo(5)
            mod_bias(NORM_MODS + 1)

            made = 0
            for b in range(FBLOCKS):
                for f in (2 * b, 2 * b + 1):
                    v.wait_ge(gsil, f + 1)
                    if f >= 4:
                        v.wait_ge(down_used, f - 3)
                    v.tensor_tensor(hid[:, f % 4, :], psum[4 + f % 2][:, T:2 * T], tmp[:, f % 2, 0:T],
                                    ALU.mult).then_inc(hid_ready, 1)
                    split_lo(UNIT[("gu", b, f % 2)] + 2)
                    v.wait_ge(hidhi_ready, f + 1)
                    v.tensor_tensor(hid_lo[:, f % 4, :], hid[:, f % 4, :], hid_hi[:, f % 4, :].bitcast(F32),
                                    ALU.subtract).then_inc(hidlo_ready, 1)
                for _ in range(TABLES_AT[b]):
                    i = S5_TABLE_ORDER[made]
                    v.wait_ge(rnd_ready, made + 1)
                    link(v.scalar_tensor_tensor(tabc[:, made, :], iota_t[:, :], sp5[:, 13, i:i + 1],
                                                tabs[:, made, :], ALU.mult, ALU.subtract))
                    link(v.scalar_tensor_tensor(tabc[:, made, :], iota_t[:, :], sp5[:, 14, i:i + 1],
                                                tabc[:, made, :], ALU.mult, ALU.add))
                    v.tensor_scalar(tabc[:, made, :], tabc[:, made, :], -0.5, 0.5, ALU.max, ALU.min).then_inc(frac_ready, 1)
                    made += 1
                if 0 < b < FBLOCKS - 1:
                    split_lo(UNIT[("down", b - 1, 0)] + 2)
            for k in range(FFN_MODS, S5_MODS):
                mod_bias(k)
            gain_cols(3, 1, SC1, "norm1_g")
            v.wait_ge(down_used, 2 * FBLOCKS)
            for n in range(KC):
                v.scalar_tensor_tensor(hT[:, n, :], psum[n // 2][:, (n % 2) * T:(n % 2) * T + T], mc(0, G2, n),
                                       hT[:, n, :], ALU.mult, ALU.add).then_inc(h3_ready, 1)
            variance(3)
            rsqrt(3)
            scaled(yT, hT)

            v.wait_ge(tab_ready, TILES)
            ta, tb_ = tmp[:, 0, :], tmp[:, 1, :]
            for b in range(NB):
                m, qq = b // 4, b % 4
                ur, ui = psum[(b % 2) * 2][:, :], psum[(b % 2) * 2 + 1][:, :]
                tc = tabc[:, 2 * b:2 * b + 2, :].rearrange("p a t -> p (a t)")
                ts = tabs[:, 2 * b:2 * b + 2, :].rearrange("p a t -> p (a t)")
                xr = xrot[:, b % 2, 0, :, :].rearrange("p a t -> p (a t)")
                xi = xrot[:, b % 2, 1, :, :].rearrange("p a t -> p (a t)")
                v.wait_ge(bu_done, b + 1)
                if b >= 2:
                    v.wait_ge(prod_p, 4 * (b - 1))
                link(v.tensor_tensor(ta, ur, tc, ALU.mult))
                link(v.tensor_tensor(tb_, ui, ts, ALU.mult))
                link(v.tensor_tensor(xr, ta, tb_, ALU.add))
                link(v.tensor_tensor(ta, ui, tc, ALU.mult))
                v.tensor_tensor(tb_, ur, ts, ALU.mult).then_inc(bu_used, 1)
                v.wait_ge(bu_used, b + 1)
                link(v.tensor_tensor(xi, ta, tb_, ALU.subtract))
                for k in range(2):
                    i = (2 * m + k) * 4 + qq
                    mag = sp5[:, 5, i:i + 1].broadcast_to([P, T])
                    for c2 in range(2):
                        s = xrot[:, b % 2, c2, k, :]
                        ins = v.tensor_tensor_scan(s, mag, s, 0.0, ALU.mult, ALU.add)
                        if k == 0 or c2 == 0:
                            link(ins)
                ins.then_inc(scan_ready, 1)
                if b % 4 == 1 and b > 1:
                    mm = b // 4 - 1
                    v.wait_ge(prod_used, 16 * (mm + 1))
                    for k in range(2):
                        kc = 2 * mm + k
                        v.scalar_tensor_tensor(yT[:, kc, :], yT[:, kc, :], col("ssm_d", kc),
                                               psum[4 + mm % 2][:, k * T:(k + 1) * T], ALU.mult, ALU.add).then_inc(ys_pre, 1)
            v.wait_ge(scan_ready, NB)
            for t in (2, 3):
                v.wait_ge(prod_used, 4 * (NB - 2) + t + 1)
                v.tensor_tensor(prod[:, t, :, :].rearrange("p a t -> p (a t)"), ts if t == 2 else tc,
                                xr if t == 2 else xi, ALU.mult).then_inc(prod_v, 1)
            y_split_lo(z_hi, 4)
            v.wait_ge(prod_used, 4 * NB)
            for k in range(2):
                kc = 6 + k
                v.scalar_tensor_tensor(yT[:, kc, :], yT[:, kc, :], col("ssm_d", kc),
                                       psum[5][:, k * T:(k + 1) * T], ALU.mult, ALU.add).then_inc(ys_pre, 1)
            split_lo(UNIT[("glu", 0, 0)])
            y_split_lo(z_hi, 5)
            split_lo(UNIT[("glu", 0, 1)])
            for k in range(S5_MODS, len(MOD_ORDER)):
                mod_bias(k)
            gain_cols(4, 1, SC2, "norm2_g")
            for n in range(KC):
                v.wait_ge(sig_ready, KC + n + 1)
                v.scalar_tensor_tensor(tmp[:, n % 2, T:2 * T], psum[4 + n % 2][:, 0:T], col("b_glu", n),
                                       tmp[:, n % 2, 0:T], ALU.add, ALU.mult).then_inc(pair_used, 1)
                v.wait_ge(pair_used, KC + n + 1)
                v.scalar_tensor_tensor(hT[:, n, :], tmp[:, n % 2, T:2 * T], mc(1, G1, n), hT[:, n, :],
                                       ALU.mult, ALU.add).then_inc(h4_ready, 1)
                if n + 2 < KC:
                    split_lo(UNIT[("glu", 0, 0)] + n + 2)
            v.wait_ge(h4_ready, KC)
            for kc in range(KC):
                v.tensor_scalar(tmp[:, kc // 4, (kc % 4) * P:(kc % 4) * P + P], ident[:, :], mc(1, G2, kc), None, ALU.mult).then_inc(diag_ready, 1)
            v.memset(zeros[:, :], 0.0).then_inc(zeros_ready, 1)
            variance(4)
            rsqrt(4)
            scaled(yT, hT)

            def r(n):
                return rt[:, n, :, :]

            def rb(n, c0):
                return rt[:, n, :, c0:c0 + 1].broadcast_to([P, TB, NE])

            v.wait_ge(logit_t, 1)
            for tb in range(TB):
                link(v.tensor_copy(logit[:, tb, :], psum[7][:, tb * P:tb * P + NE]))
            ie = iota_e[:, :].unsqueeze(1).broadcast_to([P, TB, NE])
            for k in range(2):
                src = logit[:, :, :] if k == 0 else r(3)
                link(v.tensor_reduce(rt[:, 5 + k, :, 0:1], src, axis=AX.X, op=ALU.max))
                link(v.tensor_tensor(r(7), src, rb(5 + k, 0), ALU.is_equal))
                link(v.tensor_scalar(r(8), ie, -1.0, float(NE), ALU.mult, ALU.add))
                link(v.tensor_tensor(r(7), r(7), r(8), ALU.mult))
                link(v.tensor_reduce(rt[:, 9, :, 0:1], r(7), axis=AX.X, op=ALU.max))
                link(v.tensor_tensor(r(k), r(8), rb(9, 0), ALU.is_equal))
                if k == 0:
                    link(v.tensor_scalar(r(3), r(0), -3.0e38, None, ALU.mult))
                    link(v.tensor_tensor(r(3), r(3), logit[:, :, :], ALU.add))
            v.tensor_tensor(r(2), r(0), r(1), ALU.add).then_inc(mask_ready, 1)
            v.tensor_tensor(rt[:, 4, :, 0], rt[:, 6, :, 0], rt[:, 5, :, 0], ALU.subtract).then_inc(exp2_in, 1)
            v.wait_ge(exp2, 1)
            link(v.tensor_scalar(rt[:, 4, :, 2], rt[:, 4, :, 1], 1.0, None, ALU.add))
            link(v.reciprocal(rt[:, 4, :, 3], rt[:, 4, :, 2]))
            link(v.tensor_tensor(rt[:, 4, :, 4], rt[:, 4, :, 3], rt[:, 4, :, 1], ALU.mult))
            link(v.tensor_tensor(r(0), r(0), rb(4, 3), ALU.mult))
            link(v.tensor_tensor(r(1), r(1), rb(4, 4), ALU.mult))
            link(v.tensor_tensor(r(11), r(0), r(1), ALU.add))
            v.wait_ge(rank_done, 1)
            for tb in range(TB):
                link(v.tensor_scalar(rt[:, 10, tb, :], psum[6][:, 128 + 64 * tb:128 + 64 * tb + NE], 999.0, None, ALU.add))
            link(v.tensor_tensor(r(10), r(10), r(2), ALU.mult))
            link(v.tensor_scalar(r(10), r(10), -1000.0, None, ALU.add))
            over, upto = rt[:, 0, 0, :], rt[:, 1, 0, :]
            link(v.tensor_scalar(over, psum[6][:, 256:256 + NE], float(P), None, ALU.is_gt))
            over0 = rt[:, 0, 0, 0:1]
            link(v.scalar_tensor_tensor(rt[:, 9, :, 0], over0.broadcast_to([P, TB]), -1000.0, rt[:, 10, :, 0], ALU.mult, ALU.add))
            v.wait_ge(consts, 6)
            for tb in range(TB):
                v.tensor_scalar(sel[:, tb, :], iota_s[:, :], rt[:, 9, tb, 0:1], None, ALU.is_equal).then_inc(sel_ready, 1)
            link(v.memset(rt[:, 0, 1, :], 1.0))
            link(v.tensor_tensor_scan(upto, rt[:, 0, 1, :], over, 0.0, ALU.mult, ALU.add))
            over1, upto1, narrow, wide = (rt[:, 3 + n // 2, n % 2, :] for n in range(4))
            link(v.tensor_copy(over1, over))
            link(v.memset(rt[:, 3, 0, 0:1], 0.0))
            link(v.tensor_scalar(upto1, upto, rt[:, 0, 0, 0:1], None, ALU.subtract))
            link(v.tensor_tensor(narrow, iota_e[:, :], upto1, ALU.subtract))
            link(v.scalar_tensor_tensor(narrow, over1, -1000.0, narrow, ALU.mult, ALU.add))
            link(v.tensor_scalar(rt[:, 5, 0, 0:1], rt[:, 3, 1, NE - 1:NE], -1.0, float(NE), ALU.mult, ALU.add))
            link(v.tensor_scalar(wide, upto, rt[:, 5, 0, 0:1], 999.0, ALU.add, ALU.add))
            link(v.tensor_tensor(wide, wide, over, ALU.mult))
            link(v.tensor_scalar(wide, wide, -1000.0, None, ALU.add))
            row = iota_s[:, 0:MAX_ROWS].unsqueeze(2).broadcast_to([P, MAX_ROWS, NE])
            link(v.tensor_tensor(place[:, :, :], narrow.unsqueeze(1).broadcast_to([P, MAX_ROWS, NE]), row, ALU.is_equal))
            link(v.tensor_tensor(placed[:, :, :], wide.unsqueeze(1).broadcast_to([P, MAX_ROWS, NE]), row, ALU.is_equal))
            link(v.tensor_tensor(place[:, :, :], place[:, :, :], placed[:, :, :], ALU.add))
            link(v.tensor_tensor(picked[:, :, :, :], place[:, :, :].unsqueeze(2).broadcast_to([P, MAX_ROWS, 4, NE]),
                                 rt[:, 10:12, :, :].rearrange("p a b e -> p (a b) e").unsqueeze(1).broadcast_to([P, MAX_ROWS, 4, NE]),
                                 ALU.mult))
            link(v.tensor_reduce(items[:, :, :].unsqueeze(3), picked[:, :, :, :], axis=AX.X, op=ALU.add))
            link(v.tensor_tensor(placed[:, :, :], place[:, :, :], iota_e[:, :].unsqueeze(1).broadcast_to([P, MAX_ROWS, NE]), ALU.mult))
            link(v.tensor_reduce(rt[:, 7:9, :, :].rearrange("p a b e -> p (a b e)")[:, 0:MAX_ROWS].unsqueeze(2), placed[:, :, :], axis=AX.X, op=ALU.add))
            link(v.tensor_copy(order_i[:, :], rt[:, 7:9, :, :].rearrange("p a b e -> p (a b e)")[:, 0:MAX_ROWS]))
            link(v.tensor_copy(counts_i[:, 0:1], rt[:, 5, 0, 0:1]))
            link(v.tensor_copy(counts_i[:, 1:2], rt[:, 1, 0, NE - 1:NE]))
            v.tensor_scalar(counts_i[:, 2:3], rt[:, 1, 0, NE - 1:NE], rt[:, 5, 0, 0:1], None, ALU.add).then_inc(items_ready, 1)
            for g in range(2):
                bank = psum[7 - g]
                v.wait_ge(gath_done, g + 1)
                v.tensor_copy(xe_hi[:, 4 * g:4 * g + 4, :], bank[:, :].rearrange("p (k s) -> p k s", k=4)).then_inc(xh_ready, 1)
                v.wait_ge(xh_ready, g + 1)
                v.tensor_tensor(xe_lo[:, 4 * g:4 * g + 4, :].rearrange("p k s -> p (k s)"), bank[:, :],
                                xe_hi[:, 4 * g:4 * g + 4, :].rearrange("p k s -> p (k s)").bitcast(F32),
                                ALU.subtract).then_inc(xl_ready, 1)
            v.wait_ge(g2row_ready, 2)

            def evac_y(i):
                v.wait_ge(lo_used, i * NH + LO_SLOTS)
                for h in range(2):
                    v.tensor_tensor(y_exp[:, h * 512:(h + 1) * 512], psum[4 + h][:, :],
                                    g2_row[:, h * 512:(h + 1) * 512], ALU.mult).then_inc(yx_ready, 1)

            def y_low(i, h):
                v.wait_ge(yxh_ready, i * 2 + (h + 1))
                v.tensor_tensor(yx_lo[:, h * 512:(h + 1) * 512], y_exp[:, h * 512:(h + 1) * 512],
                                yx_hi[:, :].bitcast(F32), ALU.subtract).then_inc(yxl_ready, 1)

            def combined(i, m, bank, done):
                h, tb = m // 2, m % 2
                v.wait_ge(comb_done, i * NCOMB + m + 1)
                a = acc[:, tb, h * 512:(h + 1) * 512]
                v.scalar_tensor_tensor(a, bank[:, :], now[:, 2 + tb:3 + tb], a, ALU.mult, ALU.add).then_inc(done, 1)

            link(v.memset(now[:, :], 0.0))
            v.wait_ge(items_ready, 1)
            narrow = v.value_load(counts_i[0:1, 0:1], min_val=NE - MAX_WIDE, max_val=NE)
            wide = v.value_load(counts_i[0:1, 1:2], min_val=0, max_val=MAX_WIDE)
            with v.Fori(0, narrow) as i:
                for n in range(NH):
                    s = n % RAW_SLOTS
                    v.wait_ge(hi_ready, i * NH + n + 1)
                    v.wait_ge(lo_used, i * NH + n + 1)
                    v.tensor_tensor(wlo[:, n % LO_SLOTS, :], ring[:, s * HW:(s + 1) * HW],
                                    whi[:, n % HI_SLOTS, :].bitcast(F32), ALU.subtract).then_inc(lo_ready, 1)
                    if n == 1:
                        evac_y(i)
                    if n == 3:
                        y_low(i, 0)
                    if n == COMB_SLOTS[1] + 4:
                        y_low(i, 1)
                    if n >= 2 and n - 2 in COMB_AFTER:
                        combined(i, COMB_AFTER[n - 2], psum[7], comb_used)
                    if n >= 3 and HALVES[n - 3][0] == "U" and HALVES[n - 3][2] == 1:
                        j = HALVES[n - 3][1]
                        v.wait_ge(s_ready, i * FT + j + 1)
                        v.tensor_tensor(hid_e[:, :], silu_g[:, :], psum[2 + j % 2][:, :], ALU.mult).then_inc(he_ready, 1)
                    if n - 3 in T_AFTER:
                        j = T_AFTER[n - 3]
                        v.wait_ge(hh_ready, i * FT + j + 1)
                        v.tensor_tensor(hl[:, j % 2, :, :].rearrange("p k s -> p (k s)"), psum[6][:, :],
                                        hh[:, j % 2, :, :].rearrange("p k s -> p (k s)").bitcast(F32),
                                        ALU.subtract).then_inc(hl_ready, 1)
                    if n == AT[("G", 4, 0)]:
                        v.wait_ge(comb_used, (i + 1) * NCOMB)
                        v.tensor_copy(now[:, 0:4], items[:, bass.ds(i, 1), :].rearrange("p a k -> p (a k)")).then_inc(now_ready, 1)
                        v.tensor_copy(now[:, 4:8], items[:, bass.ds(i + 1, 1), :].rearrange("p a k -> p (a k)")).then_inc(now_ready, 1)
                    if n == AT[("G", 5, 0)]:
                        v.wait_ge(now_ready, i * 2 + 2)
                        v.wait_ge(sel_t, i + 1)
                        for tb in range(TB):
                            v.tensor_scalar(sel[:, tb, :], iota_s[:, :], now[:, 4 + tb:5 + tb], None, ALU.is_equal).then_inc(sel_ready, 1)
                    g = GATHER_AFTER.get(n - 2)
                    if g is not None:
                        v.wait_ge(xh_ready, i * 2 + g + 3)
                        v.tensor_tensor(xe_lo[:, 4 * g:4 * g + 4, :].rearrange("p k s -> p (k s)"), psum[7][:, :],
                                        xe_hi[:, 4 * g:4 * g + 4, :].rearrange("p k s -> p (k s)").bitcast(F32),
                                        ALU.subtract).then_inc(xl_ready, 1)
            evac_y(narrow)
            y_low(narrow, 0)
            for m in range(NCOMB):
                if m == 2:
                    y_low(narrow, 1)
                combined(narrow, m, psum[m], acc_half)
            with v.If(wide > 0):
                for n in range(4):
                    v.wait_ge(xwh_ready, n + 1)
                    v.tensor_tensor(xw_lo[:, 2 * n:2 * n + 2, :].rearrange("p k t -> p (k t)"), psum[4 + n][:, :],
                                    xw_hi[:, 2 * n:2 * n + 2, :].rearrange("p k t -> p (k t)").bitcast(F32),
                                    ALU.subtract).then_inc(xwl_ready, 1)
                with v.Fori(0, wide) as k:
                    i = narrow + k
                    for n in range(NH):
                        s = n % RAW_SLOTS
                        v.wait_ge(hi_ready, i * NH + n + 1)
                        v.wait_ge(lo_used, i * NH + n + 1)
                        v.tensor_tensor(wlo[:, n % LO_SLOTS, :], ring[:, s * HW:(s + 1) * HW],
                                        whi[:, n % HI_SLOTS, :].bitcast(F32), ALU.subtract).then_inc(lo_ready, 1)
                        if n >= 3 and HALVES[n - 3][0] == "U" and HALVES[n - 3][2]:
                            j = HALVES[n - 3][1]
                            v.wait_ge(lo_used, i * NH + (n - 2 + LO_SLOTS))
                            for g in range(2):
                                v.wait_ge(sw_ready, k * 2 * FT + (2 * j + g + 1))
                                h_ = hw[j % 3][:, 2 * g:2 * g + 2, :].rearrange("p c t -> p (c t)")
                                v.tensor_tensor(h_, h_, psum[2 + g][:, :], ALU.mult).then_inc(hw_ready, 1)
                            v.wait_ge(hwh_ready, k * FT + (j + 1))
                            v.tensor_tensor(hw_lo[j % 3][:, :, :], hw[j % 3][:, :, :], hw_hi[j % 3][:, :, :].bitcast(F32),
                                            ALU.subtract).then_inc(hwl_ready, 1)
                    v.tensor_copy(now[:, 0:4], items[:, bass.ds(i, 1), :].rearrange("p a k -> p (a k)")).then_inc(now_ready, 1)
                    v.wait_ge(now_ready, narrow * 2 + k + 1)
                    for m in range(4):
                        h, tb = m // 2, m % 2
                        v.wait_ge(outw_t, k * 4 + m + 1)
                        a = acc[:, tb, h * 512:(h + 1) * 512]
                        v.scalar_tensor_tensor(a, psum[m][:, :], now[:, 2 + tb:3 + tb], a, ALU.mult, ALU.add).then_inc(acc_half, 1)
            v.wait_ge(act_own, 2 * TILES + 2 * TB)
            v.tensor_scalar(now[:, 6:8], now[:, 4:6], 1.0 / D, EPS, ALU.mult, ALU.add).then_inc(fin_var, 1)
            v.wait_ge(fin_std, 1)
            v.wait_ge(fin_var, 1)
            link(v.reciprocal(now[:, 0:2], now[:, 2:4]))
            link(v.tensor_tensor(now[:, 2:4], now[:, 6:8], now[:, 0:2], ALU.mult))
            link(v.scalar_tensor_tensor(now[:, 2:4], now[:, 2:4], -0.5, now[:, 0:2], ALU.mult, ALU.mult))
            link(v.scalar_tensor_tensor(now[:, 2:4], now[:, 2:4], 1.5, now[:, 0:2], ALU.add, ALU.mult))
            v.wait_ge(fg_in, 16)
            for tb in range(TB):
                v.scalar_tensor_tensor(acc[:, tb, :], acc[:, tb, :], now[:, 2 + tb:3 + tb], fin_g[:, :],
                                       ALU.mult, ALU.mult).then_inc(fin_ready, 1)

        @block.tensor
        def _(pe):
            mm = nc.tensor.matmul
            pe.wait_ge(consts, 2)
            pe.wait_ge(rows_ready, 1)
            for n, k in enumerate(ROW_TILES):
                nc.tensor.transpose(psum[0 if n < 4 else 1][:, (n % 4) * P:(n % 4) * P + k], rows[0:k, n, :],
                                    ident[0:k, 0:k]).then_inc(rows_t, 1)
            pe.wait_ge(x_in, 32)
            for n in range(4):
                if n >= 2:
                    pe.wait_ge(h_ready, n - 1)
                for k in range(2):
                    for tb in range(TB):
                        kc = 2 * n + k
                        ins = nc.tensor.transpose(psum[4 + n % 2][:, k * T + tb * P:k * T + (tb + 1) * P],
                                                  x_tok[:, tb, kc * P:(kc + 1) * P], ident[:, :])
                ins.then_inc(x_t, 1)

            def sums(base, ready, src, done):
                for kc in range(KC):
                    pe.wait_ge(ready, base + kc + 1)
                    ins = mm(psum[7][:, 0:T], ones[:, :], src[:, kc, :], start=kc == 0, stop=kc == KC - 1)
                ins.then_inc(done, 1)

            def split_product(out, u, high, k):
                _, lo, hi = unit_views(u)
                for p in range(3):
                    if p == 2:
                        pe.wait_ge(elo_ready, u + 1)
                    for kc in range(KC):
                        ins = mm(out, (lo if p == 2 else hi)[:, kc, k, :], (y_lo if p == 1 else high)[:, kc, :],
                                 start=p == 0 and kc == 0, stop=p == 2 and kc == KC - 1)
                return ins

            def split_pairs():
                for n in range(KC):
                    u = UNIT[("glu", n // 2, n % 2)]
                    pe.wait_ge(ehi_ready, u + 1)
                    pe.wait_ge(pair_used, KC + n - 1)
                    if n == 0:
                        pe.wait_ge(ylo_ready, 6)
                    for g in range(2):
                        ins = split_product(psum[4 + n % 2][:, g * T:(g + 1) * T], u, z_hi, g)
                    ins.then_inc(pair_done, 1)

            def s5_transposes(ns):
                pe.wait_ge(blk_ready, 8)
                for n in ns:
                    if n >= 2:
                        pe.wait_ge(blk_c, n - 1)
                    src = bblk[n // 2] if n < 4 else cblk[n // 2 - 2]
                    for k in range(4):
                        kc = (n % 2) * 4 + k
                        a = src[:, 4 * kc:4 * kc + 4, :].rearrange("p i c -> p (i c)") if n < 4 else src[:, kc, :]
                        ins = nc.tensor.transpose(psum[3 + 3 * (n % 2)][:, k * P:(k + 1) * P], a, ident[:, :])
                    ins.then_inc(blk_t, 1)

            def pairs():
                for n in range(KC):
                    t = WHERE[("pw1", n // 2)]
                    if n % 2 == 0:
                        pe.wait_ge(arr[slot_of(t)], arrived_count(t))
                    w = early(t, KC)
                    if n >= 2:
                        pe.wait_ge(pair_used, n - 1)
                    for g in range(2):
                        for kc in range(KC):
                            if n == 0:
                                pe.wait_ge(y_ready, kc + 1)
                            o = g * 256 + (n % 2) * P
                            ins = mm(psum[4 + n % 2][:, g * T:(g + 1) * T], w[:, kc, o:o + P], yT[:, kc, :],
                                     start=kc == 0, stop=kc == KC - 1)
                    ins.then_inc(pair_done, 1)
                    m = 2 * CONV_MODS + n // 2
                    if n % 2:
                        pe.wait_ge(blk_c, sum(len(S5_TURNS.get(q, ())) for q in range(n)))
                        mod_partial(m)
                    elif n in S5_TURNS:
                        pe.wait_ge(mod_acc, m)
                        s5_transposes(S5_TURNS[n])
                    if n:
                        taps(n - 1)
                    if n % 2:
                        mod_sums(m)
                taps(KC - 1)

            def taps(n):
                pe.wait_ge(diag_made, n + 1)
                pe.wait_ge(pair_used, n + 1)
                if n < 2:
                    pe.wait_ge(cols_ready, 5)
                else:
                    pe.wait_ge(conv_ready, n - 1)
                for k in range(PE_TAPS):
                    ins = mm(psum[n % 2][:, 0:T], diag[:, n % 2, k, :], upad[:, n, k:k + T],
                             start=k == 0, stop=k == PE_TAPS - 1)
                ins.then_inc(taps_done, 1)

            def mod_partial(m):
                n = WHERE[("mod", m)]
                bank = mod_place(m)[0]
                pe.wait_ge(arr[slot_of(n)], arrived_count(n))
                if m >= 2:
                    pe.wait_ge(mod_acc, m - 1 if 2 <= m < 2 * FFN_MODS else m)
                w, cc = early(n, KC), cond if m < 2 * FFN_MODS else cond_late
                for first in (True, False):
                    for j in range(4):
                        kc = 2 * j + (not first)
                        ins = mm(bank[32 * j:32 * j + 32, :], cc[:, kc, :], w[:, kc, :],
                                 start=first, stop=not first)
                ins.then_inc(mod_part, 1)

            def mod_sums(m):
                _, bank, part = mod_place(m)
                k, h = m // 2, m % 2
                if k and h == 0:
                    pe.wait_ge(mod_raw, k)
                pe.wait_ge(mod_acc, m + 1)
                for o in range(4):
                    ins = mm(bank[:, 4 * h + o:4 * h + o + 1], part[:, o // 2, (o % 2) * P:(o % 2) * P + P],
                             sum_col[:, :], start=True, stop=True)
                ins.then_inc(mod_sum, 1)

            def mod_tiles(first, last):
                mod_partial(first)
                for m in range(first, last):
                    if m + 1 < last:
                        mod_partial(m + 1)
                    mod_sums(m)

            sums(0, sq_ready, sq, sum_ready)
            pe.wait_ge(cond_ready, 1)
            pe.wait_ge(sum_col_ready, 1)
            mod_tiles(0, 2 * CONV_MODS)
            pe.wait_ge(h_ready, 4)
            pairs()
            sums(0, conv_ready, conv, mean_sum)
            pe.wait_ge(cent_ready, 1)
            sums(KC, sq_ready, sq, sum_ready)
            pe.wait_ge(blk_c, 8)
            mod_tiles(2 * NORM_MODS, 2 * NORM_MODS + 2)
            for n in range(KC):
                u = UNIT[("pw2", n // 4, n // 2 % 2)]
                pe.wait_ge(ehi_ready, u + 1)
                if n >= 2:
                    pe.wait_ge(pw2_tmp, n - 1)
                if n == 0:
                    pe.wait_ge(ylo_ready, 2)
                ins = split_product(psum[4 + n % 2][:, 0:T], u, y_hi, n % 2)
                ins.then_inc(pw2_done, 1)
            sums(2 * KC, sq_ready, conv, sum_ready)
            mod_tiles(2 * NORM_MODS + 2, 2 * FFN_MODS)

            def down(b):
                u = UNIT[("down", b, 0)]
                _, lo, hi = unit_views(u)
                pe.wait_ge(elo_ready, u + 1)
                for k in range(2):
                    f = 2 * b + k
                    if f == 0:
                        pe.wait_ge(mod_raw, FFN_MODS)
                    pe.wait_ge(hidlo_ready, f + 1)
                    for n in range(KC):
                        for p in range(3):
                            w = (lo if p == 2 else hi)[:, k, n // 4, (n % 4) * P:(n % 4) * P + P]
                            ins = mm(psum[n // 2][:, (n % 2) * T:(n % 2) * T + T], w,
                                     (hid_lo if p == 1 else hid_hi)[:, f % 4, :],
                                     start=f == 0 and n % 2 == 0 and p == 0,
                                     stop=f == 2 * FBLOCKS - 1 and p == 2, skip_group_check=True)
                    ins.then_inc(down_used, 1)

            for b in range(FBLOCKS):
                for k in range(2):
                    f = 2 * b + k
                    u = UNIT[("gu", b, k)]
                    pe.wait_ge(ehi_ready, u + 1)
                    if f >= 2:
                        pe.wait_ge(hid_ready, f - 1)
                    if f == 0:
                        pe.wait_ge(ylo_ready, 4)
                    for g in range(2):
                        ins = split_product(psum[4 + f % 2][:, g * T:(g + 1) * T], u, y_hi, g)
                    ins.then_inc(gu_done, 1)
                if b in FFN_MOD_BLOCKS:
                    m = 2 * FFN_MODS + FFN_MOD_BLOCKS.index(b)
                    pe.wait_ge(cond_ready, 2)
                    pe.wait_ge(var_ready, 3)
                    mod_partial(m)
                if b:
                    down(b - 1)
                if b in FFN_MOD_BLOCKS:
                    mod_sums(m)
            down(FBLOCKS - 1)
            pe.wait_ge(mod_raw, S5_MODS)
            sums(3 * KC, sq_ready, sq, sum_ready)

            def b_products(b):
                m, qq = b // 4, b % 4
                if b >= 2:
                    pe.wait_ge(bu_used, b - 1)
                for k in range(2):
                    kc = 2 * m + k
                    pe.wait_ge(y_ready, 3 * KC + kc + 1)
                    rows_q = slice(32 * qq, 32 * qq + 32)
                    for c2 in range(2):
                        ins = mm(psum[(b % 2) * 2 + c2][:, k * T:(k + 1) * T], bbT[c2][rows_q, kc, :],
                                 yT[rows_q, kc, :], start=True, stop=True)
                ins.then_inc(bu_done, 1)

            def c_products(b):
                m, qq = b // 4, b % 4
                if qq == 0 and m >= 2:
                    pe.wait_ge(ys_pre, 2 * (m - 1))
                for t, c_ in enumerate((cT[0], cT_neg, cT[1], cT[1])):
                    if b == NB - 1 and t >= 2:
                        pe.wait_ge(prod_v, t - 1)
                    else:
                        pe.wait_ge(prod_p, 4 * b + t + 1)
                    for k in range(2):
                        ins = mm(psum[4 + m % 2][32 * qq:32 * qq + 32, k * T:(k + 1) * T],
                                 c_[:, 2 * m + k, 32 * qq:32 * qq + 32], prod[:, t, k, :],
                                 start=t == 0 and k == 0, stop=t == 3, skip_group_check=True)
                    ins.then_inc(prod_used, 1)

            b_products(0)
            b_products(1)
            pe.wait_ge(cneg_ready, 1)
            for b in range(NB):
                if b + 2 < NB:
                    b_products(b + 2)
                if b % 2 == 0:
                    if b == 0:
                        pe.wait_ge(y_ready, 4 * KC)
                    mod_partial(2 * S5_MODS + b // 2)
                c_products(b)
                if b % 2 == 0:
                    mod_sums(2 * S5_MODS + b // 2)
            def token_major(n):
                if n >= 4:
                    pe.wait_ge(tok_c, n - 3)
                src, tb, h = (hT if n < 4 else yT), (n // 2) % 2, n % 2
                for k in range(4):
                    ins = nc.tensor.transpose(psum[n % 4][:, k * P:(k + 1) * P],
                                              src[:, 4 * h + k, tb * P:(tb + 1) * P], ident[:, :])
                ins.then_inc(tok_t, 1)

            split_pairs()
            pe.wait_ge(mod_raw, len(MOD_ORDER))
            sums(4 * KC, sq_ready, sq_late, sum_ready)

            pe.wait_ge(pair_used, 2 * KC)
            for kc in range(KC):
                pe.wait_ge(diag_ready, kc + 1)
                ins = mm(psum[4 + kc // 4][:, (kc % 4) * P:(kc % 4) * P + P], ones[:, :],
                         tmp[:, kc // 4, (kc % 4) * P:(kc % 4) * P + P], start=True, stop=True)
                if kc % 4 == 3:
                    ins.then_inc(g2_done, 1)
            for n in range(4):
                token_major(n)

            pe.wait_ge(g2row_ready, 2)
            pe.wait_ge(zeros_ready, 1)
            for bank, free, slots in ((4, hi_used, HI_SLOTS), (5, lo_used, LO_SLOTS)):
                for k in range(4):
                    ins = mm(psum[bank][:, k * P:(k + 1) * P], zeros[:, :], ones[:, :], start=True, stop=True)
                ins.then_inc(free, slots)

            pe.wait_ge(wr_in, 32)
            for kc in range(KC):
                pe.wait_ge(y_ready, 4 * KC + kc + 1)
                ins = mm(psum[6][0:NE, 0:T], wr[:, kc, :], yT[:, kc, :], start=kc == 0, stop=kc == KC - 1)
            ins.then_inc(log_done, 1)
            token_major(4)
            pe.wait_ge(logT_ready, 1)
            for tb in range(TB):
                ins = nc.tensor.transpose(psum[7][:, tb * P:tb * P + NE], logT[:, tb * P:(tb + 1) * P], ident[0:NE, 0:NE])
            ins.then_inc(logit_t, 1)
            for n in range(5, 8):
                token_major(n)
            pe.wait_ge(mask_ready, 1)
            pe.wait_ge(consts, 6)
            mm(psum[6][:, 128:128 + NE], tri[:, :], rt[:, 2, 0, :], start=True, stop=True)
            mm(psum[6][:, 192:192 + NE], tri[:, :], rt[:, 2, 1, :], start=True, stop=False)
            mm(psum[6][:, 192:192 + NE], ones[:, :], rt[:, 2, 0, :], start=False, stop=True)
            mm(psum[6][:, 256:256 + NE], ones[:, :], rt[:, 2, 0, :], start=True, stop=False)
            mm(psum[6][:, 256:256 + NE], ones[:, :], rt[:, 2, 1, :], start=False, stop=True).then_inc(rank_done, 1)

            def gather(k, g, bank=psum[7]):
                pe.wait_ge(sel_ready, k)
                for c4 in range(4):
                    kc = 4 * g + c4
                    for tb in range(TB):
                        ins = mm(bank[:, c4 * P:(c4 + 1) * P], y_tok[:, tb, kc * P:(kc + 1) * P], sel[:, tb, :],
                                 start=tb == 0, stop=tb == TB - 1)
                ins.then_inc(gath_done, 1)

            pe.wait_ge(tok_c, 8)
            pe.wait_ge(sel_ready, TB)
            gather(TB, 0)
            gather(TB, 1, psum[6])

            pe.wait_ge(items_ready, 1)
            narrow = pe.value_load(counts_i[0:1, 0:1], min_val=NE - MAX_WIDE, max_val=NE)
            wide = pe.value_load(counts_i[0:1, 1:2], min_val=0, max_val=MAX_WIDE)

            def product(i, n):
                kind, j, h = HALVES[n]
                pe.wait_ge(hi_ready, i * NH + n + 1)
                hi, lo = whi[:, n % HI_SLOTS, :], wlo[:, n % LO_SLOTS, :]
                if kind == "D":
                    if h == 0:
                        pe.wait_ge(hl_ready, i * FT + j + 1)
                        if j == 0:
                            pe.wait_ge(yx_ready, (i + 1) * 2)
                    steps = [(hh[:, j % 2, 2 * h + k, :], hl[:, j % 2, 2 * h + k, :], psum[4 + s],
                              (k * D + s * 512), j == 0 and h == 0 and k == 0, j == FT - 1 and h == 1 and k == 1)
                             for k in range(2) for s in range(2)]
                else:
                    if n == 0:
                        pe.wait_ge(xl_ready, i * 2 + 2)
                    bank = psum[(0 if kind == "G" else 2) + j % 2]
                    steps = [(xe_hi[:, 4 * h + k, :], xe_lo[:, 4 * h + k, :], bank, k * 512,
                              h == 0 and k == 0, h == 1 and k == 3) for k in range(4)]
                for k, (xh, xl, o, w, first, last) in enumerate(steps):
                    mm(o[:, :], xh, hi[:, w:w + 512], start=first, stop=False)
                    if k == len(steps) - 1:
                        pe.wait_ge(lo_ready, i * NH + n + 1)
                    ins = mm(o[:, :], xl, hi[:, w:w + 512], start=False, stop=False)
                ins.then_inc(hi_used, 1)
                for xh, xl, o, w, first, last in steps:
                    ins = mm(o[:, :], xh, lo[:, w:w + 512], start=False, stop=last)
                ins.then_inc(lo_used, 1)

            def combine(i, m, bank):
                h, tb = m // 2, m % 2
                if tb == 0:
                    pe.wait_ge(yxl_ready, i * 2 + (h + 1))
                mm(bank[:, :], selT[:, tb * P:(tb + 1) * P], yx_hi[:, :], start=True, stop=False)
                mm(bank[:, :], selT[:, tb * P:(tb + 1) * P], yx_lo[:, h * 512:(h + 1) * 512],
                   start=False, stop=True).then_inc(comb_done, 1)

            with pe.Fori(0, narrow) as i:
                for n in range(NH):
                    product(i, n)
                    if n in COMB_AFTER:
                        m = COMB_AFTER[n]
                        if m:
                            pe.wait_ge(comb_used, i * NCOMB + m)
                        combine(i, m, psum[7])
                    if n == SEL_T_AFTER:
                        pe.wait_ge(comb_used, (i + 1) * NCOMB)
                        pe.wait_ge(sel_ready, (i + 1) * TB)
                        for tb in range(TB):
                            ins = nc.tensor.transpose(psum[7][:, tb * P:(tb + 1) * P], sel[:, tb, :], ident[:, :])
                        ins.then_inc(sel_t, 1)
                    if n in GATHER_AFTER:
                        g = GATHER_AFTER[n]
                        if g == 0:
                            pe.wait_ge(selT_ready, i + 1)
                            gather(i * TB + 2 * TB, 0)
                        else:
                            pe.wait_ge(xl_ready, i * 2 + 3)
                            gather(i * TB + 2 * TB, 1)
                    if n in T_AFTER:
                        j = T_AFTER[n]
                        pe.wait_ge(he_ready, i * FT + j + 1)
                        if j:
                            pe.wait_ge(hl_ready, i * FT + j)
                        for k in range(4):
                            ins = nc.tensor.transpose(psum[6][:, k * P:(k + 1) * P], hid_e[:, k * P:(k + 1) * P], ident[:, :])
                        ins.then_inc(t_done, 1)
            pe.wait_ge(selT_ready, narrow)
            for m in range(NCOMB):
                combine(narrow, m, psum[m])

            with pe.If(wide > 0):
                pe.wait_ge(yx_ready, (narrow + 1) * 2)
                for n in range(4):
                    for k in range(2):
                        for tb in range(TB):
                            kc = 2 * n + k
                            if n == 2 and k == 0 and tb == 0:
                                pe.wait_ge(hl_ready, narrow * FT)
                                pe.wait_ge(xl_ready, narrow * 2 + 2)
                            ins = nc.tensor.transpose(psum[4 + n][:, k * T + tb * P:k * T + (tb + 1) * P],
                                                      y_tok[:, tb, kc * P:(kc + 1) * P], ident[:, :])
                    ins.then_inc(xw_t, 1)

                def wide_product(i, k, n):
                    kind, j, h = HALVES[n]
                    pe.wait_ge(hi_ready, i * NH + n + 1)
                    hi, lo = whi[:, n % HI_SLOTS, :], wlo[:, n % LO_SLOTS, :]
                    if kind == "D":
                        if h == 0:
                            pe.wait_ge(hwl_ready, k * FT + (j + 1))
                        steps = [(psum[4 + o // 2], o % 2, c * D + o * P, hw_hi[j % 3][:, 2 * h + c, :],
                                  hw_lo[j % 3][:, 2 * h + c, :], h == 0 and c == 0, h == 1 and c == 1)
                                 for c in range(2) for o in range(KC)]
                        opens, closes = j == 0, j == FT - 1
                    else:
                        if h == 0 and j:
                            pe.wait_ge(*((sw_ready, k * 2 * FT + 2 * j) if kind == "G" else (hw_ready, k * 2 * FT + 2 * j)))
                        b0 = 0 if kind == "G" else 2
                        steps = [(psum[b0 + c // 2], c % 2, kc * 512 + c * P, xw_hi[:, 4 * h + kc, :],
                                  xw_lo[:, 4 * h + kc, :], h == 0 and kc == 0, h == 1 and kc == 3)
                                 for kc in range(4) for c in range(4)]
                        opens = closes = True
                    for p in range(3):
                        if p == 2:
                            pe.wait_ge(lo_ready, i * NH + n + 1)
                        for q, (bank, half, w, xh, xl, first, last) in enumerate(steps):
                            if p == 1 and q == len(steps) - 1:
                                pe.wait_ge(lo_ready, i * NH + n + 1)
                            ins = mm(bank[:, half * T:(half + 1) * T], (lo if p == 2 else hi)[:, w:w + P],
                                     xl if p == 1 else xh, start=opens and first and p == 0 and half == 0,
                                     stop=closes and last and p == 2, skip_group_check=True)
                        if p:
                            ins.then_inc(hi_used if p == 1 else lo_used, 1)

                pe.wait_ge(xwl_ready, 4)
                with pe.Fori(0, wide) as k:
                    i = narrow + k
                    pe.wait_ge(acc_half, k * 4 + NCOMB)
                    for n in range(NH):
                        wide_product(i, k, n)
                    for m in range(4):
                        h, tb = m // 2, m % 2
                        pe.wait_ge(outw_ready, k * KC + (4 * h + 4))
                        for c in range(4):
                            ins = nc.tensor.transpose(psum[m][:, c * P:(c + 1) * P],
                                                      out_w[:, 4 * h + c, tb * P:(tb + 1) * P], ident[:, :])
                        ins.then_inc(outw_t, 1)


_INS = ["x", "c", "mod_w", "mod_b", "norm1_g", "norm2_g", "conv_w_pw1", "conv_b_pw1", "conv_w_dw",
        "conv_b_dw", "conv_ln_g", "conv_ln_b", "conv_w_pw2", "conv_b_pw2", "ssm_a_re", "ssm_a_im",
        "ssm_log_dt", "ssm_b_re", "ssm_b_im", "ssm_c_re", "ssm_c_im", "ssm_d", "ssm_w_glu",
        "ssm_b_glu", "ffn_w_gate", "ffn_w_up", "ffn_w_down", "moe_w_router", "moe_b_router",
        "moe_w_gate", "moe_w_up", "moe_w_down", "final_norm_g"]


def kernel(**inputs):
    import numpy as _np
    import concourse.bacc as _bacc
    from concourse import mybir as _mybir
    from concourse.bass_utils import run_bass_kernel_spmd as _run

    nc = _bacc.Bacc("TRN2", target_bir_lowering=False, num_devices=1)
    arrays, args = {}, []
    for name in _INS:
        a = _np.ascontiguousarray(inputs[name])
        arrays[f"in_{name}_dram"] = a
        args.append(nc.dram_tensor(f"in_{name}_dram", a.shape, _mybir.dt.from_np(a.dtype),
                                   kind="ExternalInput").ap())
    o = nc.dram_tensor("out_dram", (1, T, D), F32, kind="ExternalOutput").ap()
    trunk(nc, *args, o)
    r = _run(nc, [arrays], core_ids=[0])
    return r.results[0]["out_dram"]
```
